# Optimizing a Trainium2 kernel written in Bass

```python
import jax, jax.numpy as jnp
from jax import lax
import numpy as np

D_MODEL = 1024
BATCH = 1
SEQ = 256
DEPTH = 1
DEC_BATCH = 8
DEC_SEQ = 1
PAST_LEN = 2048
PAGE_SIZE = 128

HG_HEADS = 8
HG_KEY = 128
HG_VAL = D_MODEL // HG_HEADS
HG_KW = HG_HEADS * HG_KEY
HG_VW = HG_HEADS * HG_VAL
HG_CHUNK = 32
POOL_WINDOWS = (2, 4, 8, 16)
POOL_GROUPS = 4
POOL_W = D_MODEL
POOL_GW = POOL_W // POOL_GROUPS
POOL_BUF = 15
N_EXPERTS = 32
TOP_K = 4
D_FF = D_MODEL
SWIGLU_LIMIT = 7.0
SWIGLU_ALPHA = 1.702
MOE_BLOCK = 128
PLE_DIM = 256
EPS = 1e-6
IN_COLS = 2 * HG_KW + 2 * HG_VW + POOL_W + 2 * D_MODEL

kernel_name = "hgrn2_pool_gated_moe_ple_step"

def rmsnorm(x, g):
    xf = x.astype(jnp.float32)
    xf = xf * lax.rsqrt(jnp.mean(xf * xf, axis=-1, keepdims=True) + EPS)
    return (xf * g.astype(jnp.float32)).astype(x.dtype)

def hgrn2_chunked(q, k, v, logf):
    B, T, H, K = q.shape
    V = v.shape[-1]
    C = min(HG_CHUNK, T)
    N = T // C
    causal = jnp.tril(jnp.ones((C, C), dtype=bool))

    def to_chunks(a):
        return jnp.moveaxis(a.reshape(B, N, C, H, a.shape[-1]), 1, 0)

    def chunk_step(S, xs):
        qc, kc, vc, lc = xs
        b = jnp.cumsum(lc, axis=1)
        b_last = b[:, -1]
        qe = qc * jnp.exp(b)
        ke = kc * jnp.exp(-b)
        scores = jnp.where(causal[None, None], jnp.einsum('bchk,bshk->bhcs', qe, ke), 0.0)
        o = jnp.einsum('bchk,bhkv->bchv', qe, S) + jnp.einsum('bhcs,bshv->bchv', scores, vc)
        S_new = jnp.exp(b_last)[..., None] * S + jnp.einsum(
            'bchk,bchv->bhkv', kc * jnp.exp(b_last[:, None] - b), vc)
        return S_new, o

    S0 = jnp.zeros((B, H, K, V), jnp.float32)
    S_fin, o = lax.scan(chunk_step, S0, (to_chunks(q), to_chunks(k), to_chunks(v), to_chunks(logf)))
    o = jnp.moveaxis(o, 0, 1).reshape(B, T, H, V)
    return o, S_fin

def hgrn2_recurrent(q, k, v, logf, S0):
    def step(S, xs):
        qt, kt, vt, lt = xs
        S = jnp.exp(lt)[..., None] * S + kt[..., None] * vt[..., None, :]
        return S, jnp.einsum('bhk,bhkv->bhv', qt, S)

    S_fin, o = lax.scan(step, S0, tuple(jnp.moveaxis(a, 1, 0) for a in (q, k, v, logf)))
    return jnp.moveaxis(o, 0, 1), S_fin

def pool_mixer(u, buf, start_pos, w_pool, pool_scale):
    B, T, _ = u.shape
    ext = jnp.concatenate([buf, u], axis=1).astype(jnp.float32)
    cs = jnp.concatenate([jnp.zeros((B, 1, POOL_W), jnp.float32), jnp.cumsum(ext, axis=1)], axis=1)
    pos = start_pos + jnp.arange(T)
    end = cs[:, POOL_BUF + 1:POOL_BUF + 1 + T]
    uf = u.astype(jnp.float32)
    outs = []
    for g, w in enumerate(POOL_WINDOWS):
        lo, hi = g * POOL_GW, (g + 1) * POOL_GW
        s = end[..., lo:hi] - cs[:, POOL_BUF + 1 - w:POOL_BUF + 1 - w + T, lo:hi]
        cnt = jnp.minimum(pos + 1, w).astype(jnp.float32)[None, :, None]
        d = s / cnt - uf[..., lo:hi]
        outs.append(jnp.einsum('btc,cd->btd', d, w_pool[g].astype(jnp.float32)))
    y = jnp.concatenate(outs, axis=-1) * pool_scale.astype(jnp.float32)
    new_buf = ext[:, -POOL_BUF:].astype(u.dtype)
    return y, new_buf

def moe(h, w_router, b_router, w_gate, b_gate, w_up, b_up, w_down, b_down):
    lead = h.shape[:-1]
    xt = h.reshape(-1, D_MODEL)
    T = xt.shape[0]
    logits = xt.astype(jnp.float32) @ w_router.astype(jnp.float32) + b_router.astype(jnp.float32)
    top_v, top_i = lax.top_k(logits, TOP_K)
    top_w = jax.nn.softmax(top_v, axis=-1)
    flat_e = top_i.reshape(-1)
    flat_w = top_w.reshape(-1)
    n_assign = T * TOP_K
    order = jnp.argsort(flat_e)
    e_sorted = flat_e[order]
    counts = jnp.bincount(flat_e, length=N_EXPERTS)
    padded = (counts + MOE_BLOCK - 1) // MOE_BLOCK * MOE_BLOCK
    start = jnp.cumsum(counts) - counts
    pstart = jnp.cumsum(padded) - padded
    dest = pstart[e_sorted] + (jnp.arange(n_assign) - start[e_sorted])
    n_blocks = -(-n_assign // MOE_BLOCK) + N_EXPERTS
    n_rows = n_blocks * MOE_BLOCK
    row_tok = jnp.full((n_rows,), T, jnp.int32).at[dest].set((order // TOP_K).astype(jnp.int32))
    row_w = jnp.zeros((n_rows,), jnp.float32).at[dest].set(flat_w[order])
    block_e = jnp.minimum(jnp.searchsorted(jnp.cumsum(padded), jnp.arange(n_blocks) * MOE_BLOCK,
                                           side='right'), N_EXPERTS - 1).astype(jnp.int32)
    x_pad = jnp.concatenate([xt, jnp.zeros((1, D_MODEL), xt.dtype)], axis=0)
    x_rows = x_pad[row_tok].reshape(n_blocks, MOE_BLOCK, D_MODEL)

    def expert_block(args):
        xb, e = args
        gate = jnp.minimum(xb @ w_gate[e] + b_gate[e], SWIGLU_LIMIT)
        up = jnp.clip(xb @ w_up[e] + b_up[e], -SWIGLU_LIMIT, SWIGLU_LIMIT)
        act = (up + 1.0) * gate * jax.nn.sigmoid(SWIGLU_ALPHA * gate)
        return act @ w_down[e] + b_down[e]

    y_rows = lax.map(expert_block, (x_rows, block_e)).reshape(n_rows, D_MODEL)
    y = jax.ops.segment_sum(y_rows * row_w[:, None].astype(y_rows.dtype), row_tok, num_segments=T + 1)[:T]
    return y.reshape(*lead, D_MODEL)

def decoder_layer(x, p, S0, pool_buf, start_pos, is_prompt, lb, g_mix, w_in, hg_norm, w_pool, pool_scale,
                  w_out, g_ffn, w_router, b_router, w_gate, b_gate, w_up, b_up, w_down, b_down,
                  g_ple, w_ple_gate, w_ple_proj):
    B, T, _ = x.shape
    h = rmsnorm(x, g_mix)
    z = jnp.einsum('btd,dc->btc', h, w_in)
    cuts = [HG_KW, 2 * HG_KW, 2 * HG_KW + HG_VW, 2 * HG_KW + 2 * HG_VW,
            2 * HG_KW + 2 * HG_VW + POOL_W, 2 * HG_KW + 2 * HG_VW + POOL_W + D_MODEL]
    q_raw, f_raw, i_raw, g_raw, u, gate_a, gate_b = jnp.split(z, cuts, axis=-1)
    q = jax.nn.silu(q_raw.astype(jnp.float32)).reshape(B, T, HG_HEADS, HG_KEY)
    f = lb + (1.0 - lb) * jax.nn.sigmoid(f_raw.astype(jnp.float32))
    k = (1.0 - f).reshape(B, T, HG_HEADS, HG_KEY)
    logf = jnp.log(f).reshape(B, T, HG_HEADS, HG_KEY)
    v = i_raw.astype(jnp.float32).reshape(B, T, HG_HEADS, HG_VAL)
    if is_prompt:
        o, S_new = hgrn2_chunked(q, k, v, logf)
    else:
        o, S_new = hgrn2_recurrent(q, k, v, logf, S0.astype(jnp.float32))
    o = rmsnorm(o, hg_norm).reshape(B, T, HG_VW) * jax.nn.silu(g_raw.astype(jnp.float32))
    y_pool, new_buf = pool_mixer(u, pool_buf, start_pos, w_pool, pool_scale)
    merged = jax.nn.sigmoid(gate_a.astype(jnp.float32)) * o + jax.nn.sigmoid(gate_b.astype(jnp.float32)) * y_pool
    x = x + jnp.einsum('btc,cd->btd', merged.astype(x.dtype), w_out)
    x = x + moe(rmsnorm(x, g_ffn), w_router, b_router, w_gate, b_gate, w_up, b_up, w_down, b_down)
    gate_p = jax.nn.sigmoid(jnp.einsum('btd,de->bte', rmsnorm(x, g_ple), w_ple_gate).astype(jnp.float32))
    x = x + (gate_p * jnp.einsum('btp,pd->btd', p, w_ple_proj).astype(jnp.float32)).astype(x.dtype)
    return x, S_new.astype(x.dtype), new_buf

def setup_inputs(seed: int = 0) -> dict:
    key = jax.random.key(seed)
    ks = iter(jax.random.split(key, 32))

    def nrm(shape, scale):
        return scale * jax.random.normal(next(ks), shape, jnp.float32)

    def gain(shape):
        return 1.0 + nrm(shape, 0.05)

    return {
        "x_prompt": nrm((BATCH, SEQ, D_MODEL), 1.0),
        "x_sample": nrm((DEC_BATCH, DEC_SEQ, D_MODEL), 1.0),
        "p_prompt": nrm((DEPTH, BATCH, SEQ, PLE_DIM), 1.0),
        "p_sample": nrm((DEPTH, DEC_BATCH, DEC_SEQ, PLE_DIM), 1.0),
        "state_hgrn": nrm((DEPTH, DEC_BATCH, HG_HEADS, HG_KEY, HG_VAL), 0.5),
        "state_pool": nrm((DEPTH, DEC_BATCH, POOL_BUF, POOL_W), 1.0),
        "g_mix": gain((DEPTH, D_MODEL)),
        "w_in": nrm((DEPTH, D_MODEL, IN_COLS), D_MODEL ** -0.5),
        "hg_lb_logits": nrm((DEPTH + 1, HG_KW), 0.1),
        "hg_norm": gain((DEPTH, HG_VAL)),
        "w_pool": nrm((DEPTH, POOL_GROUPS, POOL_GW, POOL_GW), POOL_GW ** -0.5),
        "pool_scale": gain((DEPTH, POOL_W)),
        "w_out": nrm((DEPTH, D_MODEL, D_MODEL), D_MODEL ** -0.5),
        "g_ffn": gain((DEPTH, D_MODEL)),
        "w_router": nrm((DEPTH, D_MODEL, N_EXPERTS), D_MODEL ** -0.5),
        "b_router": nrm((DEPTH, N_EXPERTS), 0.01),
        "w_gate": nrm((DEPTH, N_EXPERTS, D_MODEL, D_FF), D_MODEL ** -0.5),
        "b_gate": nrm((DEPTH, N_EXPERTS, D_FF), 0.01),
        "w_up": nrm((DEPTH, N_EXPERTS, D_MODEL, D_FF), D_MODEL ** -0.5),
        "b_up": nrm((DEPTH, N_EXPERTS, D_FF), 0.01),
        "w_down": nrm((DEPTH, N_EXPERTS, D_FF, D_MODEL), D_FF ** -0.5),
        "b_down": nrm((DEPTH, N_EXPERTS, D_MODEL), 0.01),
        "g_ple": gain((DEPTH, D_MODEL)),
        "w_ple_gate": nrm((DEPTH, D_MODEL, D_MODEL), D_MODEL ** -0.5),
        "w_ple_proj": nrm((DEPTH, PLE_DIM, D_MODEL), PLE_DIM ** -0.5),
        "g_final": gain((D_MODEL,)),
    }

def reference(x_prompt, x_sample, p_prompt, p_sample, state_hgrn, state_pool, g_mix, w_in, hg_lb_logits,
              hg_norm, w_pool, pool_scale, w_out, g_ffn, w_router, b_router, w_gate, b_gate, w_up, b_up,
              w_down, b_down, g_ple, w_ple_gate, w_ple_proj, g_final):
    lb_all = jnp.cumsum(jax.nn.softmax(hg_lb_logits.astype(jnp.float32), axis=0), axis=0)
    xp, xs = x_prompt, x_sample
    hg_p, pool_p, hg_s, pool_s = [], [], [], []
    for i in range(DEPTH):
        lw = (lb_all[i], g_mix[i], w_in[i], hg_norm[i], w_pool[i], pool_scale[i], w_out[i], g_ffn[i],
              w_router[i], b_router[i], w_gate[i], b_gate[i], w_up[i], b_up[i], w_down[i], b_down[i],
              g_ple[i], w_ple_gate[i], w_ple_proj[i])
        zero_buf = jnp.zeros((xp.shape[0], POOL_BUF, POOL_W), xp.dtype)
        xp, sp, bp = decoder_layer(xp, p_prompt[i], None, zero_buf, 0, True, *lw)
        xs, ss, bs = decoder_layer(xs, p_sample[i], state_hgrn[i], state_pool[i], PAST_LEN, False, *lw)
        hg_p.append(sp)
        pool_p.append(bp)
        hg_s.append(ss)
        pool_s.append(bs)
    y_prompt = rmsnorm(xp, g_final)
    y_sample = rmsnorm(xs, g_final)
    return (y_prompt, y_sample, jnp.stack(hg_p), jnp.stack(pool_p), jnp.stack(hg_s), jnp.stack(pool_s))


_drawn_inputs = setup_inputs


def setup_inputs(seed=0):
    import zlib

    import numpy as np

    out = dict(_drawn_inputs(seed))
    spreads = {}
    factors = {'b_gate': 8.0, 'b_up': 8.0, 'b_down': 8.0, 'g_ple': 7.31}
    for name, (base, spread) in spreads.items():
        noise = np.random.default_rng([zlib.crc32(name.encode()), seed]).standard_normal(out[name].shape)
        drawn = base * np.exp(spread * noise) if base else spread * noise
        out[name] = __import__('jax').numpy.asarray(drawn.astype(out[name].dtype))
    for name, factor in factors.items():
        out[name] = (out[name] * factor).astype(out[name].dtype)
    return out
```

```python
from contextlib import ExitStack

import numpy as np

import concourse.bass as bass
from concourse import mybir

F32 = mybir.dt.float32
I32 = mybir.dt.int32
U32 = mybir.dt.uint32
ALU = mybir.AluOpType
ACT = mybir.ActivationFunctionType
AX_X = mybir.AxisListType.X

P = 128
D = 1024
SEQ = 256
NS = 8
T = SEQ + NS
TS = (P, P, NS)
NT = len(TS)
KD = D // P
H = 8
CH = 32
NCH = SEQ // CH
WINDOWS = (2, 4, 8, 16)
BUF = 15
NE = 32
TOPK = 4
CAP = 64
NBLK = -(-T // CAP)
NTAB = NBLK * NE + 1
LIMIT = 7.0
ALPHA = 1.702
EPS = 1e-6
FAR = 4096.0
HALF = 512
PLE = 256
GRAN = 2048
NGRAN = 3 * D * D // (P * GRAN)

W_CHUNKS = [("f", 1024), ("f", 1536), ("q", 0), ("q", 512), ("v", 2048), ("v", 2560),
            ("g", 3072), ("g", 3584), ("ga", 5120), ("ga", 5632),
            ("u", 4096), ("u", 4608), ("gb", 6144), ("gb", 6656)]
NSLOT = 4


def bank_jobs():
    jobs = []

    def norm(tag):
        for t in range(NT):
            for half in range(2 if t < 2 else 1):
                n = 2 * t + half
                jobs.append(((tag, t, half), n, "av"[n % 2]))

    def chunk(kind, n, pair, drains):
        for t in range(2):
            jobs.append(((kind, n, t), 2 * pair + t, drains[t]))

    jobs.append((("lb",), 7, "v"))
    norm("hT")
    for kind, drain in (("f", "a"), ("q", "v")):
        for h in range(H):
            jobs.append(((kind, h), h % 4, drain))
    chunk("v", 0, 0, "av")
    jobs += [(("v", "s", j), 4, "v") for j in range(2)]
    chunk("v", 1, 1, "av")
    chunk("g", 0, 0, "vv")
    chunk("g", 1, 1, "vv")
    chunk("ga", 0, 0, "vv")
    for n in range(4):
        jobs.append((("score", n // 2, n % 2), 5 + n % 3, "v"))
    for n in range(4):
        jobs.append((("kT", n // 2, n % 2), 5 + (n + 1) % 3, "a"))
    jobs += [(("g", "s", j), 4, "v") for j in range(4)]
    chunk("ga", 1, 1, "vv")
    for n in range(NCH):
        jobs.append((("dS", n, 0), 4, "v"))
        jobs.append((("dS", n, 1), 7, "v"))
        if n % 4 == 3:
            for half in range(2):
                jobs.append((("o", n // 4, half), 5 + half, "v"))
    chunk("u", 0, 0, "av")
    chunk("u", 1, 1, "av")
    for b in range(NS):
        for half in range(2):
            jobs.append((("vb", b, half), 5 + (2 * b + half) % 2, "v"))
    chunk("gb", 0, 0, "aa")
    jobs += [(("u", "s", j), 4, "a") for j in range(4)]
    chunk("gb", 1, 1, "aa")
    jobs.append((("os",), 7, "v"))
    for c in range(KD):
        jobs.append((("dT", c), c % 4, "av"[c % 2]))
    for t in range(NT):
        for half in range(2):
            jobs.append((("yp", t, half), 4 + (2 * t + half) % 4, "v"))
    norm("mT")
    for t in range(2):
        for half in range(2):
            jobs.append((("x1", t, half), 2 * t + half, "v"))
    jobs += [(("x1", 2, half), 4, "v") for half in range(2)]
    norm("h2T")
    jobs.append((("lgT",), 6, "v"))
    jobs.append((("lg",), 7, "v"))
    jobs.append((("rank",), 0, "v"))
    jobs.append((("count",), 1, "v"))
    jobs.append((("wT",), 2, "v"))
    for t in range(2):
        for half in range(2):
            jobs.append((("bd", t, half), 4 + 2 * t + half, "v"))
    jobs += [(("bd", 2, half), 3, "v") for half in range(2)]
    norm("h3T")
    jobs += [(("pT", k), 5 + k, "a") for k in range(2)]
    for t in range(2):
        for half in range(2):
            jobs.append((("pg", t, half), 6 + (2 * t + half) % 2, "a"))
            jobs.append((("pp", t, half), (2 * t + half) % 4, "v"))
    jobs += [(("pg", 2, half), 6, "a") for half in range(2)]
    jobs += [(("pp", 2, half), 4, "v") for half in range(2)]
    return jobs


def build(nc, x_prompt, x_sample, p_prompt, p_sample, state_hgrn, state_pool, g_mix, w_in,
          hg_lb_logits, hg_norm, w_pool, pool_scale, w_out, g_ffn, w_router, b_router, w_gate, b_gate,
          w_up, b_up, w_down, b_down, g_ple, w_ple_gate, w_ple_proj, g_final,
          y_prompt, y_sample, new_hgrn_prompt, new_pool_prompt, new_hgrn_sample, new_pool_sample):
    jobs = bank_jobs()
    order = {name: n for n, (name, _, _) in enumerate(jobs)}
    drainer = {name: e for name, _, e in jobs}
    drain_count, before = {}, {}
    seen, last = {"a": 0, "v": 0}, {}
    for name, bank, e in jobs:
        seen[e] += 1
        drain_count[name] = seen[e]
        before[name] = last.get(bank)
        last[bank] = name

    with ExitStack() as ctx:
        def sem(name):
            return ctx.enter_context(nc.semaphore(name))

        arena = ctx.enter_context(nc.sbuf_tensor("arena", [P, 53200], F32))
        bank = [ctx.enter_context(nc.psum_tensor(f"bank{n}", [P, HALF], F32)) for n in range(8)]
        at = [0]

        def take(floats):
            at[0] += floats
            assert at[0] <= 53200, at[0]
            return at[0] - floats

        def view(start, floats, rows=P):
            return arena[0:rows, start:start + floats]

        R = take(NGRAN * GRAN)
        X = take(3 * D)
        HT = take(KD * T)
        HG = take(5 * KD * T)
        V = take(3 * D)
        OG = take(3 * D)
        TMP = take(2 * HALF)
        G0 = take(D)
        G12 = take(2 * D)
        ident = view(take(P), P)
        cmask = view(take(P), P).bitcast(I32)
        before_t = view(take(P), P)
        ones = view(take(P), P)
        BAND = take(4 * (144 + P))
        dm8 = view(take(64), 64).rearrange("p (b c) -> p b c", b=8)
        selw = view(take(32), 32).rearrange("p (g b) -> p g b", g=4)
        wr = view(take(KD * NE), KD * NE).rearrange("p (k e) -> p k e", k=KD)
        lb = view(take(8), 8)
        omlb = view(take(8), 8)
        lgin = view(OG, P)
        lbt = view(take(32), 32)
        hgn = view(take(P), P)
        brt = view(take(1), 1, NE)
        stat = view(take(32), 32)
        eps = view(take(1), 1)
        flag = view(take(1), 1, 1).bitcast(I32)
        fs = view(take(64), 64).rearrange("p (h b) -> p h b", h=H)
        ks = view(take(64), 64).rearrange("p (h b) -> p h b", h=H)
        ebl = view(take(64), 64).rearrange("p (h n) -> p h n", h=H)

        def rows3(start):
            return view(start, 3 * D).rearrange("p (t d) -> p t d", t=3)

        def heads(start):
            return view(start, KD * T).rearrange("p (k t) -> p k t", k=KD)

        x = rows3(X)
        hT = heads(HT)
        w_slot = [view(R + s * 4096, 4096).rearrange("p (k n) -> p k n", k=KD) for s in range(NSLOT)]
        s0 = view(R + 4 * 4096, 8192).rearrange("p (b h v) -> p b h v", b=NS, h=H)
        qh, fh, kh, t1, t2 = (heads(HG + n * KD * T) for n in range(5))
        score = view(HG + 4 * KD * T, 2048).rearrange("p (n c) -> p n c", n=4)
        ktok = view(HG + 2 * KD * T, 2048).rearrange("p (t k) -> p t k", t=2)
        sel8 = view(HG + 3 * KD * T, 1024, NS).rearrange("p (b k) -> p b k", b=NS)
        qm = view(HG + 3 * KD * T + 1024, 512).rearrange("p (h b c) -> p h b c", h=H, b=NS)
        state = [view(HG + KD * T + n * 1024, 1024).rearrange("p (h v) -> p h v", h=H) for n in range(2)]
        v = rows3(V)
        og = rows3(OG)
        tmp = [view(TMP + n * HALF, HALF) for n in range(2)]
        u = rows3(HG)
        gb = rows3(HG + 3072)
        dT = heads(HG + 6144)
        mT = heads(HG + 8256)
        htok = rows3(V)
        bufrows = view(V, D, NS * BUF)
        gmix_b = view(G0, D)
        pscale_b = view(G0, D)
        gffn_b = view(V + D, D)
        wpool = view(G12, 2048).rearrange("p (g k n) -> p g k n", g=4, k=2)
        wout = view(R + 8 * GRAN, 8192).rearrange("p (k n) -> p k n", k=KD)
        band0 = [view(BAND + g * 144, 144) for g in range(4)]
        band1 = [view(BAND + 4 * 144 + g * P, P) for g in range(4)]

        h2 = rows3(OG)
        gran = [view(R + g * GRAN, GRAN).rearrange("p (j n) -> p j n", j=2) for g in range(NGRAN)]
        wple = view(HG, 8192).rearrange("p (k n) -> p k n", k=KD)
        wproj = view(HG + 8192, 2048).rearrange("p (k n) -> p k n", k=2)
        bias_g = view(V, D, NE)
        bias_u = view(V + D, D, NE)
        bias_d = view(V + 2 * D, D, NE)
        xg_tok, xT_e, actT, y_sb = (view(G12 + n * HALF, HALF) for n in range(4))
        g_sb, u_sb = (view(TMP + n * HALF, HALF) for n in range(2))
        act_sb = view(G0, HALF)
        comb = view(BAND, T)
        slot_tab = view(HT, 3 * NTAB).rearrange("p (t c) -> p t c", t=3)
        wt_tab = view(HT + 3 * NTAB, 3 * NTAB).rearrange("p (t c) -> p t c", t=3)
        ohw = view(HT + 6 * NTAB, 3 * P).rearrange("p (t c) -> p t c", t=3)
        oh = view(HT + 6 * NTAB + 3 * P, 3 * CAP).rearrange("p (t c) -> p t c", t=3)
        esel = view(HT + 6 * NTAB + 3 * P + 3 * CAP, CAP, NE)
        eis = view(HT + 6 * NTAB + 3 * P + 4 * CAP, NTAB, NE)
        sig_sb = view(G0 + HALF, HALF)
        iota = view(take(P), P)
        dw8 = view(take(32), 32, NS).rearrange("p (g b) -> p g b", g=4)

        def small(n, k=1):
            start = G12 + small.at
            small.at += 3 * n
            return view(start, 3 * n).rearrange("p (t c) -> p t c", t=3)
        small.at = 0
        lg, msk, wdn, tmpr, tmpw, isk = (small(NE) for _ in range(6))
        top, topf, exw = small(8), small(8), small(4)
        topi = small(8).bitcast(U32)
        ssum, rsum = small(1), small(1)
        wT = view(G12 + small.at, T, NE)
        lgT = view(G12 + small.at + T, T, NE)
        assert small.at + 2 * T <= 2048

        h3 = rows3(R)
        gple_b = view(R + 3072, D)
        gfin_b = view(R + 4096, D)
        ptok = view(R + 5120, 3 * PLE).rearrange("p (t d) -> p t d", t=3)
        pT = view(R + 6144, 2 * T).rearrange("p (k t) -> p k t", k=2)
        pgs = rows3(R + 7168)
        yout = rows3(R + 10240)
        sq = view(R + 13312, D)

        filled = sem("bank_filled")
        drained = {"a": sem("bank_drained_by_scalar"), "v": sem("bank_drained_by_vector")}
        s_pool = sem("pool_step")
        s_dve = sem("vector_step")
        s_act = sem("scalar_step")
        s_const = sem("constants_ready")
        s_x = sem("x_loaded")
        s_w = [sem(f"w_in_slot{n}_loaded") for n in range(NSLOT)]
        names = ("gmix pscale gffn lbin hgn br wr wpool s0 wout bufrows bias bdown ple gple gfin ptok").split()
        ld = {n: sem(f"{n}_loaded") for n in names}
        s_rows = sem("normalised_rows_ready")
        s_sumsq = sem("squares_summed")
        s_osq = sem("sample_output_rms_ready")
        s_lb = sem("lower_bound_ready")
        s_lbe = sem("lower_bound_exponentials")
        s_sig = sem("sigmoid_in_sbuf")
        s_tfull = sem("tmp_filled")
        s_fdone = sem("forget_gate_ready")
        s_prep = sem("hgrn_vector_step")
        s_prepa = sem("hgrn_scalar_step")
        s_sczero = sem("score_buffer_zeroed")
        s_inter = sem("state_read_by_tensor")
        s_ogp = sem("output_gate_times_norm_gain")
        s_sel8 = sem("row_selectors_ready")
        s_decay = sem("sample_state_decayed")
        s_snst = sem("sample_state_stored")
        s_merged = sem("merged_ready")
        s_rt = sem("router_vector_step")
        s_rta = sem("router_exponentials")
        s_tab = sem("routing_tables_ready")
        s_oh = sem("token_selectors_ready")
        s_ohw = sem("weighted_selectors_ready")
        s_used = sem("granule_used")
        s_gr = [sem(f"granule{g}_loaded") for g in range(NGRAN)]
        s_gate = sem("gate_sums_ready")
        s_up = sem("up_sums_ready")
        s_gclip = sem("gate_clipped")
        s_gsig = sem("gate_sigmoid_ready")
        s_uclip = sem("up_clipped")
        s_actr = sem("activation_ready")
        s_xg = sem("gathered_rows_in_psum")
        s_xgs = sem("gathered_rows_in_sbuf")
        s_xgt = sem("gathered_rows_transposed")
        s_xe = sem("expert_input_ready")
        s_cT = sem("combine_matrix_in_psum")
        s_c = sem("combine_matrix_ready")
        s_aT = sem("activation_transposed")
        s_aTs = sem("activation_transposed_in_sbuf")
        s_y = sem("expert_output_in_psum")
        s_ys = sem("expert_output_in_sbuf")
        s_mix = sem("combined_rows_in_psum")
        s_free01, s_free67, s_free45 = (sem(f"banks_{n}_added_to_x") for n in ("01", "67", "45"))
        s_esel = sem("expert_selector_ready")
        s_end = sem("experts_done")
        s_stst = sem("prompt_state_stored")
        s_dloop = sem("vector_step_in_expert")
        s_xfin = sem("x_final")
        s_yout = sem("y_ready")
        s_out = sem("outputs_stored")
        n_out = [0]

        def fill_done(ins, name):
            ins.then_inc(filled, 1)

        def wait_filled(eng, name):
            eng.wait_ge(filled, order[name] + 1)

        def wait_drained(eng, name):
            eng.wait_ge(drained[drainer[name]], drain_count[name])

        def drain_done(ins, name):
            ins.then_inc(drained[drainer[name]], 1)

        def job_bank(name):
            return bank[jobs[order[name]][1]]

        def lanes(t):
            return slice(0, TS[t])

        def toks(t):
            return slice(t * P, t * P + TS[t])

        def halves(h):
            return slice(h * HALF, (h + 1) * HALF)

        last_use = [("f", 3), ("f", 7), ("q", 3), ("q", 7), ("v", "s", 1), ("v", 1, 1),
                    ("g", "s", 3), ("g", "s", 3), ("g", "s", 3), ("ga", 1, 1)]
        rows_of = state_pool.rearrange("o b j d -> (o b j) d")

        tmp_jobs = [("g", n, t) for n in range(2) for t in range(2)] + [("ga", 0, 0), ("ga", 0, 1)]
        tmp_jobs += [("g", "s", j) for j in range(4)] + [("ga", 1, 0), ("ga", 1, 1)]
        tmp_jobs += [("o", t, half) for t in range(2) for half in range(2)]
        after_x = [(), ("x1",), ()]

        def turned_bank(name, dst, copy):
            _, t, half = name
            n = TS[t]
            ks_ = slice(4 * half, 4 * half + 4) if t < 2 else slice(0, KD)
            src = job_bank(name)[:, 0:(ks_.stop - ks_.start) * n].rearrange("p (k t) -> p k t", t=n)
            copy(name, dst[:, ks_, toks(t)], src)

        block = ctx.enter_context(nc.Block())

        @block.sync
        def _(sp):
            xp = x_prompt[0].rearrange("(t p) d -> p t d", p=P)
            sp.dma_start(x[:, 0, :], xp[:, 0, :]).then_inc(s_x, 16)
            sp.dma_start(x[:, 1, :], xp[:, 1, :]).then_inc(s_x, 16)
            sp.dma_start(x[0:NS, 2, :], x_sample[:, 0, :]).then_inc(s_x, 16)
            wi = w_in[0].rearrange("(k p) n -> p k n", p=P)
            for c, (_, col) in enumerate(W_CHUNKS):
                if c >= NSLOT:
                    wait_filled(sp, last_use[c - NSLOT])
                sp.dma_start(w_slot[c % NSLOT], wi[:, :, col:col + HALF]).then_inc(s_w[c % NSLOT], 16)

            parts = [w.rearrange("o e (g j p) n -> (o e) g p j n", j=2, p=P) for w in (w_gate, w_up, w_down)]

            def load_expert(i, e):
                for g in range(NGRAN):
                    sp.wait_ge(s_used, NGRAN * i + g + 1)
                    sp.dma_start(gran[g], parts[g // 4][e, g % 4]).then_inc(s_gr[g], 16)

            with sp.Fori(0, NE) as e:
                load_expert(e, e)
            sp.wait_ge(s_tab, 1)
            more = sp.value_load(flag)
            with sp.If(more > 0):
                with sp.Fori(1, NBLK) as b:
                    with sp.Fori(0, NE) as e:
                        load_expert(b * NE + e, e)

        @block.gpsimd
        def _(pool):
            chain = [0]

            def step(ins):
                chain[0] += 1
                ins.then_inc(s_pool, 1)
                pool.wait_ge(s_pool, chain[0])

            def store(dst, src):
                pool.dma_start(dst, src).then_inc(s_out, 16)
                n_out[0] += 1

            pool.dma_start(gmix_b, g_mix.partition_broadcast(P)[:, 0, :]).then_inc(ld["gmix"], 16)
            pool.dma_start(lgin[0:16, :], hg_lb_logits.rearrange("d (h k) -> (d h) k", k=P)).then_inc(ld["lbin"], 16)
            pool.dma_start(hgn, hg_norm.partition_broadcast(P)[:, 0, :]).then_inc(ld["hgn"], 16)
            pool.dma_start(brt, b_router.rearrange("o e -> e o")).then_inc(ld["br"], 16)
            pool.dma_start(wr, w_router[0].rearrange("(k p) e -> p k e", p=P)).then_inc(ld["wr"], 16)
            pool.dma_start(wpool, w_pool[0].rearrange("g (k p) n -> p g k n", p=P)).then_inc(ld["wpool"], 16)
            for b in range(NS):
                pool.dma_start(s0[:, b], state_hgrn[0, b].rearrange("h k v -> k h v")).then_inc(ld["s0"], 16)
            for b in range(NS):
                store(new_pool_sample[0, b, 0:BUF - 1, :], state_pool[0, b, 1:BUF, :])

            step(pool.memset(ident, 0.0))
            step(pool.affine_select(out=ident, in_=ident, compare_op=ALU.not_equal, fill=1.0, base=0,
                                    pattern=[[-1, P]], channel_multiplier=1))
            step(pool.memset(ones, 1.0))
            step(pool.memset(eps, EPS))
            pool.memset(stat, 0.0).then_inc(s_const, 1)
            step(pool.memset(before_t, 1.0))
            step(pool.affine_select(out=before_t, in_=before_t, compare_op=ALU.is_gt, fill=0.0, base=0,
                                    pattern=[[1, P]], channel_multiplier=-1))
            cm = iota
            step(pool.memset(cm, 1.0))
            step(pool.affine_select(out=cm, in_=cm, compare_op=ALU.is_ge, fill=0.0, base=0,
                                    pattern=[[1, P]], channel_multiplier=-1))
            step(pool.affine_select(out=cm, in_=cm, compare_op=ALU.is_ge, fill=0.0, base=0,
                                    pattern=[[-CH, P // CH], [0, CH]], channel_multiplier=1))
            step(pool.tensor_copy(cmask, cm))
            step(pool.iota(iota.rearrange("p (c n) -> p c n", c=2), [[0, 2], [1, CAP]], base=0,
                           channel_multiplier=0, allow_small_or_imprecise_dtypes=True))
            step(pool.memset(dm8, 0.0))
            step(pool.affine_select(out=dm8, in_=dm8, compare_op=ALU.not_equal, fill=1.0, base=0,
                                    pattern=[[1, 8], [-1, 8]], channel_multiplier=0))
            for g, w in enumerate(WINDOWS):
                step(pool.memset(band0[g], 1.0 / w))
                for t in range(w - 1):
                    pool.memset(band0[g][:, t:t + 1], 1.0 / (t + 1))
                step(pool.memset(band1[g], 1.0 / w))
                for m, n in ((band0[g], 144), (band1[g], P)):
                    step(pool.affine_select(out=m, in_=m, compare_op=ALU.is_ge, fill=0.0, base=0,
                                            pattern=[[1, n]], channel_multiplier=-1))
                    step(pool.affine_select(out=m, in_=m, compare_op=ALU.is_ge, fill=0.0, base=w - 1,
                                            pattern=[[-1, n]], channel_multiplier=1))
                    step(pool.tensor_tensor(m[:, 0:P], m[:, 0:P], ident, ALU.subtract))
                m = selw[:, g, :]
                step(pool.memset(m, 1.0 / w))
                step(pool.affine_select(out=m, in_=m, compare_op=ALU.is_ge, fill=0.0, base=-(BUF + 1 - w),
                                        pattern=[[-BUF, 8]], channel_multiplier=1))
                step(pool.affine_select(out=m, in_=m, compare_op=ALU.is_ge, fill=0.0, base=BUF - 1,
                                        pattern=[[BUF, 8]], channel_multiplier=-1))
            pool.memset(dm8[:, 0, 0:1], 1.0).then_inc(s_const, 1)

            pool.wait_ge(s_prepa, 5)
            pool.memset(score, 0.0).then_inc(s_sczero, 1)
            wait_drained(pool, ("score", 1, 1))
            step(pool.memset(sel8, 1.0))
            step(pool.affine_select(out=sel8, in_=sel8, compare_op=ALU.is_ge, fill=0.0, base=0,
                                    pattern=[[-1, 8], [0, P]], channel_multiplier=1))
            step(pool.affine_select(out=sel8, in_=sel8, compare_op=ALU.is_ge, fill=0.0, base=0,
                                    pattern=[[1, 8], [0, P]], channel_multiplier=-1))
            pool.tensor_tensor(qm, dm8.unsqueeze(1).to_broadcast([P, H, 8, 8]),
                               qh[:, :, SEQ:T].unsqueeze(3).to_broadcast([P, H, 8, 8]),
                               ALU.mult).then_inc(s_sel8, 1)
            pool.wait_ge(ld["hgn"], 16)
            wait_drained(pool, ("ga", 1, 1))
            for t in range(NT):
                o = og[lanes(t), t, :].rearrange("p (h v) -> p h v", h=H)
                pool.tensor_tensor(o, o, hgn[lanes(t)].unsqueeze(1).to_broadcast([TS[t], H, P]),
                                   ALU.mult).then_inc(s_ogp, 1)
            wait_drained(pool, ("o", 1, 1))
            wait_drained(pool, ("dS", NCH - 1, 1))
            pool.dma_start(pscale_b, pool_scale.partition_broadcast(P)[:, 0, :]).then_inc(ld["pscale"], 16)
            pool.dma_start(bufrows, rows_of).then_inc(ld["bufrows"], 16)
            pool.dma_start(gffn_b, g_ffn.partition_broadcast(P)[:, 0, :]).then_inc(ld["gffn"], 16)
            pool.dma_start(new_hgrn_prompt[0, 0].rearrange("h k v -> k h v"), state[NCH % 2]).then_inc(s_stst, 16)
            for b in range(NS):
                wait_drained(pool, ("vb", b, 1))
                pool.dma_start(new_hgrn_sample[0, b].rearrange("h k v -> k h v"), s0[:, b]).then_inc(s_snst, 16)
            wait_drained(pool, ("u", 0, 1))
            wait_drained(pool, ("u", 1, 1))
            store(new_pool_prompt[0, 0], u[P - BUF:P, 1, :])
            wait_drained(pool, ("u", "s", 3))
            store(new_pool_sample[0, :, BUF - 1, :], u[0:NS, 2, :])
            pool.wait_ge(s_snst, 16 * NS)
            wait_drained(pool, ("os",))
            for k in range(4):
                pool.dma_start(wout[:, 2 * k:2 * k + 2], w_out[0].rearrange("(k p) n -> p k n", p=P)[
                    :, 2 * k:2 * k + 2]).then_inc(ld["wout"], 16)
            pool.wait_ge(s_rows, 6)
            pool.dma_start(bias_g, b_gate[0]).then_inc(ld["bias"], 16)
            pool.dma_start(bias_u, b_up[0]).then_inc(ld["bias"], 16)
            pool.dma_start(bias_d, b_down[0]).then_inc(ld["bdown"], 16)
            pool.wait_ge(s_out, 16 * n_out[0])
            pool.wait_ge(s_stst, 16)
            pool.dma_start(wple, w_ple_gate[0].rearrange("(k p) n -> p k n", p=P)).then_inc(ld["ple"], 16)
            pool.dma_start(wproj, w_ple_proj[0].rearrange("(k p) n -> p k n", p=P)).then_inc(ld["ple"], 16)
            pool.wait_ge(s_end, 1)
            pool.dma_start(gple_b, g_ple.partition_broadcast(P)[:, 0, :]).then_inc(ld["gple"], 16)
            pool.dma_start(gfin_b, g_final.partition_broadcast(P)).then_inc(ld["gfin"], 16)
            pool.dma_start(ptok[:, 0:2, :], p_prompt[0, 0].rearrange("(t p) d -> p t d", p=P)).then_inc(ld["ptok"], 16)
            pool.dma_start(ptok[0:NS, 2, :], p_sample[0, :, 0, :]).then_inc(ld["ptok"], 16)
            for t in range(2):
                pool.wait_ge(s_yout, t + 1)
                store(y_prompt[0, toks(t), :], yout[:, t, :])
            pool.wait_ge(s_yout, 3)
            store(y_sample[:, 0, :], yout[0:NS, 2, :])
            pool.wait_ge(s_out, 16 * n_out[0])

        @block.tensor
        def _(pe):
            def begin(name):
                if before[name]:
                    wait_drained(pe, before[name])

            def turn_rows(tag, src, ready, n_used=0):
                for t in range(NT):
                    pe.wait_ge(*ready(t))
                    n = TS[t]
                    for half in range(2 if t < 2 else 1):
                        name = (tag, t, half)
                        begin(name)
                        ks_ = range(4 * half, 4 * half + 4) if t < 2 else range(KD)
                        for j, k in enumerate(ks_):
                            ins = pe.transpose(job_bank(name)[:, j * n:(j + 1) * n], src[0:n, t, k * P:(k + 1) * P],
                                               ident[0:n, 0:n])
                            if n_used and j < 2:
                                n_used -= 1
                                ins.then_inc(s_used, 1)
                        fill_done(ins, name)

            def wait_turned(tag):
                for t in range(NT):
                    for half in range(2 if t < 2 else 1):
                        wait_drained(pe, (tag, t, half))

            chunk_no = {}
            for c, (kind, _) in enumerate(W_CHUNKS):
                chunk_no[(kind, c - [k for k, _ in W_CHUNKS].index(kind))] = c

            def wait_chunk(c):
                pe.wait_ge(s_w[c % NSLOT], 16 * (c // NSLOT + 1))

            def chunk_step(kind, n, k, signal=None):
                w = w_slot[chunk_no[(kind, n)] % NSLOT]
                for t in range(2):
                    name = (kind, n, t)
                    if k == 0:
                        begin(name)
                    ins = pe.matmul(job_bank(name)[:, :], hT[:, k, toks(t)], w[:, k, :],
                                    start=(k == 0), stop=(k == KD - 1))
                    if k == KD - 1:
                        fill_done(ins, name)
                    elif t == 0 and signal:
                        ins.then_inc(signal, 1)

            def chunk(kind, n):
                wait_chunk(chunk_no[(kind, n)])
                for k in range(KD):
                    chunk_step(kind, n, k)

            def sample_rows(kind, chunks):
                name = (kind, "s", 0)
                begin(name)
                for c in chunks:
                    wait_chunk(c)
                for k in range(KD):
                    for j, c in enumerate(chunks):
                        ins = pe.matmul(job_bank(name)[32 * j:32 * j + NS, :], hT[:, k, toks(2)],
                                        w_slot[c % NSLOT][:, k, :], start=(k == 0), stop=(k == KD - 1))
                        if k == KD - 1:
                            fill_done(ins, (kind, "s", j))

            pe.wait_ge(s_const, 1)
            pe.wait_ge(ld["lbin"], 16)
            fill_done(pe.transpose(bank[7][:, 0:16], lgin[0:16, :], ident[0:16, 0:16]), ("lb",))
            turn_rows("hT", htok, lambda t: (s_rows, t + 1))
            wait_turned("hT")

            for kind in ("f", "q"):
                for h in range(H):
                    c = chunk_no[(kind, h // 4)]
                    wait_chunk(c)
                    begin((kind, h))
                    for k in range(KD):
                        ins = pe.matmul(job_bank((kind, h))[:, 0:T],
                                        w_slot[c % NSLOT][:, k, (h % 4) * P:(h % 4 + 1) * P], hT[:, k, :],
                                        start=(k == 0), stop=(k == KD - 1))
                    fill_done(ins, (kind, h))
            chunk("v", 0)
            sample_rows("v", (4, 5))
            chunk("v", 1)
            chunk("g", 0)
            chunk("g", 1)
            chunk("ga", 0)

            pe.wait_ge(s_prep, 5)
            for t in range(2):
                for half in range(2):
                    name = ("score", t, half)
                    begin(name)
                    for j in range(4):
                        h = 4 * half + j
                        ins = pe.matmul(job_bank(name)[:, j * P:(j + 1) * P], t1[:, h, toks(t)], qh[:, h, toks(t)],
                                        start=True, stop=True)
                    fill_done(ins, name)
            for t in range(2):
                for half in range(2):
                    name = ("kT", t, half)
                    begin(name)
                    for j in range(4):
                        ins = pe.transpose(job_bank(name)[:, j * P:(j + 1) * P], fh[:, 4 * half + j, toks(t)], ident)
                    fill_done(ins, name)
            sample_rows("g", (6, 7, 8, 9))
            chunk("ga", 1)

            wait_chunk(chunk_no[("u", 0)])
            for name in [("kT", t, half) for t in range(2) for half in range(2)] + [("v", n, t) for n in range(2) for t in range(2)]:
                wait_drained(pe, name)
            for n in range(NCH):
                t, row = n // 4, CH * (n % 4)
                rr = slice(row, row + CH)
                for half in range(2):
                    name = ("dS", n, half)
                    begin(name)
                    for j in range(4):
                        hh = slice((4 * half + j) * P, (4 * half + j + 1) * P)
                        ins = pe.matmul(job_bank(name)[:, j * P:(j + 1) * P], ktok[rr, t, hh], v[rr, t, hh],
                                        start=True, stop=True)
                    fill_done(ins, name)
                for half in range(2):
                    name = ("o", t, half)
                    if n % 4 == 0:
                        begin(name)
                        wait_drained(pe, ("score", t, half))
                        for j in range(4):
                            h = 4 * half + j
                            ins = pe.matmul(job_bank(name)[:, j * P:(j + 1) * P],
                                            score[:, 2 * t + half, j * P:(j + 1) * P], v[:, t, h * P:(h + 1) * P],
                                            start=(j == 0), stop=True, skip_group_check=True)
                    if n > 0:
                        wait_drained(pe, ("dS", n - 1, 1))
                        for j in range(4):
                            h = 4 * half + j
                            ins = pe.matmul(job_bank(name)[rr, j * P:(j + 1) * P], qh[:, h, n * CH:(n + 1) * CH],
                                            state[n % 2][:, h, :], start=False, stop=True,
                                            skip_group_check=True, tile_position=(0, row))
                    if n % 4 == 3:
                        fill_done(ins, name)
                chunk_step("u", 0, n, signal=s_inter)
            chunk("u", 1)
            wait_chunk(chunk_no[("gb", 0)])
            pe.wait_ge(s_sel8, 1)
            wait_drained(pe, ("v", "s", 1))
            for b in range(NS):
                for half in range(2):
                    name = ("vb", b, half)
                    begin(name)
                    fill_done(pe.matmul(job_bank(name)[:, :], sel8[:, b, :], v[0:NS, 2, halves(half)],
                                        start=True, stop=True), name)
                chunk_step("gb", 0, b)
            sample_rows("u", (10, 11, 12, 13))
            chunk("gb", 1)
            begin(("os",))
            wait_drained(pe, ("vb", NS - 1, 1))
            for hh in range(2):
                for b in range(NS):
                    for j in range(4):
                        h = 4 * hh + j
                        ins = pe.matmul(job_bank(("os",))[32 * j:32 * j + NS, hh * P:(hh + 1) * P], qm[:, h, b, :],
                                        s0[:, b, h, :], start=(b == 0), stop=(b == NS - 1))
            fill_done(ins, ("os",))

            for name in [("u", n, t) for n in range(2) for t in range(2)] + [("u", "s", 3)]:
                wait_drained(pe, name)
            pe.wait_ge(ld["bufrows"], 16)
            pe.wait_ge(s_const, 2)
            for c in range(KD):
                name, g = ("dT", c), c // 2
                begin(name)
                o, cc = job_bank(name), slice(c * P, (c + 1) * P)
                pe.matmul(o[:, 0:144], u[:, 0, cc], band0[g], start=True, stop=True, skip_group_check=True).then_inc(s_used, 1)
                pe.matmul(o[:, P:SEQ], u[:, 1, cc], band1[g], start=False, stop=True, skip_group_check=True)
                pe.matmul(o[:, SEQ:T], bufrows[:, cc], selw[0:NS * BUF, g, :], start=True, stop=False)
                ins = pe.matmul(o[:, SEQ:T], u[0:NS, 2, cc], dw8[0:NS, g, :], start=False, stop=True)
                fill_done(ins, name)
            pe.wait_ge(ld["wpool"], 16)
            for c in range(KD):
                wait_drained(pe, ("dT", c))
            for t in range(NT):
                for half in range(2):
                    name = ("yp", t, half)
                    begin(name)
                    for gg in range(2):
                        g = 2 * half + gg
                        for k in range(2):
                            ins = pe.matmul(job_bank(name)[lanes(t), gg * 256:(gg + 1) * 256],
                                            dT[:, 2 * g + k, toks(t)], wpool[:, g, k, :],
                                            start=(k == 0), stop=(k == 1))
                    fill_done(ins, name)
            turn_rows("mT", og, lambda t: (s_merged, t + 1))
            pe.wait_ge(ld["wout"], 64)
            wait_turned("mT")

            def product(tag, t, src, w, slices=KD):
                if t < 2:
                    for half in range(2):
                        name = (tag, t, half)
                        begin(name)
                        for k in range(slices):
                            ins = pe.matmul(job_bank(name)[:, :], src[:, k, toks(t)], w[:, k, halves(half)],
                                            start=(k == 0), stop=(k == slices - 1))
                        fill_done(ins, name)
                else:
                    begin((tag, 2, 0))
                    for k in range(slices):
                        for half in range(2):
                            ins = pe.matmul(job_bank((tag, 2, 0))[32 * half:32 * half + NS, :], src[:, k, toks(2)],
                                            w[:, k, halves(half)], start=(k == 0), stop=(k == slices - 1))
                            if k == slices - 1:
                                fill_done(ins, (tag, 2, half))

            for t in range(NT):
                product("x1", t, mT, wout)

            turn_rows("h2T", h2, lambda t: (s_rows, t + 4), n_used=4)
            pe.wait_ge(ld["wr"], 16)
            wait_turned("h2T")
            begin(("lgT",))
            for k in range(KD):
                ins = pe.matmul(bank[6][0:NE, 0:T], wr[:, k, :], hT[:, k, :], start=(k == 0), stop=(k == KD - 1))
            fill_done(ins, ("lgT",))
            begin(("lg",))
            wait_drained(pe, ("lgT",))
            for t in range(NT):
                ins = pe.transpose(bank[7][lanes(t), t * NE:(t + 1) * NE], lgT[:, toks(t)], ident[0:NE, 0:NE])
            fill_done(ins, ("lg",))
            pe.wait_ge(s_rt, 2)
            begin(("rank",))
            for t in range(NT):
                for s in range(t):
                    pe.matmul(bank[0][:, t * NE:(t + 1) * NE], ones, msk[:, s, :], start=(s == 0), stop=False)
                n = TS[t]
                ins = pe.matmul(bank[0][:, t * NE:(t + 1) * NE], before_t[0:n, :], msk[0:n, t, :],
                                start=(t == 0), stop=True)
            fill_done(ins, ("rank",))
            begin(("count",))
            for t in range(NT):
                n = TS[t]
                ins = pe.matmul(bank[1][0:8, 0:NE], ones[0:n, 0:8], msk[0:n, t, :], start=(t == 0), stop=(t == NT - 1))
            fill_done(ins, ("count",))
            begin(("wT",))
            for t in range(NT):
                ins = pe.transpose(bank[2][0:NE, toks(t)], wdn[lanes(t), t, :], ident[lanes(t), lanes(t)])
            fill_done(ins, ("wT",))
            pe.wait_ge(ld["bdown"], 16)
            wait_drained(pe, ("wT",))
            for t in range(2):
                for half in range(2):
                    name = ("bd", t, half)
                    begin(name)
                    fill_done(pe.matmul(job_bank(name)[:, :], wT[:, toks(t)], bias_d[:, halves(half)],
                                        start=True, stop=True), name)
            begin(("bd", 2, 0))
            for half in range(2):
                fill_done(pe.matmul(bank[3][32 * half:32 * half + NS, :], wT[:, toks(2)], bias_d[:, halves(half)],
                                    start=True, stop=True), ("bd", 2, half))

            GATE, UP, Y, XG, AT, CT = bank[0], bank[1], bank[2], bank[3], bank[4], bank[5]

            def hp(c):
                return slice(CAP * c, CAP * c + CAP)

            def gather():
                for t in range(NT):
                    for c in range(2):
                        ins = pe.matmul(XG[hp(c), :], oh[lanes(t), t, :], h2[lanes(t), t, halves(c)],
                                        start=(t == 0), stop=(t == NT - 1))
                return ins

            def turn_gathered():
                for j in range(4):
                    ins = pe.transpose(XG[:, j * P:(j + 1) * P], xg_tok[:, j * P:(j + 1) * P], ident)
                return ins

            def in_slice(src, k):
                return src[:, (k % 4) * P + (k // 4) * CAP:(k % 4) * P + (k // 4) * CAP + CAP]

            def expert(i):
                pe.wait_ge(s_esel, i + 1)
                pe.wait_ge(s_xe, i + 1)
                pe.wait_ge(s_free01, i + 1)
                for m, (out, bias, done) in enumerate(((GATE, bias_g, s_gate), (UP, bias_u, s_up))):
                    for c in range(2):
                        ins = pe.matmul(out[hp(c), :], esel, bias[:, halves(c)], start=True, stop=False)
                        if m == 1 and c == 0:
                            ins.then_inc(s_used, 1)
                    for g in range(4):
                        pe.wait_ge(s_gr[4 * m + g], i * 16 + 16)
                        for j in range(2):
                            k = 2 * g + j
                            for c in range(2):
                                ins = pe.matmul(out[hp(c), :], in_slice(xT_e, k), gran[4 * m + g][:, j, halves(c)],
                                                start=False, stop=(k == KD - 1))
                        if g < 3:
                            ins.then_inc(s_used, 1)
                    ins.then_inc(done, 1)
                pe.wait_ge(s_ohw, i + 1)
                pe.wait_ge(s_free45, i + 1)
                for t in range(NT):
                    ins = pe.transpose(CT[:, toks(t)], ohw[lanes(t), t, :], ident[lanes(t), lanes(t)])
                    if t == 0:
                        ins.then_inc(s_used, 1)
                ins.then_inc(s_cT, 1)
                pe.wait_ge(s_oh, i + 2)
                gather().then_inc(s_xg, 1)
                pe.wait_ge(s_actr, i + 1)
                for j in range(4):
                    ins = pe.transpose(AT[:, j * P:(j + 1) * P], act_sb[:, j * P:(j + 1) * P], ident)
                ins.then_inc(s_aT, 1)
                pe.wait_ge(s_xgs, i + 2)
                turn_gathered().then_inc(s_xgt, 1)
                pe.wait_ge(s_aTs, i + 1)
                for g in range(4):
                    pe.wait_ge(s_gr[8 + g], i * 16 + 16)
                    for j in range(2):
                        k = 2 * g + j
                        for c in range(2):
                            ins = pe.matmul(Y[hp(c), :], in_slice(actT, k), gran[8 + g][:, j, halves(c)],
                                            start=(k == 0), stop=(k == KD - 1))
                    if g < 3:
                        ins.then_inc(s_used, 1)
                ins.then_inc(s_y, 1)
                pe.wait_ge(s_ys, i + 1)
                pe.wait_ge(s_c, i + 1)
                pe.wait_ge(s_free67, i + 1)
                for t, banks in ((0, (GATE, UP)), (1, (bank[6], bank[7]))):
                    for c in range(2):
                        ins = pe.matmul(banks[c][:, :], comb[hp(c), toks(t)], y_sb[hp(c), :], start=True, stop=True)
                        if t == 0 and c == 0:
                            ins.then_inc(s_used, 1)
                    ins.then_inc(s_mix, 1)
                for c, out in enumerate((AT, CT)):
                    ins = pe.matmul(out[0:NS, :], comb[hp(c), toks(2)], y_sb[hp(c), :], start=True, stop=True)
                ins.then_inc(s_mix, 1)

            pe.wait_ge(s_oh, 1)
            for name in [("bd", t, half) for t in range(NT) for half in range(2)]:
                wait_drained(pe, name)
            gather().then_inc(s_xg, 1)
            pe.wait_ge(s_xgs, 1)
            turn_gathered().then_inc(s_xgt, 1)
            pe.wait_ge(ld["bias"], 32)
            with pe.Fori(0, NE) as i:
                expert(i)
            pe.wait_ge(s_tab, 1)
            more = pe.value_load(flag)
            with pe.If(more > 0):
                with pe.Fori(1, NBLK) as b:
                    with pe.Fori(0, NE) as e:
                        expert(b * NE + e)

            turn_rows("h3T", h3, lambda t: (s_rows, t + 7))
            pe.wait_ge(ld["ptok"], 32)
            for k in range(2):
                begin(("pT", k))
                for t in range(NT):
                    ins = pe.transpose(job_bank(("pT", k))[:, toks(t)], ptok[lanes(t), t, k * P:(k + 1) * P],
                                       ident[lanes(t), lanes(t)])
                fill_done(ins, ("pT", k))
            pe.wait_ge(ld["ple"], 32)
            wait_turned("h3T")
            wait_drained(pe, ("pT", 1))
            for t in range(2):
                for half in range(2):
                    for tag, src, w, slices in (("pg", hT, wple, KD), ("pp", pT, wproj, 2)):
                        name = (tag, t, half)
                        begin(name)
                        for k in range(slices):
                            ins = pe.matmul(job_bank(name)[:, :], src[:, k, toks(t)], w[:, k, halves(half)],
                                            start=(k == 0), stop=(k == slices - 1))
                        fill_done(ins, name)
            product("pg", 2, hT, wple)
            product("pp", 2, pT, wproj, 2)

        @block.scalar
        def _(act):
            def copy_out(name, dst, src):
                wait_filled(act, name)
                drain_done(act.activation(dst, src, ACT.Copy), name)

            def turned(tag, dst):
                for t in range(NT):
                    for half in range(2 if t < 2 else 1):
                        name = (tag, t, half)
                        if drainer[name] == "a":
                            turned_bank(name, dst, copy_out)

            chain = [0]

            def rms(s, n, done):
                act.wait_ge(s_act, chain[0])
                act.activation(s, s, ACT.Sqrt, bias=eps[0:s.shape[0]], scale=1.0 / n).then_inc(done, 1)

            def sum_squares(src, dst, s):
                chain[0] += 1
                act.activation(dst, src, ACT.Square, accum_out=s).then_inc(s_act, 1)

            def squares(scratch, count):
                for t in range(NT):
                    for tag in after_x[count]:
                        wait_drained(act, (tag, t, 1))
                    s = stat[lanes(t), 4 * count + t:4 * count + t + 1]
                    sum_squares(x[lanes(t), t, :], scratch[lanes(t)], s)
                    rms(s, D, s_sumsq)

            act.wait_ge(s_x, 48)
            act.wait_ge(s_const, 1)
            squares(view(TMP, D), 0)
            turned("hT", hT)
            act.wait_ge(s_lb, 1)
            act.activation(lbt[:, 0:16], lbt[:, 0:16], ACT.Exp).then_inc(s_lbe, 1)
            for h in range(H):
                wait_filled(act, ("f", h))
                drain_done(act.activation(fh[:, h, :], job_bank(("f", h))[:, 0:T], ACT.Sigmoid), ("f", h))
            act.wait_ge(s_fdone, 1)
            act.activation(fh[:, :, 0:SEQ], fh[:, :, 0:SEQ], ACT.Ln).then_inc(s_prepa, 1)
            act.wait_ge(s_prep, 1)
            act.activation(t1[:, :, 0:SEQ], t2[:, :, 0:SEQ], ACT.Exp).then_inc(s_prepa, 1)
            act.wait_ge(s_prep, 2)
            act.activation(fh[:, :, 0:SEQ], fh[:, :, 0:SEQ], ACT.Exp).then_inc(s_prepa, 1)
            act.activation(ebl, t2[:, :, CH - 1:SEQ:CH], ACT.Exp).then_inc(s_prepa, 1)
            for h in range(H):
                wait_filled(act, ("q", h))
                act.activation(qh[:, h, :], job_bank(("q", h))[:, 0:T], ACT.Sigmoid).then_inc(s_sig, 1)
            act.wait_ge(s_prep, 4)
            act.activation(t1[:, :, 0:SEQ], t2[:, :, 0:SEQ], ACT.Exp, scale=-1.0).then_inc(s_prepa, 1)

            n_tmp = [0]

            def to_tmp(name, rows, src, func):
                m = n_tmp[0]
                n_tmp[0] += 1
                wait_filled(act, name)
                if m >= 2:
                    wait_drained(act, tmp_jobs[m - 2])
                act.activation(tmp[m % 2][rows], src, func).then_inc(s_tfull, 1)

            def gate_chunk(kind, n):
                for t in range(2):
                    to_tmp((kind, n, t), slice(0, P), job_bank((kind, n, t))[:, :], ACT.Sigmoid)

            copy_out(("v", 0, 0), v[:, 0, halves(0)], job_bank(("v", 0, 0))[:, :])
            copy_out(("v", 1, 0), v[:, 0, halves(1)], job_bank(("v", 1, 0))[:, :])
            gate_chunk("g", 0)
            gate_chunk("g", 1)
            gate_chunk("ga", 0)
            act.wait_ge(s_prep, 5)
            for t in range(2):
                for half in range(2):
                    name = ("kT", t, half)
                    copy_out(name, ktok[:, t, halves(half)], job_bank(name)[:, :])
            for j in range(4):
                to_tmp(("g", "s", j), slice(0, NS), bank[4][32 * j:32 * j + NS, :], ACT.Sigmoid)
            gate_chunk("ga", 1)

            def decay(b):
                for h in range(H):
                    ins = act.activation(s0[:, b, h, :], s0[:, b, h, :], ACT.Copy, scale=fs[:, h, b:b + 1])
                ins.then_inc(s_decay, 1)

            act.wait_ge(ld["s0"], 16 * NS)
            for t in range(2):
                for b in range(4 * t, 4 * t + 4):
                    decay(b)
                for half in range(2):
                    name, m = ("o", t, half), n_tmp[0]
                    n_tmp[0] += 1
                    wait_filled(act, name)
                    wait_drained(act, tmp_jobs[m - 2])
                    for j in range(4):
                        hh = slice(j * P, (j + 1) * P)
                        sum_squares(job_bank(name)[:, hh], tmp[m % 2][:, hh],
                                    stat[:, 16 + 4 * (m % 2) + j:17 + 4 * (m % 2) + j])
                    rms(stat[:, 16 + 4 * (m % 2):20 + 4 * (m % 2)], P, s_tfull)
            act.wait_ge(s_sel8, 1)
            copy_out(("u", 0, 0), u[:, 0, halves(0)], job_bank(("u", 0, 0))[:, :])
            copy_out(("u", 1, 0), u[:, 0, halves(1)], job_bank(("u", 1, 0))[:, :])
            act.wait_ge(s_stst, 16)

            def pool_gate(n):
                for t in range(2):
                    name = ("gb", n, t)
                    wait_filled(act, name)
                    drain_done(act.activation(gb[:, t, halves(n)], job_bank(name)[:, :], ACT.Sigmoid), name)

            pool_gate(0)
            for j in range(4):
                name = ("u", "s", j)
                wait_filled(act, name)
                dst = (u if j < 2 else gb)[0:NS, 2, halves(j % 2)]
                drain_done(act.activation(dst, bank[4][32 * j:32 * j + NS, :], ACT.Copy if j < 2 else ACT.Sigmoid), name)
            pool_gate(1)
            wait_drained(act, ("os",))
            wait_drained(act, ("o", 1, 1))
            for h in range(H):
                sum_squares(v[0:NS, 2, h * P:(h + 1) * P], view(TMP + h * P, P, NS), stat[0:NS, 16 + h:17 + h])
            rms(stat[0:NS, 16:24], P, s_osq)
            for c in range(0, KD, 2):
                copy_out(("dT", c), dT[:, c, :], job_bank(("dT", c))[:, 0:T])
            turned("mT", mT)
            squares(view(TMP, D), 1)
            turned("h2T", hT)
            act.wait_ge(s_rt, 1)
            act.activation(exw, exw, ACT.Exp).then_inc(s_rta, 1)

            act.wait_ge(s_xg, 1)
            act.activation(xg_tok, bank[3][:, :], ACT.Copy).then_inc(s_xgs, 1)
            act.wait_ge(s_xgt, 1)
            act.activation(xT_e, bank[3][:, :], ACT.Copy).then_inc(s_xe, 1)

            def expert(i):
                act.wait_ge(s_gclip, i + 1)
                act.activation(sig_sb, g_sb, ACT.Sigmoid, scale=ALPHA).then_inc(s_gsig, 1)
                act.wait_ge(s_cT, i + 1)
                act.activation(comb, bank[5][:, 0:T], ACT.Copy).then_inc(s_c, 1)
                act.wait_ge(s_xg, i + 2)
                act.activation(xg_tok, bank[3][:, :], ACT.Copy).then_inc(s_xgs, 1)
                act.wait_ge(s_xgt, i + 2)
                act.activation(xT_e, bank[3][:, :], ACT.Copy).then_inc(s_xe, 1)
                act.wait_ge(s_y, i + 1)
                act.activation(y_sb, bank[2][:, :], ACT.Copy).then_inc(s_ys, 1)

            with act.Fori(0, NE) as i:
                expert(i)
            act.wait_ge(s_tab, 1)
            more = act.value_load(flag)
            with act.If(more > 0):
                with act.Fori(1, NBLK) as b:
                    with act.Fori(0, NE) as e:
                        expert(b * NE + e)

            act.wait_ge(s_end, 1)
            squares(sq, 2)
            turned("h3T", hT)
            for k in range(2):
                name = ("pT", k)
                copy_out(name, pT[:, k, :], job_bank(name)[:, 0:T])
            for t in range(NT):
                for half in range(2):
                    name = ("pg", t, half)
                    src = job_bank(name)[:, :] if t < 2 else bank[6][32 * half:32 * half + NS, :]
                    wait_filled(act, name)
                    drain_done(act.activation(pgs[lanes(t), t, halves(half)], src, ACT.Sigmoid), name)
            for t in range(NT):
                act.wait_ge(s_xfin, t + 1)
                s = stat[lanes(t), 12 + t:13 + t]
                sum_squares(x[lanes(t), t, :], sq[lanes(t)], s)
                rms(s, D, s_sumsq)

        @block.vector
        def _(dve):
            chain = [0]

            def step(ins):
                chain[0] += 1
                ins.then_inc(s_dve, 1)
                dve.wait_ge(s_dve, chain[0])

            def copy_out(name, dst, src):
                wait_filled(dve, name)
                drain_done(dve.tensor_copy(dst, src), name)

            def turned(tag, dst):
                for t in range(NT):
                    for half in range(2 if t < 2 else 1):
                        name = (tag, t, half)
                        if drainer[name] == "v":
                            turned_bank(name, dst, copy_out)

            def normalise(count, gain, dst):
                for t in range(NT):
                    dve.wait_ge(s_sumsq, 3 * count + t + 1)
                    s = stat[lanes(t), 4 * count + t:4 * count + t + 1]
                    step(dve.reciprocal(s, s))
                    dve.scalar_tensor_tensor(dst[lanes(t), t, :], x[lanes(t), t, :], s, gain[lanes(t)],
                                             ALU.mult, ALU.mult).then_inc(s_rows, 1)

            dve.wait_ge(s_const, 1)
            for g, w in enumerate(WINDOWS):
                dve.tensor_scalar(dw8[:, g, :], ident[0:NS, 0:NS], 1.0 / w - 1.0, None, ALU.mult)
            dve.wait_ge(ld["gmix"], 16)
            normalise(0, gmix_b, htok)
            l0, l1, m = lbt[:, 0:8], lbt[:, 8:16], lbt[:, 16:24]
            wait_filled(dve, ("lb",))
            drain_done(dve.tensor_copy(lbt[:, 0:16], bank[7][:, 0:16]), ("lb",))
            wait_drained(dve, ("lb",))
            step(dve.tensor_tensor(m, l0, l1, ALU.max))
            dve.tensor_tensor(l0, l0, m, ALU.subtract)
            dve.tensor_tensor(l1, l1, m, ALU.subtract).then_inc(s_lb, 1)
            turned("hT", hT)
            dve.wait_ge(s_lbe, 1)
            step(dve.tensor_tensor(m, l0, l1, ALU.add))
            step(dve.reciprocal(m, m))
            step(dve.tensor_tensor(lb, l0, m, ALU.mult))
            step(dve.tensor_scalar(omlb, lb, -1.0, 1.0, ALU.mult, ALU.add))
            tmask = view(TMP, SEQ)
            step(dve.memset(tmask, 1.0))
            dve.memset(tmask[:, 0:SEQ:CH], 0.0)

            for h in range(H):
                wait_drained(dve, ("f", h))
                ins = dve.tensor_scalar(fh[:, h, :], fh[:, h, :], omlb[:, h:h + 1], lb[:, h:h + 1], ALU.mult, ALU.add)
            step(ins)
            step(dve.tensor_scalar(kh, fh, -1.0, 1.0, ALU.mult, ALU.add))
            dve.tensor_copy(ks, kh[:, :, SEQ:T])
            dve.tensor_copy(fs, fh[:, :, SEQ:T]).then_inc(s_fdone, 1)
            dve.wait_ge(s_prepa, 1)
            for h in range(H):
                ins = dve.tensor_tensor_scan(t2[:, h, 0:SEQ], tmask, fh[:, h, 0:SEQ], 0.0, ALU.mult, ALU.add)
            ins.then_inc(s_prep, 1)
            dve.wait_ge(s_prep, 1)
            b4 = [a[:, :, 0:SEQ].rearrange("p h (n c) -> p h n c", c=CH) for a in (fh, t2)]
            for h in range(H):
                ins = dve.tensor_tensor(b4[0][:, h], b4[1][:, h, :, CH - 1:CH].to_broadcast([P, NCH, CH]), b4[1][:, h],
                                        ALU.subtract)
            ins.then_inc(s_prep, 1)
            dve.wait_ge(s_prepa, 3)
            dve.tensor_tensor(fh[:, :, 0:SEQ], fh[:, :, 0:SEQ], kh[:, :, 0:SEQ], ALU.mult).then_inc(s_prep, 1)
            for h in range(H):
                dve.wait_ge(s_sig, h + 1)
                drain_done(dve.tensor_tensor(qh[:, h, :], job_bank(("q", h))[:, 0:T], qh[:, h, :], ALU.mult), ("q", h))
            wait_drained(dve, ("q", H - 1))
            dve.tensor_tensor(qh[:, :, 0:SEQ], qh[:, :, 0:SEQ], t1[:, :, 0:SEQ], ALU.mult).then_inc(s_prep, 1)
            dve.wait_ge(s_prepa, 5)
            dve.tensor_tensor(t1[:, :, 0:SEQ], t1[:, :, 0:SEQ], kh[:, :, 0:SEQ], ALU.mult).then_inc(s_prep, 1)

            n_tmp = [0]

            def tmp_full():
                n_tmp[0] += 1
                dve.wait_ge(s_tfull, n_tmp[0])
                return tmp[(n_tmp[0] - 1) % 2]

            def gate_chunk(kind, n):
                for t in range(2):
                    name = (kind, n, t)
                    o = og[:, t, halves(n)]
                    w = tmp_full()
                    src = job_bank(name)[:, :] if kind == "g" else o
                    drain_done(dve.tensor_tensor(o, src, w, ALU.mult), name)

            copy_out(("v", 0, 1), v[:, 1, halves(0)], job_bank(("v", 0, 1))[:, :])
            for j in range(2):
                copy_out(("v", "s", j), v[0:NS, 2, halves(j)], bank[4][32 * j:32 * j + NS, :])
            copy_out(("v", 1, 1), v[:, 1, halves(1)], job_bank(("v", 1, 1))[:, :])
            gate_chunk("g", 0)
            gate_chunk("g", 1)
            wait_drained(dve, ("g", 1, 1))
            gate_chunk("ga", 0)
            dve.wait_ge(s_sczero, 1)
            dve.wait_ge(s_const, 2)
            for t in range(2):
                for half in range(2):
                    name = ("score", t, half)
                    wait_filled(dve, name)
                    drain_done(dve.copy_predicated(score[:, 2 * t + half, :].rearrange("p (h c) -> p h c", h=4),
                                                   cmask.unsqueeze(1).to_broadcast([P, 4, P]),
                                                   job_bank(name)[:, :].rearrange("p (h c) -> p h c", h=4)), name)
            for j in range(4):
                w = tmp_full()
                o = og[0:NS, 2, halves(j % 2)]
                if j == 2:
                    wait_drained(dve, ("g", "s", 1))
                src = bank[4][32 * j:32 * j + NS, :] if j < 2 else o
                drain_done(dve.tensor_tensor(o, src, w[0:NS], ALU.mult), ("g", "s", j))
            gate_chunk("ga", 1)

            def head_norm(name, rows, t, half):
                tmp_full()
                s = stat[:, 16 + 4 * ((n_tmp[0] - 1) % 2):20 + 4 * ((n_tmp[0] - 1) % 2)]
                step(dve.reciprocal(s, s))
                for j in range(4):
                    hh = slice((4 * half + j) * P, (4 * half + j + 1) * P)
                    ins = dve.scalar_tensor_tensor(og[rows, t, hh], job_bank(name)[rows, j * P:(j + 1) * P],
                                                   s[:, j:j + 1], og[rows, t, hh], ALU.mult, ALU.mult)
                drain_done(ins, name)

            for n in range(NCH):
                if n >= 1:
                    wait_drained(dve, ("dS", n - 1, 1))
                if n >= 2:
                    dve.wait_ge(s_inter, n)
                for half in range(2):
                    name = ("dS", n, half)
                    if n == 0:
                        copy_out(name, state[1][:, 4 * half:4 * half + 4, :],
                                 job_bank(name)[:, :].rearrange("p (h v) -> p h v", h=4))
                        continue
                    wait_filled(dve, name)
                    for j in range(4):
                        h = 4 * half + j
                        ins = dve.scalar_tensor_tensor(state[(n + 1) % 2][:, h, :], state[n % 2][:, h, :],
                                                       ebl[:, h, n:n + 1], job_bank(name)[:, j * P:(j + 1) * P],
                                                       ALU.mult, ALU.add)
                    drain_done(ins, name)
                if n % 4 == 3:
                    t = n // 4
                    dve.wait_ge(s_ogp, t + 1)
                    for half in range(2):
                        head_norm(("o", t, half), slice(0, P), t, half)
            dve.wait_ge(s_sel8, 1)
            copy_out(("u", 0, 1), u[:, 1, halves(0)], job_bank(("u", 0, 1))[:, :])
            copy_out(("u", 1, 1), u[:, 1, halves(1)], job_bank(("u", 1, 1))[:, :])
            for b in range(NS):
                dve.wait_ge(s_decay, b + 1)
                for half in range(2):
                    name = ("vb", b, half)
                    wait_filled(dve, name)
                    for j in range(4):
                        h = 4 * half + j
                        ins = dve.scalar_tensor_tensor(s0[:, b, h, :], job_bank(name)[:, j * P:(j + 1) * P],
                                                       ks[:, h, b:b + 1], s0[:, b, h, :], ALU.mult, ALU.add)
                    drain_done(ins, name)
            name = ("os",)
            wait_filled(dve, name)
            osb = v[0:NS, 2, :].rearrange("p (a j v) -> p j a v", a=2, j=4)
            for j in range(4):
                ins = dve.tensor_copy(osb[:, j], bank[7][32 * j:32 * j + NS, 0:2 * P].rearrange("p (a v) -> p a v", a=2))
            drain_done(ins, name)
            wait_drained(dve, name)
            flat, s = v[0:NS, 2, :], stat[0:NS, 16:24]
            by_head = flat.rearrange("p (h v) -> p h v", h=H)
            dve.wait_ge(s_osq, 1)
            step(dve.reciprocal(s, s))
            step(dve.tensor_tensor(by_head, by_head, s.unsqueeze(2).to_broadcast([NS, H, P]), ALU.mult))
            dve.wait_ge(s_ogp, NT)
            dve.tensor_tensor(og[0:NS, 2, :], og[0:NS, 2, :], flat, ALU.mult)
            for c in range(1, KD, 2):
                copy_out(("dT", c), dT[:, c, :], job_bank(("dT", c))[:, 0:T])
            dve.wait_ge(ld["pscale"], 16)
            wait_drained(dve, ("gb", 1, 1))
            for t in range(NT):
                step(dve.tensor_tensor(gb[lanes(t), t, :], gb[lanes(t), t, :], pscale_b[lanes(t)], ALU.mult))
            for t in range(NT):
                for half in range(2):
                    name = ("yp", t, half)
                    wait_filled(dve, name)
                    o = gb[lanes(t), t, halves(half)]
                    drain_done(dve.tensor_tensor(o, job_bank(name)[lanes(t), :], o, ALU.mult), name)
                wait_drained(dve, name)
                dve.tensor_tensor(og[lanes(t), t, :], og[lanes(t), t, :], gb[lanes(t), t, :], ALU.add)\
                   .then_inc(s_merged, 1)
            turned("mT", mT)

            def add_to_x(tag, t, half):
                name = (tag, t, half)
                wait_filled(dve, name)
                xs = x[lanes(t), t, halves(half)]
                src = job_bank(name)[:, :] if t < 2 else job_bank(name)[32 * half:32 * half + NS, :]
                drain_done(dve.tensor_tensor(xs, src, xs, ALU.add), name)

            for t in range(NT):
                for half in range(2):
                    add_to_x("x1", t, half)
            dve.wait_ge(ld["gffn"], 16)
            normalise(1, gffn_b, h2)
            turned("h2T", hT)

            dve.wait_ge(ld["br"], 16)
            wait_filled(dve, ("lgT",))
            drain_done(dve.tensor_scalar(lgT, bank[6][0:NE, 0:T], brt, None, ALU.add), ("lgT",))
            step(dve.memset(lg, 0.0))
            wait_filled(dve, ("lg",))
            dve.tensor_copy(lg[:, 0:2, :], bank[7][:, 0:2 * NE].rearrange("p (t e) -> p t e", t=2))
            drain_done(dve.tensor_copy(lg[0:NS, 2, :], bank[7][0:NS, 2 * NE:3 * NE]), ("lg",))
            wait_drained(dve, ("lg",))
            for t in range(NT):
                ins = dve.max(top[:, t, :], lg[:, t, :])
            step(ins)
            for t in range(NT):
                ins = dve.max_index(topi[:, t, :], top[:, t, :], lg[:, t, :])
            step(ins)
            dve.tensor_copy(topf, topi)
            dve.tensor_tensor(exw, top[:, :, 0:TOPK], top[:, :, 0:1].to_broadcast([P, NT, TOPK]), ALU.subtract)\
               .then_inc(s_rt, 1)
            dve.wait_ge(s_rta, 1)
            step(dve.tensor_reduce(ssum, exw, AX_X, ALU.add))
            step(dve.reciprocal(rsum, ssum))
            step(dve.tensor_tensor(exw, exw, rsum.to_broadcast([P, NT, TOPK]), ALU.mult))
            experts = iota[:, 0:NE].unsqueeze(1).to_broadcast([P, NT, NE])
            for k in range(TOPK):
                hit, dst_m, dst_w = (msk, msk, wdn) if k == 0 else (isk, tmpr, tmpw)
                step(dve.tensor_tensor(hit, experts, topf[:, :, k:k + 1].to_broadcast([P, NT, NE]), ALU.is_equal))
                if k == 0:
                    ins = dve.tensor_tensor(wdn, hit, exw[:, :, 0:1].to_broadcast([P, NT, NE]), ALU.mult)
                    step(ins)
                    continue
                step(dve.tensor_tensor(tmpw, hit, exw[:, :, k:k + 1].to_broadcast([P, NT, NE]), ALU.mult))
                step(dve.tensor_tensor(msk, msk, hit, ALU.add))
                ins = dve.tensor_tensor(wdn, wdn, tmpw, ALU.add)
                if k < TOPK - 1:
                    step(ins)
            ins.then_inc(s_rt, 1)
            dve.wait_ge(s_rt, 2)
            wait_filled(dve, ("rank",))
            for b in range(NBLK):
                cols = slice(b * NE, (b + 1) * NE)
                ins = dve.scalar_tensor_tensor(slot_tab[:, :, cols],
                                               bank[0][:, 0:NT * NE].rearrange("p (t e) -> p t e", t=NT),
                                               FAR - CAP * b, msk, ALU.add, ALU.mult)
                dve.tensor_copy(wt_tab[:, :, cols], wdn)
                dve.tensor_copy(eis[:, cols], ident[0:NE, 0:NE])
            step(dve.memset(slot_tab[:, :, NTAB - 1:NTAB], 0.0))
            drain_done(dve.tensor_scalar(slot_tab, slot_tab, -FAR, None, ALU.add), ("rank",))
            wait_filled(dve, ("count",))
            drain_done(dve.tensor_reduce(stat[0:8, 16:17], bank[1][0:8, 0:NE], AX_X, ALU.max), ("count",))
            wait_drained(dve, ("count",))
            dve.tensor_scalar(flag, stat[0:1, 16:17], CAP + 0.5, None, ALU.is_gt).then_inc(s_tab, 1)
            copy_out(("wT",), wT, bank[2][0:NE, 0:T])
            dve.memset(wt_tab[:, :, NTAB - 1:NTAB], 0.0).then_inc(s_free01, 1)
            dve.memset(eis[:, NTAB - 1:NTAB], 0.0).then_inc(s_free67, 1)
            step(dve.memset(stat[:, 20:21], 0.0))
            dve.memset(stat[:, 21:22], 0.0).then_inc(s_free45, 1)

            def select_tokens(i, weighted):
                for t in range(NT):
                    if weighted:
                        ins = dve.tensor_scalar(ohw[:, t, :], iota, slot_tab[:, t, bass.ds(i, 1)],
                                                wt_tab[:, t, bass.ds(i, 1)], ALU.is_equal, ALU.mult)
                    else:
                        ins = dve.tensor_scalar(oh[:, t, :], iota[:, 0:CAP], slot_tab[:, t, bass.ds(i, 1)], None,
                                                ALU.is_equal)
                ins.then_inc(s_ohw if weighted else s_oh, 1)

            def select_expert(i):
                dve.tensor_scalar(esel, ones[0:NE, 0:CAP], eis[:, bass.ds(i, 1)], None, ALU.mult).then_inc(s_esel, 1)

            select_tokens(0, False)
            select_expert(0)
            for t in range(NT):
                for half in range(2):
                    add_to_x("bd", t, half)
            wait_drained(dve, ("bd", 2, 1))

            def expert(i):
                dve.wait_ge(s_xg, i + 1)
                select_tokens(i + 1, False)
                select_tokens(i, True)
                dve.wait_ge(s_gate, i + 1)
                dve.tensor_scalar(g_sb, bank[0][:, :], LIMIT, None, ALU.min).then_inc(s_gclip, 1)
                dve.wait_ge(s_up, i + 1)
                dve.tensor_scalar(u_sb, bank[1][:, :], LIMIT, -LIMIT, ALU.min, ALU.max).then_inc(s_uclip, 1)
                select_expert(i + 1)
                dve.wait_ge(s_gsig, i + 1)
                dve.tensor_tensor(g_sb, g_sb, sig_sb, ALU.mult).then_inc(s_dloop, 1)
                dve.wait_ge(s_dloop, i + 1)
                dve.wait_ge(s_uclip, i + 1)
                dve.scalar_tensor_tensor(act_sb, u_sb, 1.0, g_sb, ALU.add, ALU.mult).then_inc(s_actr, 1)
                dve.wait_ge(s_aT, i + 1)
                dve.tensor_copy(actT, bank[4][:, :]).then_inc(s_aTs, 1)
                for t, banks, done in ((0, bank[0:2], s_free01), (1, bank[6:8], s_free67), (2, bank[4:6], s_free45)):
                    dve.wait_ge(s_mix, 3 * i + t + 1)
                    for c in range(2):
                        xs = x[lanes(t), t, halves(c)]
                        ins = dve.tensor_tensor(xs, banks[c][lanes(t), :], xs, ALU.add)
                    ins.then_inc(done, 1)
                dve.wait_ge(s_free45, i + 2)

            with dve.Fori(0, NE) as i:
                expert(i)
            more = dve.value_load(flag)
            with dve.If(more > 0):
                with dve.Fori(1, NBLK) as b:
                    with dve.Fori(0, NE) as e:
                        expert(b * NE + e)

            dve.memset(stat[:, 22:23], 0.0).then_inc(s_end, 1)
            dve.wait_ge(ld["gple"], 16)
            normalise(2, gple_b, h3)
            turned("h3T", hT)
            dve.wait_ge(ld["gfin"], 16)
            for t in range(NT):
                for half in range(2):
                    name = ("pp", t, half)
                    wait_filled(dve, name)
                    wait_drained(dve, ("pg", t, half))
                    src = job_bank(name)[:, :] if t < 2 else bank[4][32 * half:32 * half + NS, :]
                    o = pgs[lanes(t), t, halves(half)]
                    drain_done(dve.tensor_tensor(o, src, o, ALU.mult), name)
                wait_drained(dve, name)
                xs = x[lanes(t), t, :]
                dve.tensor_tensor(xs, xs, pgs[lanes(t), t, :], ALU.add).then_inc(s_xfin, 1)
            for t in range(NT):
                dve.wait_ge(s_sumsq, 9 + t + 1)
                s = stat[lanes(t), 12 + t:13 + t]
                step(dve.reciprocal(s, s))
                dve.scalar_tensor_tensor(yout[lanes(t), t, :], x[lanes(t), t, :], s, gfin_b[lanes(t)],
                                         ALU.mult, ALU.mult).then_inc(s_yout, 1)


_INS = ["x_prompt", "x_sample", "p_prompt", "p_sample", "state_hgrn", "state_pool", "g_mix", "w_in",
        "hg_lb_logits", "hg_norm", "w_pool", "pool_scale", "w_out", "g_ffn", "w_router", "b_router", "w_gate",
        "b_gate", "w_up", "b_up", "w_down", "b_down", "g_ple", "w_ple_gate", "w_ple_proj", "g_final"]
_OUTS = [(1, SEQ, D), (NS, 1, D), (1, 1, H, P, P), (1, 1, BUF, D), (1, NS, H, P, P), (1, NS, BUF, D)]


def kernel(**inputs):
    import concourse.bacc as _bacc
    from concourse.bass_utils import run_bass_kernel_spmd as _run

    nc = _bacc.Bacc("TRN2", target_bir_lowering=False, num_devices=1)
    arrays, args = {}, []
    for name in _INS:
        a = np.ascontiguousarray(inputs[name])
        arrays[f"in_{name}_dram"] = a
        args.append(nc.dram_tensor(f"in_{name}_dram", a.shape, mybir.dt.from_np(a.dtype), kind="ExternalInput").ap())
    for i, shape in enumerate(_OUTS):
        args.append(nc.dram_tensor(f"out_{i}_dram", shape, F32, kind="ExternalOutput").ap())
    build(nc, *args)
    r = _run(nc, [arrays], core_ids=[0])
    return tuple(r.results[0][f"out_{i}_dram"] for i in range(len(_OUTS)))
```

```python
from contextlib import ExitStack

import numpy as np

import concourse.bass as bass
from concourse import mybir

F32 = mybir.dt.float32
I32 = mybir.dt.int32
U32 = mybir.dt.uint32
ALU = mybir.AluOpType
ACT = mybir.ActivationFunctionType
AX_X = mybir.AxisListType.X

P = 128
D = 1024
SEQ = 256
NS = 8
T = SEQ + NS
TS = (P, P, NS)
NT = len(TS)
KD = D // P
H = 8
CH = 32
NCH = SEQ // CH
WINDOWS = (2, 4, 8, 16)
BUF = 15
NE = 32
TOPK = 4
CAP = 64
NBLK = -(-T // CAP)
NTAB = NBLK * NE + 2
LIMIT = 7.0
ALPHA = 1.702
EPS = 1e-6
FAR = 4096.0
HALF = 512
PLE = 256
GRAN = 2048
NGRAN = 3 * D * D // (P * GRAN)
RING = 16
PAIRS = NE // 2
PER = 2
assert PER * 2 * NGRAN % RING == 0 and PAIRS % (2 * PER) == 0

W_CHUNKS = [("f", 1024), ("f", 1536), ("q", 0), ("q", 512), ("v", 2048), ("v", 2560),
            ("g", 3072), ("g", 3584), ("ga", 5120), ("ga", 5632),
            ("u", 4096), ("u", 4608), ("gb", 6144), ("gb", 6656)]
NSLOT = 4


def bank_jobs():
    jobs = []

    def norm(tag):
        for t in range(NT):
            for half in range(2 if t < 2 else 1):
                n = 2 * t + half
                jobs.append(((tag, t, half), n, "av"[n % 2]))

    def chunk(kind, n, pair, drains):
        for t in range(2):
            jobs.append(((kind, n, t), 2 * pair + t, drains[t]))

    jobs.append((("lb",), 7, "v"))
    norm("hT")
    for kind, drain in (("f", "a"), ("q", "v")):
        for h in range(H):
            jobs.append(((kind, h), h % 4, drain))
    chunk("v", 0, 0, "av")
    jobs += [(("v", "s", j), 4, "v") for j in range(2)]
    chunk("v", 1, 1, "av")
    chunk("g", 0, 0, "vv")
    chunk("g", 1, 1, "vv")
    chunk("ga", 0, 0, "vv")
    for n in range(4):
        jobs.append((("score", n // 2, n % 2), 5 + n % 3, "v"))
    for n in range(4):
        jobs.append((("kT", n // 2, n % 2), 5 + (n + 1) % 3, "a"))
    jobs += [(("g", "s", j), 4, "v") for j in range(4)]
    chunk("ga", 1, 1, "vv")
    for n in range(NCH):
        jobs.append((("dS", n, 0), 4, "v"))
        jobs.append((("dS", n, 1), 7, "v"))
        if n % 4 == 3:
            for half in range(2):
                jobs.append((("o", n // 4, half), 5 + half, "v"))
    chunk("u", 0, 0, "av")
    chunk("u", 1, 1, "av")
    for b in range(NS):
        for half in range(2):
            jobs.append((("vb", b, half), 5 + (2 * b + half) % 2, "v"))
    chunk("gb", 0, 0, "aa")
    jobs += [(("u", "s", j), 4, "a") for j in range(4)]
    chunk("gb", 1, 1, "aa")
    jobs.append((("os",), 7, "v"))
    for c in range(KD):
        jobs.append((("dT", c), c % 4, "av"[c % 2]))
    for t in range(NT):
        for half in range(2):
            jobs.append((("yp", t, half), 4 + (2 * t + half) % 4, "v"))
    norm("mT")
    for t in range(2):
        for half in range(2):
            jobs.append((("x1", t, half), 2 * t + half, "v"))
    jobs += [(("x1", 2, half), 4, "v") for half in range(2)]
    norm("h2T")
    jobs.append((("lgT",), 6, "v"))
    jobs.append((("lg",), 7, "v"))
    jobs.append((("rank",), 0, "v"))
    jobs.append((("count",), 1, "v"))
    jobs.append((("wT",), 2, "v"))
    for t in range(2):
        for half in range(2):
            jobs.append((("bd", t, half), (0, 1, 6, 7)[2 * t + half], "v"))
    jobs += [(("bd", 2, half), 4, "v") for half in range(2)]
    jobs += [(("pT", k), 5 + k, "a") for k in range(2)]
    for t in range(2):
        for half in range(2):
            jobs.append((("pp", t, half), (7, 5, 6, 7)[2 * t + half], "a"))
    jobs += [(("pp", 2, half), 5, "a") for half in range(2)]
    norm("h3T")
    for t in range(2):
        for half in range(2):
            jobs.append((("pg", t, half), 4 * t + half, "a"))
    jobs += [(("pg", 2, half), 6, "a") for half in range(2)]
    return jobs


def build(nc, x_prompt, x_sample, p_prompt, p_sample, state_hgrn, state_pool, g_mix, w_in,
          hg_lb_logits, hg_norm, w_pool, pool_scale, w_out, g_ffn, w_router, b_router, w_gate, b_gate,
          w_up, b_up, w_down, b_down, g_ple, w_ple_gate, w_ple_proj, g_final,
          y_prompt, y_sample, new_hgrn_prompt, new_pool_prompt, new_hgrn_sample, new_pool_sample):
    jobs = bank_jobs()
    order = {name: n for n, (name, _, _) in enumerate(jobs)}
    drainer = {name: e for name, _, e in jobs}
    drain_count, before = {}, {}
    seen, last = {"a": 0, "v": 0}, {}
    for name, bank, e in jobs:
        seen[e] += 1
        drain_count[name] = seen[e]
        before[name] = last.get(bank)
        last[bank] = name

    with ExitStack() as ctx:
        def sem(name):
            return ctx.enter_context(nc.semaphore(name))

        arena = ctx.enter_context(nc.sbuf_tensor("arena", [P, 53200], F32))
        bank = [ctx.enter_context(nc.psum_tensor(f"bank{n}", [P, HALF], F32)) for n in range(8)]
        at = [0]

        def take(floats):
            at[0] += floats
            assert at[0] <= 53200, at[0]
            return at[0] - floats

        def view(start, floats, rows=P):
            return arena[0:rows, start:start + floats]

        R = take(NGRAN * GRAN)
        X = take(3 * D)
        HT = take(KD * T)
        HG = take(5 * KD * T)
        V = take(3 * D)
        OG = take(3 * D)
        TMP = take(2 * HALF)
        G0 = take(D)
        G12 = take(2 * D)
        ident = view(take(P), P)
        cmask = view(take(P), P).bitcast(I32)
        before_t = view(take(P), P)
        ones = view(take(P), P)
        BAND = take(4 * (144 + P))
        dm8 = view(take(64), 64).rearrange("p (b c) -> p b c", b=8)
        selw = view(take(32), 32).rearrange("p (g b) -> p g b", g=4)
        wr = view(take(KD * NE), KD * NE).rearrange("p (k e) -> p k e", k=KD)
        lb = view(take(8), 8)
        omlb = view(take(8), 8)
        lgin = view(OG, P)
        lbt = view(take(32), 32)
        hgn = view(take(P), P)
        brt = view(take(1), 1, NE)
        stat = view(take(32), 32)
        eps = view(take(1), 1)
        flag = view(take(1), 1, 1).bitcast(I32)
        fs = view(take(64), 64).rearrange("p (h b) -> p h b", h=H)
        ks = view(take(64), 64).rearrange("p (h b) -> p h b", h=H)
        ebl = view(take(64), 64).rearrange("p (h n) -> p h n", h=H)

        def rows3(start):
            return view(start, 3 * D).rearrange("p (t d) -> p t d", t=3)

        def heads(start):
            return view(start, KD * T).rearrange("p (k t) -> p k t", k=KD)

        x = rows3(X)
        hT = heads(HT)
        w_slot = [view(R + s * 4096, 4096).rearrange("p (k n) -> p k n", k=KD) for s in range(NSLOT)]
        s0 = view(R + 4 * 4096, 8192).rearrange("p (b h v) -> p b h v", b=NS, h=H)
        qh, fh, kh, t1, t2 = (heads(HG + n * KD * T) for n in range(5))
        score = view(HG + 4 * KD * T, 2048).rearrange("p (n c) -> p n c", n=4)
        ktok = view(HG + 2 * KD * T, 2048).rearrange("p (t k) -> p t k", t=2)
        sel8 = view(HG + 3 * KD * T, 1024, NS).rearrange("p (b k) -> p b k", b=NS)
        qm = view(HG + 3 * KD * T + 1024, 512).rearrange("p (h b c) -> p h b c", h=H, b=NS)
        state = [view(HG + KD * T + n * 1024, 1024).rearrange("p (h v) -> p h v", h=H) for n in range(2)]
        v = rows3(V)
        og = rows3(OG)
        tmp = [view(TMP + n * HALF, HALF) for n in range(2)]
        u = rows3(HG)
        gb = rows3(HG + 3072)
        dT = heads(HG + 6144)
        mT = heads(HG + 8256)
        htok = rows3(V)
        bufrows = view(V, D, NS * BUF)
        gmix_b = view(G0, D)
        pscale_b = view(G0, D)
        gffn_b = view(V + D, D)
        wpool = view(G12, 2048).rearrange("p (g k n) -> p g k n", g=4, k=2)
        wout = view(R + 8 * GRAN, 8192).rearrange("p (k n) -> p k n", k=KD)
        band0 = [view(BAND + g * 144, 144) for g in range(4)]
        band1 = [view(BAND + 4 * 144 + g * P, P) for g in range(4)]

        h2 = rows3(OG)
        gran = [view(R + g * GRAN if g < NGRAN else HG + (g - NGRAN) * GRAN, GRAN).rearrange(
            "p (j n) -> p j n", j=2) for g in range(RING)]
        wproj = view(HG + 8192, 2048).rearrange("p (k n) -> p k n", k=2)
        bias_g = view(V, D, NE)
        bias_u = view(V + D, D, NE)
        bias_d = view(V + 2 * D, D, NE)
        xT_e = view(G12, D)
        xg_tok = y_sb = sig_sb = view(G12 + D, D)
        g_sb = actT = view(TMP, D)
        u_sb = act_sb = view(G0, D)
        comb = view(BAND, T)
        slot_tab = view(HT, 3 * NTAB).rearrange("p (t c) -> p t c", t=3)
        wt_tab = view(HT + 3 * NTAB, 3 * NTAB).rearrange("p (t c) -> p t c", t=3)
        ohw = view(HT + 6 * NTAB, 3 * P).rearrange("p (t c) -> p t c", t=3)
        oh = view(HT + 6 * NTAB + 3 * P, 3 * P).rearrange("p (t c) -> p t c", t=3)
        esel = view(HT + 6 * NTAB + 6 * P, P, NE)
        eis = view(HT + 6 * NTAB + 7 * P, NTAB, NE)
        iota = view(take(P), P)
        dw8 = view(take(32), 32, NS).rearrange("p (g b) -> p g b", g=4)

        def small(n, k=1):
            start = G12 + small.at
            small.at += 3 * n
            return view(start, 3 * n).rearrange("p (t c) -> p t c", t=3)
        small.at = 0
        lg, msk, wdn, tmpr, tmpw, isk = (small(NE) for _ in range(6))
        top, topf, exw = small(8), small(8), small(4)
        topi = small(8).bitcast(U32)
        ssum, rsum = small(1), small(1)
        wT = view(HG + 10240, T, NE)
        lgT = view(G12 + small.at, T, NE)
        assert small.at + T <= 2048

        ptok = view(V + 2 * D, 3 * PLE).rearrange("p (t d) -> p t d", t=3)
        pT = view(G0, 2 * T).rearrange("p (k t) -> p k t", k=2)
        h3 = rows3(R + 8192)
        gple_b = view(R + 11264, D)
        gfin_b = view(R + 12288, D)
        pgs = rows3(R + 13312)
        yout = rows3(R + 16384)
        pps = rows3(R + 19456)
        sq = view(R + 22528, D)

        filled = sem("bank_filled")
        drained = {"a": sem("bank_drained_by_scalar"), "v": sem("bank_drained_by_vector")}
        s_pool = sem("pool_step")
        s_dve = sem("vector_step")
        s_act = sem("scalar_step")
        s_const = sem("constants_ready")
        s_x = sem("x_loaded")
        s_w = [sem(f"w_in_slot{n}_loaded") for n in range(NSLOT)]
        names = ("gmix pscale gffn lbin hgn br wr wpool s0 wout bufrows bias bdown ple wproj gple gfin ptok").split()
        ld = {n: sem(f"{n}_loaded") for n in names}
        s_rows = sem("normalised_rows_ready")
        s_sumsq = sem("squares_summed")
        s_osq = sem("sample_output_rms_ready")
        s_lb = sem("lower_bound_ready")
        s_lbe = sem("lower_bound_exponentials")
        s_sig = sem("sigmoid_in_sbuf")
        s_tfull = sem("tmp_filled")
        s_fdone = sem("forget_gate_ready")
        s_prep = sem("hgrn_vector_step")
        s_prepa = sem("hgrn_scalar_step")
        s_sczero = sem("score_buffer_zeroed")
        s_inter = sem("state_read_by_tensor")
        s_ogp = sem("output_gate_times_norm_gain")
        s_sel8 = sem("row_selectors_ready")
        s_decay = sem("sample_state_decayed")
        s_snst = sem("sample_state_stored")
        s_merged = sem("merged_ready")
        s_rt = sem("router_vector_step")
        s_rta = sem("router_exponentials")
        s_tab = sem("routing_tables_ready")
        s_oh = sem("token_selectors_ready")
        s_ohw = sem("weighted_selectors_ready")
        s_used = sem("granule_used")
        s_gr = [sem(f"granule{g}_loaded") for g in range(RING)]
        s_ust = sem("pooling_rows_stored")
        s_gbs = sem("pool_gate_scaled")
        s_gate = sem("gate_sums_ready")
        s_up = sem("up_sums_ready")
        s_gclip = sem("gate_clipped")
        s_gsig = sem("gate_sigmoid_ready")
        s_uclip = sem("up_clipped")
        s_actr = sem("activation_ready")
        s_xg = sem("gathered_rows_in_psum")
        s_xgs = sem("gathered_rows_in_sbuf")
        s_xgt = sem("gathered_rows_transposed")
        s_xe = sem("expert_input_ready")
        s_cT = sem("combine_matrix_in_psum")
        s_c = sem("combine_matrix_ready")
        s_aT = sem("activation_transposed")
        s_aTs = sem("activation_transposed_in_sbuf")
        s_y = sem("expert_output_in_psum")
        s_ys = sem("expert_output_in_sbuf")
        s_mix = sem("combined_rows_in_psum")
        s_free23, s_free45, s_free6 = (sem(f"banks_{n}_added_to_x") for n in ("23", "45", "6"))
        s_esel = sem("expert_selector_ready")
        s_end = sem("experts_done")
        s_stst = sem("prompt_state_stored")
        s_dloop = sem("vector_step_in_expert")
        s_xfin = sem("x_final")
        s_yout = sem("y_ready")
        s_out = sem("outputs_stored")
        n_out = [0]

        def fill_done(ins, name):
            ins.then_inc(filled, 1)

        def wait_filled(eng, name):
            eng.wait_ge(filled, order[name] + 1)

        def wait_drained(eng, name):
            eng.wait_ge(drained[drainer[name]], drain_count[name])

        def drain_done(ins, name):
            ins.then_inc(drained[drainer[name]], 1)

        def job_bank(name):
            return bank[jobs[order[name]][1]]

        def lanes(t):
            return slice(0, TS[t])

        def toks(t):
            return slice(t * P, t * P + TS[t])

        def halves(h):
            return slice(h * HALF, (h + 1) * HALF)

        last_use = [("f", 3), ("f", 7), ("q", 3), ("q", 7), ("v", "s", 1), ("v", 1, 1),
                    ("g", "s", 3), ("g", "s", 3), ("g", "s", 3), ("ga", 1, 1)]
        rows_of = state_pool.rearrange("o b j d -> (o b j) d")

        tmp_jobs = [("g", n, t) for n in range(2) for t in range(2)] + [("ga", 0, 0), ("ga", 0, 1)]
        tmp_jobs += [("g", "s", j) for j in range(4)] + [("ga", 1, 0), ("ga", 1, 1)]
        tmp_jobs += [("o", t, half) for t in range(2) for half in range(2)]
        after_x = [(), ("x1",), ()]

        def turned_bank(name, dst, copy):
            _, t, half = name
            n = TS[t]
            ks_ = slice(4 * half, 4 * half + 4) if t < 2 else slice(0, KD)
            src = job_bank(name)[:, 0:(ks_.stop - ks_.start) * n].rearrange("p (k t) -> p k t", t=n)
            copy(name, dst[:, ks_, toks(t)], src)

        block = ctx.enter_context(nc.Block())

        @block.sync
        def _(sp):
            xp = x_prompt[0].rearrange("(t p) d -> p t d", p=P)
            sp.dma_start(x[:, 0, :], xp[:, 0, :]).then_inc(s_x, 16)
            sp.dma_start(x[:, 1, :], xp[:, 1, :]).then_inc(s_x, 16)
            sp.dma_start(x[0:NS, 2, :], x_sample[:, 0, :]).then_inc(s_x, 16)
            wi = w_in[0].rearrange("(k p) n -> p k n", p=P)
            for c, (_, col) in enumerate(W_CHUNKS):
                if c >= NSLOT:
                    wait_filled(sp, last_use[c - NSLOT])
                sp.dma_start(w_slot[c % NSLOT], wi[:, :, col:col + HALF]).then_inc(s_w[c % NSLOT], 16)

            parts = [w.rearrange("o e (g j p) n -> (o e) g p j n", j=2, p=P) for w in (w_gate, w_up, w_down)]
            ple = w_ple_gate[0].rearrange("(g j p) n -> g p j n", j=2, p=P)

            def load_experts(i, e):
                for n in range(PER):
                    for m in range(3):
                        for g in range(4):
                            for one in range(2):
                                at_ = 2 * NGRAN * n + 8 * m + 2 * g + one
                                sp.wait_ge(s_used, 2 * NGRAN * i + at_ + 1)
                                sp.dma_start(gran[at_ % RING], parts[m][e + 2 * n + one, g])\
                                  .then_inc(s_gr[at_ % RING], 16)

            def load_ple():
                for g in range(4):
                    sp.dma_start(gran[g], ple[g]).then_inc(ld["ple"], 16)

            sp.wait_ge(s_ust, 32)
            with sp.Fori(0, PAIRS // PER) as q:
                load_experts(PER * q, 2 * PER * q)
            sp.wait_ge(s_used, NGRAN * NE + 4)
            load_ple()
            more = sp.value_load(flag)
            with sp.If(more > 0):
                sp.wait_ge(ld["ple"], 64)
                with sp.Fori(1, NBLK) as b:
                    with sp.Fori(0, PAIRS // PER) as q:
                        load_experts(b * PAIRS + PER * q, 2 * PER * q)
                sp.wait_ge(s_used, NGRAN * NE * NBLK + 4)
                load_ple()

        @block.gpsimd
        def _(pool):
            chain = [0]

            def step(ins):
                chain[0] += 1
                ins.then_inc(s_pool, 1)
                pool.wait_ge(s_pool, chain[0])

            def store(dst, src):
                pool.dma_start(dst, src).then_inc(s_out, 16)
                n_out[0] += 1

            step(pool.memset(ident, 0.0))
            step(pool.affine_select(out=ident, in_=ident, compare_op=ALU.not_equal, fill=1.0, base=0,
                                    pattern=[[-1, P]], channel_multiplier=1))
            step(pool.memset(ones, 1.0))
            step(pool.memset(eps, EPS))
            pool.memset(stat, 0.0).then_inc(s_const, 1)
            for b in range(NS):
                pool.dma_start(s0[:, b], state_hgrn[0, b].rearrange("h k v -> k h v")).then_inc(ld["s0"], 16)
            step(pool.memset(before_t, 1.0))
            step(pool.affine_select(out=before_t, in_=before_t, compare_op=ALU.is_gt, fill=0.0, base=0,
                                    pattern=[[1, P]], channel_multiplier=-1))
            cm = iota
            step(pool.memset(cm, 1.0))
            step(pool.affine_select(out=cm, in_=cm, compare_op=ALU.is_ge, fill=0.0, base=0,
                                    pattern=[[1, P]], channel_multiplier=-1))
            step(pool.affine_select(out=cm, in_=cm, compare_op=ALU.is_ge, fill=0.0, base=0,
                                    pattern=[[-CH, P // CH], [0, CH]], channel_multiplier=1))
            step(pool.tensor_copy(cmask, cm))
            step(pool.iota(iota.rearrange("p (c n) -> p c n", c=2), [[0, 2], [1, CAP]], base=0,
                           channel_multiplier=0, allow_small_or_imprecise_dtypes=True))
            step(pool.memset(dm8, 0.0))
            step(pool.affine_select(out=dm8, in_=dm8, compare_op=ALU.not_equal, fill=1.0, base=0,
                                    pattern=[[1, 8], [-1, 8]], channel_multiplier=0))
            for g, w in enumerate(WINDOWS):
                step(pool.memset(band0[g], 1.0 / w))
                for t in range(w - 1):
                    pool.memset(band0[g][:, t:t + 1], 1.0 / (t + 1))
                step(pool.memset(band1[g], 1.0 / w))
                for m, n in ((band0[g], 144), (band1[g], P)):
                    step(pool.affine_select(out=m, in_=m, compare_op=ALU.is_ge, fill=0.0, base=0,
                                            pattern=[[1, n]], channel_multiplier=-1))
                    step(pool.affine_select(out=m, in_=m, compare_op=ALU.is_ge, fill=0.0, base=w - 1,
                                            pattern=[[-1, n]], channel_multiplier=1))
                    step(pool.tensor_tensor(m[:, 0:P], m[:, 0:P], ident, ALU.subtract))
                m = selw[:, g, :]
                step(pool.memset(m, 1.0 / w))
                step(pool.affine_select(out=m, in_=m, compare_op=ALU.is_ge, fill=0.0, base=-(BUF + 1 - w),
                                        pattern=[[-BUF, 8]], channel_multiplier=1))
                step(pool.affine_select(out=m, in_=m, compare_op=ALU.is_ge, fill=0.0, base=BUF - 1,
                                        pattern=[[BUF, 8]], channel_multiplier=-1))
            pool.memset(dm8[:, 0, 0:1], 1.0).then_inc(s_const, 1)

            pool.wait_ge(s_prepa, 5)
            pool.memset(score, 0.0).then_inc(s_sczero, 1)
            wait_drained(pool, ("score", 1, 1))
            step(pool.memset(sel8, 1.0))
            step(pool.affine_select(out=sel8, in_=sel8, compare_op=ALU.is_ge, fill=0.0, base=0,
                                    pattern=[[-1, 8], [0, P]], channel_multiplier=1))
            step(pool.affine_select(out=sel8, in_=sel8, compare_op=ALU.is_ge, fill=0.0, base=0,
                                    pattern=[[1, 8], [0, P]], channel_multiplier=-1))
            pool.tensor_tensor(qm, dm8.unsqueeze(1).to_broadcast([P, H, 8, 8]),
                               qh[:, :, SEQ:T].unsqueeze(3).to_broadcast([P, H, 8, 8]),
                               ALU.mult).then_inc(s_sel8, 1)
            for b in range(NS):
                store(new_pool_sample[0, b, 0:BUF - 1, :], state_pool[0, b, 1:BUF, :])
            pool.wait_ge(ld["hgn"], 16)
            wait_drained(pool, ("ga", 1, 1))
            for t in range(NT):
                o = og[lanes(t), t, :].rearrange("p (h v) -> p h v", h=H)
                pool.tensor_tensor(o, o, hgn[lanes(t)].unsqueeze(1).to_broadcast([TS[t], H, P]),
                                   ALU.mult).then_inc(s_ogp, 1)
            wait_drained(pool, ("o", 1, 1))
            wait_drained(pool, ("dS", NCH - 1, 1))
            pool.dma_start(pscale_b, pool_scale.partition_broadcast(P)[:, 0, :]).then_inc(ld["pscale"], 16)
            pool.dma_start(bufrows, rows_of).then_inc(ld["bufrows"], 16)
            pool.dma_start(gffn_b, g_ffn.partition_broadcast(P)[:, 0, :]).then_inc(ld["gffn"], 16)
            pool.dma_start(new_hgrn_prompt[0, 0].rearrange("h k v -> k h v"), state[NCH % 2]).then_inc(s_stst, 16)
            for b in range(NS):
                wait_drained(pool, ("vb", b, 1))
                pool.dma_start(new_hgrn_sample[0, b].rearrange("h k v -> k h v"), s0[:, b]).then_inc(s_snst, 16)
            wait_drained(pool, ("u", 0, 1))
            wait_drained(pool, ("u", 1, 1))
            pool.dma_start(new_pool_prompt[0, 0], u[P - BUF:P, 1, :]).then_inc(s_ust, 16)
            wait_drained(pool, ("u", "s", 3))
            pool.dma_start(new_pool_sample[0, :, BUF - 1, :], u[0:NS, 2, :]).then_inc(s_ust, 16)
            pool.wait_ge(s_snst, 16 * NS)
            wait_drained(pool, ("os",))
            for k in range(4):
                pool.dma_start(wout[:, 2 * k:2 * k + 2], w_out[0].rearrange("(k p) n -> p k n", p=P)[
                    :, 2 * k:2 * k + 2]).then_inc(ld["wout"], 16)
            pool.wait_ge(ld["pscale"], 16)
            wait_drained(pool, ("gb", 1, 1))
            for t in range(NT):
                pool.tensor_tensor(gb[lanes(t), t, :], gb[lanes(t), t, :], pscale_b[lanes(t)],
                                   ALU.mult).then_inc(s_gbs, 1)
            pool.wait_ge(s_rows, 6)
            pool.dma_start(bias_g, b_gate[0]).then_inc(ld["bias"], 16)
            pool.dma_start(bias_u, b_up[0]).then_inc(ld["bias"], 16)
            pool.dma_start(bias_d, b_down[0]).then_inc(ld["bdown"], 16)
            pool.wait_ge(s_stst, 16)
            pool.wait_ge(s_ust, 32)
            pool.dma_start(wproj, w_ple_proj[0].rearrange("(k p) n -> p k n", p=P)).then_inc(ld["wproj"], 16)
            wait_filled(pool, ("bd", 2, 1))
            pool.dma_start(ptok[:, 0:2, :], p_prompt[0, 0].rearrange("(t p) d -> p t d", p=P)).then_inc(ld["ptok"], 16)
            pool.dma_start(ptok[0:NS, 2, :], p_sample[0, :, 0, :]).then_inc(ld["ptok"], 16)
            pool.wait_ge(s_end, 1)
            pool.dma_start(gple_b, g_ple.partition_broadcast(P)[:, 0, :]).then_inc(ld["gple"], 16)
            pool.dma_start(gfin_b, g_final.partition_broadcast(P)).then_inc(ld["gfin"], 16)
            for t in range(2):
                pool.wait_ge(s_yout, t + 1)
                store(y_prompt[0, toks(t), :], yout[:, t, :])
            pool.wait_ge(s_yout, 3)
            store(y_sample[:, 0, :], yout[0:NS, 2, :])
            pool.wait_ge(s_out, 16 * n_out[0])

        @block.tensor
        def _(pe):
            def begin(name):
                if before[name]:
                    wait_drained(pe, before[name])

            def turn_rows(tag, src, ready, n_used=0):
                for t in range(NT):
                    pe.wait_ge(*ready(t))
                    n = TS[t]
                    for half in range(2 if t < 2 else 1):
                        name = (tag, t, half)
                        begin(name)
                        ks_ = range(4 * half, 4 * half + 4) if t < 2 else range(KD)
                        for j, k in enumerate(ks_):
                            ins = pe.transpose(job_bank(name)[:, j * n:(j + 1) * n], src[0:n, t, k * P:(k + 1) * P],
                                               ident[0:n, 0:n])
                            if n_used and k != ks_[-1]:
                                n_used -= 1
                                ins.then_inc(s_used, 1)
                        fill_done(ins, name)

            def wait_turned(tag):
                for t in range(NT):
                    for half in range(2 if t < 2 else 1):
                        wait_drained(pe, (tag, t, half))

            chunk_no = {}
            for c, (kind, _) in enumerate(W_CHUNKS):
                chunk_no[(kind, c - [k for k, _ in W_CHUNKS].index(kind))] = c

            def wait_chunk(c):
                pe.wait_ge(s_w[c % NSLOT], 16 * (c // NSLOT + 1))

            def chunk_step(kind, n, k, signal=None):
                w = w_slot[chunk_no[(kind, n)] % NSLOT]
                for t in range(2):
                    name = (kind, n, t)
                    if k == 0:
                        begin(name)
                    ins = pe.matmul(job_bank(name)[:, :], hT[:, k, toks(t)], w[:, k, :],
                                    start=(k == 0), stop=(k == KD - 1))
                    if k == KD - 1:
                        fill_done(ins, name)
                    elif t == 0 and signal:
                        ins.then_inc(signal, 1)

            def chunk(kind, n):
                wait_chunk(chunk_no[(kind, n)])
                for k in range(KD):
                    chunk_step(kind, n, k)

            def sample_rows(kind, chunks):
                name = (kind, "s", 0)
                begin(name)
                for c in chunks:
                    wait_chunk(c)
                for k in range(KD):
                    for j, c in enumerate(chunks):
                        ins = pe.matmul(job_bank(name)[32 * j:32 * j + NS, :], hT[:, k, toks(2)],
                                        w_slot[c % NSLOT][:, k, :], start=(k == 0), stop=(k == KD - 1))
                        if k == KD - 1:
                            fill_done(ins, (kind, "s", j))

            pe.wait_ge(s_const, 1)
            pe.wait_ge(ld["lbin"], 16)
            fill_done(pe.transpose(bank[7][:, 0:16], lgin[0:16, :], ident[0:16, 0:16]), ("lb",))
            turn_rows("hT", htok, lambda t: (s_rows, t + 1))
            wait_turned("hT")

            for kind in ("f", "q"):
                for h in range(H):
                    c = chunk_no[(kind, h // 4)]
                    wait_chunk(c)
                    begin((kind, h))
                    for k in range(KD):
                        ins = pe.matmul(job_bank((kind, h))[:, 0:T],
                                        w_slot[c % NSLOT][:, k, (h % 4) * P:(h % 4 + 1) * P], hT[:, k, :],
                                        start=(k == 0), stop=(k == KD - 1))
                    fill_done(ins, (kind, h))
            chunk("v", 0)
            sample_rows("v", (4, 5))
            chunk("v", 1)
            chunk("g", 0)
            chunk("g", 1)
            chunk("ga", 0)

            pe.wait_ge(s_prep, 5)
            for t in range(2):
                for half in range(2):
                    name = ("score", t, half)
                    begin(name)
                    for j in range(4):
                        h = 4 * half + j
                        ins = pe.matmul(job_bank(name)[:, j * P:(j + 1) * P], t1[:, h, toks(t)], qh[:, h, toks(t)],
                                        start=True, stop=True)
                    fill_done(ins, name)
            for t in range(2):
                for half in range(2):
                    name = ("kT", t, half)
                    begin(name)
                    for j in range(4):
                        ins = pe.transpose(job_bank(name)[:, j * P:(j + 1) * P], fh[:, 4 * half + j, toks(t)], ident)
                    fill_done(ins, name)
            sample_rows("g", (6, 7, 8, 9))
            chunk("ga", 1)

            wait_chunk(chunk_no[("u", 0)])
            for name in [("kT", t, half) for t in range(2) for half in range(2)] + [("v", n, t) for n in range(2) for t in range(2)]:
                wait_drained(pe, name)
            for n in range(NCH):
                t, row = n // 4, CH * (n % 4)
                rr = slice(row, row + CH)
                for half in range(2):
                    name = ("dS", n, half)
                    begin(name)
                    for j in range(4):
                        hh = slice((4 * half + j) * P, (4 * half + j + 1) * P)
                        ins = pe.matmul(job_bank(name)[:, j * P:(j + 1) * P], ktok[rr, t, hh], v[rr, t, hh],
                                        start=True, stop=True)
                    fill_done(ins, name)
                for half in range(2):
                    name = ("o", t, half)
                    if n % 4 == 0:
                        begin(name)
                        wait_drained(pe, ("score", t, half))
                        for j in range(4):
                            h = 4 * half + j
                            ins = pe.matmul(job_bank(name)[:, j * P:(j + 1) * P],
                                            score[:, 2 * t + half, j * P:(j + 1) * P], v[:, t, h * P:(h + 1) * P],
                                            start=(j == 0), stop=True, skip_group_check=True)
                    if n > 0:
                        wait_drained(pe, ("dS", n - 1, 1))
                        for j in range(4):
                            h = 4 * half + j
                            ins = pe.matmul(job_bank(name)[rr, j * P:(j + 1) * P], qh[:, h, n * CH:(n + 1) * CH],
                                            state[n % 2][:, h, :], start=False, stop=True,
                                            skip_group_check=True, tile_position=(0, row))
                    if n % 4 == 3:
                        fill_done(ins, name)
                chunk_step("u", 0, n, signal=s_inter)
            chunk("u", 1)
            wait_chunk(chunk_no[("gb", 0)])
            pe.wait_ge(s_sel8, 1)
            wait_drained(pe, ("v", "s", 1))
            for b in range(NS):
                for half in range(2):
                    name = ("vb", b, half)
                    begin(name)
                    fill_done(pe.matmul(job_bank(name)[:, :], sel8[:, b, :], v[0:NS, 2, halves(half)],
                                        start=True, stop=True), name)
                chunk_step("gb", 0, b)
            sample_rows("u", (10, 11, 12, 13))
            chunk("gb", 1)
            begin(("os",))
            wait_drained(pe, ("vb", NS - 1, 1))
            for hh in range(2):
                for b in range(NS):
                    for j in range(4):
                        h = 4 * hh + j
                        ins = pe.matmul(job_bank(("os",))[32 * j:32 * j + NS, hh * P:(hh + 1) * P], qm[:, h, b, :],
                                        s0[:, b, h, :], start=(b == 0), stop=(b == NS - 1))
            fill_done(ins, ("os",))

            for name in [("u", n, t) for n in range(2) for t in range(2)] + [("u", "s", 3)]:
                wait_drained(pe, name)
            pe.wait_ge(ld["bufrows"], 16)
            pe.wait_ge(s_const, 2)
            for c in range(KD):
                name, g = ("dT", c), c // 2
                begin(name)
                o, cc = job_bank(name), slice(c * P, (c + 1) * P)
                pe.matmul(o[:, 0:144], u[:, 0, cc], band0[g], start=True, stop=True, skip_group_check=True).then_inc(s_used, 1)
                pe.matmul(o[:, P:SEQ], u[:, 1, cc], band1[g], start=False, stop=True, skip_group_check=True)
                pe.matmul(o[:, SEQ:T], bufrows[:, cc], selw[0:NS * BUF, g, :], start=True, stop=False)
                ins = pe.matmul(o[:, SEQ:T], u[0:NS, 2, cc], dw8[0:NS, g, :], start=False, stop=True)
                fill_done(ins, name)
            pe.wait_ge(ld["wpool"], 16)
            for c in range(KD):
                wait_drained(pe, ("dT", c))
            for t in range(NT):
                for half in range(2):
                    name = ("yp", t, half)
                    begin(name)
                    for gg in range(2):
                        g = 2 * half + gg
                        for k in range(2):
                            ins = pe.matmul(job_bank(name)[lanes(t), gg * 256:(gg + 1) * 256],
                                            dT[:, 2 * g + k, toks(t)], wpool[:, g, k, :],
                                            start=(k == 0), stop=(k == 1))
                    fill_done(ins, name)
            turn_rows("mT", og, lambda t: (s_merged, t + 1))
            pe.wait_ge(ld["wout"], 64)
            wait_turned("mT")

            def weights(w, k, half):
                return gran[k // 2][:, k % 2, halves(half)] if w is None else w[:, k, halves(half)]

            def product(tag, t, src, w, slices=KD):
                if t < 2:
                    for half in range(2):
                        name = (tag, t, half)
                        begin(name)
                        for k in range(slices):
                            ins = pe.matmul(job_bank(name)[:, :], src[:, k, toks(t)], weights(w, k, half),
                                            start=(k == 0), stop=(k == slices - 1))
                        fill_done(ins, name)
                else:
                    begin((tag, 2, 0))
                    for k in range(slices):
                        for half in range(2):
                            ins = pe.matmul(job_bank((tag, 2, 0))[32 * half:32 * half + NS, :], src[:, k, toks(2)],
                                            weights(w, k, half), start=(k == 0), stop=(k == slices - 1))
                            if k == slices - 1:
                                fill_done(ins, (tag, 2, half))

            for t in range(NT):
                product("x1", t, mT, wout)

            turn_rows("h2T", h2, lambda t: (s_rows, t + 4), n_used=8)
            pe.wait_ge(ld["wr"], 16)
            wait_turned("h2T")
            begin(("lgT",))
            for k in range(KD):
                ins = pe.matmul(bank[6][0:NE, 0:T], wr[:, k, :], hT[:, k, :], start=(k == 0), stop=(k == KD - 1))
            fill_done(ins, ("lgT",))
            begin(("lg",))
            wait_drained(pe, ("lgT",))
            for t in range(NT):
                ins = pe.transpose(bank[7][lanes(t), t * NE:(t + 1) * NE], lgT[:, toks(t)], ident[0:NE, 0:NE])
            fill_done(ins, ("lg",))
            pe.wait_ge(s_rt, 2)
            begin(("rank",))
            for t in range(NT):
                for s in range(t):
                    pe.matmul(bank[0][:, t * NE:(t + 1) * NE], ones, msk[:, s, :], start=(s == 0), stop=False)
                n = TS[t]
                ins = pe.matmul(bank[0][:, t * NE:(t + 1) * NE], before_t[0:n, :], msk[0:n, t, :],
                                start=(t == 0), stop=True)
            fill_done(ins, ("rank",))
            begin(("count",))
            for t in range(NT):
                n = TS[t]
                ins = pe.matmul(bank[1][0:8, 0:NE], ones[0:n, 0:8], msk[0:n, t, :], start=(t == 0), stop=(t == NT - 1))
            fill_done(ins, ("count",))
            begin(("wT",))
            for t in range(NT):
                ins = pe.transpose(bank[2][0:NE, toks(t)], wdn[lanes(t), t, :], ident[lanes(t), lanes(t)])
            fill_done(ins, ("wT",))
            GATE, UP, AT, XG, Y, CT = bank[0:2], bank[2:4], bank[4:6], bank[6:8], bank[0:2], bank[4]

            def hp(one):
                return slice(CAP * one, CAP * one + CAP)

            def gather():
                for c in range(2):
                    for t in range(NT):
                        ins = pe.matmul(XG[c][:, :], oh[lanes(t), t, :], h2[lanes(t), t, halves(c)],
                                        start=(t == 0), stop=(t == NT - 1))
                return ins

            def turn_half(out, src, c):
                for j in range(4):
                    k = 4 * c + j
                    ins = pe.transpose(out[c][:, j * P:(j + 1) * P], src[:, k * P:(k + 1) * P], ident)
                return ins

            def turn_gathered():
                turn_half(XG, xg_tok, 0)
                return turn_half(XG, xg_tok, 1)

            def pair(i0, n):
                i = i0 + n

                def granules(m, g):
                    for one in range(2):
                        turn, place = divmod(2 * NGRAN * n + 8 * m + 2 * g + one, RING)
                        pe.wait_ge(s_gr[place], i0 * (16 * 2 * NGRAN // RING) + 16 * (turn + 1))
                        yield gran[place]

                def products(m, out, src, first):
                    for g in range(4):
                        if m == 2 and g % 2 == 0:
                            pe.wait_ge(s_aTs, 2 * i + g // 2 + 1)
                        w = list(granules(m, g))
                        for j in range(2):
                            k = 2 * g + j
                            for c in range(2):
                                for one in range(2):
                                    ins = pe.matmul(out[c][hp(one), :],
                                                    src[:, k * P + CAP * one:k * P + CAP * one + CAP],
                                                    w[one][:, j, halves(c)], start=(first and k == 0),
                                                    stop=(k == KD - 1))
                                    if j == 1 and c == 1 and not (g == 3 and one == 1):
                                        ins.then_inc(s_used, 1)
                    return ins

                pe.wait_ge(s_esel, i + 1)
                pe.wait_ge(s_xe, i + 1)
                for m, (out, bias, done) in enumerate(((GATE, bias_g, s_gate), (UP, bias_u, s_up))):
                    if m == 1:
                        pe.wait_ge(s_free23, i + 1)
                    for c in range(2):
                        ins = pe.matmul(out[c][:, :], esel, bias[:, halves(c)], start=True, stop=False)
                        if m == 1 and c == 0:
                            ins.then_inc(s_used, 1)
                    products(m, out, xT_e, False).then_inc(done, 1)
                pe.wait_ge(s_ohw, i + 1)
                pe.wait_ge(s_free45, i + 1)
                for t in range(NT):
                    ins = pe.transpose(CT[:, toks(t)], ohw[lanes(t), t, :], ident[lanes(t), lanes(t)])
                    if t == 0:
                        ins.then_inc(s_used, 1)
                ins.then_inc(s_cT, 1)
                pe.wait_ge(s_oh, i + 2)
                pe.wait_ge(s_free6, i + 1)
                gather().then_inc(s_xg, 1)
                pe.wait_ge(s_actr, i + 1)
                pe.wait_ge(s_c, i + 1)
                for c in range(2):
                    turn_half(AT, act_sb, c).then_inc(s_aT, 1)
                pe.wait_ge(s_xgs, i + 2)
                turn_gathered().then_inc(s_xgt, 1)
                products(2, Y, actT, True).then_inc(s_y, 1)
                pe.wait_ge(s_ys, 2 * i + 2)
                for t, banks in ((0, UP), (1, AT)):
                    for c in range(2):
                        ins = pe.matmul(banks[c][:, :], comb[:, toks(t)], y_sb[:, halves(c)], start=True, stop=True)
                        if t == 0 and c == 0:
                            ins.then_inc(s_used, 1)
                    ins.then_inc(s_mix, 1)
                pe.wait_ge(s_xe, i + 2)
                for c in range(2):
                    ins = pe.matmul(bank[6][32 * c:32 * c + NS, :], comb[:, toks(2)], y_sb[:, halves(c)],
                                    start=True, stop=True)
                ins.then_inc(s_mix, 1)

            pe.wait_ge(s_oh, 1)
            for name in (("rank",), ("count",), ("wT",), ("lg",)):
                wait_drained(pe, name)
            gather().then_inc(s_xg, 1)
            pe.wait_ge(s_xgs, 1)
            turn_gathered().then_inc(s_xgt, 1)
            pe.wait_ge(ld["bias"], 32)
            with pe.Fori(0, PAIRS // 2 // PER) as q:
                for n in range(PER):
                    pair(PER * q, n)
            for done in (s_free23, s_free45, s_free6):
                pe.wait_ge(done, PAIRS // 2 + 1)
            pe.wait_ge(ld["bdown"], 16)
            wait_drained(pe, ("wT",))
            for t in range(2):
                for half in range(2):
                    name = ("bd", t, half)
                    begin(name)
                    fill_done(pe.matmul(job_bank(name)[:, :], wT[:, toks(t)], bias_d[:, halves(half)],
                                        start=True, stop=True), name)
            begin(("bd", 2, 0))
            for half in range(2):
                fill_done(pe.matmul(bank[4][32 * half:32 * half + NS, :], wT[:, toks(2)], bias_d[:, halves(half)],
                                    start=True, stop=True), ("bd", 2, half))

            for t in range(NT):
                for half in range(2):
                    wait_drained(pe, ("bd", t, half))
            with pe.Fori(PAIRS // 2 // PER, PAIRS // PER) as q:
                for n in range(PER):
                    pair(PER * q, n)
            more = pe.value_load(flag)
            with pe.If(more > 0):
                with pe.Fori(1, NBLK) as b:
                    with pe.Fori(0, PAIRS // PER) as q:
                        for n in range(PER):
                            pair(b * PAIRS + PER * q, n)
                pe.wait_ge(ld["ple"], 128)

            pe.wait_ge(s_end, 1)
            pe.wait_ge(ld["ptok"], 32)
            pe.wait_ge(ld["wproj"], 16)
            for k in range(2):
                begin(("pT", k))
                for t in range(NT):
                    ins = pe.transpose(job_bank(("pT", k))[:, toks(t)], ptok[lanes(t), t, k * P:(k + 1) * P],
                                       ident[lanes(t), lanes(t)])
                fill_done(ins, ("pT", k))
            wait_drained(pe, ("pT", 1))
            for t in range(NT):
                product("pp", t, pT, wproj, 2)
            turn_rows("h3T", h3, lambda t: (s_rows, t + 7))
            pe.wait_ge(ld["ple"], 64)
            wait_turned("h3T")
            for t in range(NT):
                product("pg", t, hT, None)

        @block.scalar
        def _(act):
            def copy_out(name, dst, src):
                wait_filled(act, name)
                drain_done(act.activation(dst, src, ACT.Copy), name)

            def turned(tag, dst):
                for t in range(NT):
                    for half in range(2 if t < 2 else 1):
                        name = (tag, t, half)
                        if drainer[name] == "a":
                            turned_bank(name, dst, copy_out)

            chain = [0]

            def rms(s, n, done):
                act.wait_ge(s_act, chain[0])
                act.activation(s, s, ACT.Sqrt, bias=eps[0:s.shape[0]], scale=1.0 / n).then_inc(done, 1)

            def sum_squares(src, dst, s):
                chain[0] += 1
                act.activation(dst, src, ACT.Square, accum_out=s).then_inc(s_act, 1)

            def squares(scratch, count):
                for t in range(NT):
                    for tag in after_x[count]:
                        wait_drained(act, (tag, t, 1))
                    s = stat[lanes(t), 4 * count + t:4 * count + t + 1]
                    sum_squares(x[lanes(t), t, :], scratch[lanes(t)], s)
                    rms(s, D, s_sumsq)

            act.dma_start(gmix_b, g_mix.partition_broadcast(P)[:, 0, :]).then_inc(ld["gmix"], 16)
            act.dma_start(lgin[0:16, :], hg_lb_logits.rearrange("d (h k) -> (d h) k", k=P)).then_inc(ld["lbin"], 16)
            act.dma_start(hgn, hg_norm.partition_broadcast(P)[:, 0, :]).then_inc(ld["hgn"], 16)
            act.dma_start(brt, b_router.rearrange("o e -> e o")).then_inc(ld["br"], 16)
            act.dma_start(wr, w_router[0].rearrange("(k p) e -> p k e", p=P)).then_inc(ld["wr"], 16)
            act.dma_start(wpool, w_pool[0].rearrange("g (k p) n -> p g k n", p=P)).then_inc(ld["wpool"], 16)
            act.wait_ge(s_x, 48)
            act.wait_ge(s_const, 1)
            squares(view(TMP, D), 0)
            turned("hT", hT)
            act.wait_ge(s_lb, 1)
            act.activation(lbt[:, 0:16], lbt[:, 0:16], ACT.Exp).then_inc(s_lbe, 1)
            for h in range(H):
                wait_filled(act, ("f", h))
                drain_done(act.activation(fh[:, h, :], job_bank(("f", h))[:, 0:T], ACT.Sigmoid), ("f", h))
            act.wait_ge(s_fdone, 1)
            act.activation(fh[:, :, 0:SEQ], fh[:, :, 0:SEQ], ACT.Ln).then_inc(s_prepa, 1)
            act.wait_ge(s_prep, 1)
            act.activation(t1[:, :, 0:SEQ], t2[:, :, 0:SEQ], ACT.Exp).then_inc(s_prepa, 1)
            act.wait_ge(s_prep, 2)
            act.activation(fh[:, :, 0:SEQ], fh[:, :, 0:SEQ], ACT.Exp).then_inc(s_prepa, 1)
            act.activation(ebl, t2[:, :, CH - 1:SEQ:CH], ACT.Exp).then_inc(s_prepa, 1)
            for h in range(H):
                wait_filled(act, ("q", h))
                act.activation(qh[:, h, :], job_bank(("q", h))[:, 0:T], ACT.Sigmoid).then_inc(s_sig, 1)
            act.wait_ge(s_prep, 4)
            act.activation(t1[:, :, 0:SEQ], t2[:, :, 0:SEQ], ACT.Exp, scale=-1.0).then_inc(s_prepa, 1)

            n_tmp = [0]

            def to_tmp(name, rows, src, func):
                m = n_tmp[0]
                n_tmp[0] += 1
                wait_filled(act, name)
                if m >= 2:
                    wait_drained(act, tmp_jobs[m - 2])
                act.activation(tmp[m % 2][rows], src, func).then_inc(s_tfull, 1)

            def gate_chunk(kind, n):
                for t in range(2):
                    to_tmp((kind, n, t), slice(0, P), job_bank((kind, n, t))[:, :], ACT.Sigmoid)

            copy_out(("v", 0, 0), v[:, 0, halves(0)], job_bank(("v", 0, 0))[:, :])
            copy_out(("v", 1, 0), v[:, 0, halves(1)], job_bank(("v", 1, 0))[:, :])
            gate_chunk("g", 0)
            gate_chunk("g", 1)
            gate_chunk("ga", 0)
            act.wait_ge(s_prep, 5)
            for t in range(2):
                for half in range(2):
                    name = ("kT", t, half)
                    copy_out(name, ktok[:, t, halves(half)], job_bank(name)[:, :])
            for j in range(4):
                to_tmp(("g", "s", j), slice(0, NS), bank[4][32 * j:32 * j + NS, :], ACT.Sigmoid)
            gate_chunk("ga", 1)

            def decay(b):
                for h in range(H):
                    ins = act.activation(s0[:, b, h, :], s0[:, b, h, :], ACT.Copy, scale=fs[:, h, b:b + 1])
                ins.then_inc(s_decay, 1)

            act.wait_ge(ld["s0"], 16 * NS)
            for t in range(2):
                for b in range(4 * t, 4 * t + 4):
                    decay(b)
                for half in range(2):
                    name, m = ("o", t, half), n_tmp[0]
                    n_tmp[0] += 1
                    wait_filled(act, name)
                    wait_drained(act, tmp_jobs[m - 2])
                    for j in range(4):
                        hh = slice(j * P, (j + 1) * P)
                        sum_squares(job_bank(name)[:, hh], tmp[m % 2][:, hh],
                                    stat[:, 16 + 4 * (m % 2) + j:17 + 4 * (m % 2) + j])
                    rms(stat[:, 16 + 4 * (m % 2):20 + 4 * (m % 2)], P, s_tfull)
            act.wait_ge(s_sel8, 1)
            copy_out(("u", 0, 0), u[:, 0, halves(0)], job_bank(("u", 0, 0))[:, :])
            copy_out(("u", 1, 0), u[:, 0, halves(1)], job_bank(("u", 1, 0))[:, :])
            act.wait_ge(s_stst, 16)

            def pool_gate(n):
                for t in range(2):
                    name = ("gb", n, t)
                    wait_filled(act, name)
                    drain_done(act.activation(gb[:, t, halves(n)], job_bank(name)[:, :], ACT.Sigmoid), name)

            pool_gate(0)
            for j in range(4):
                name = ("u", "s", j)
                wait_filled(act, name)
                dst = (u if j < 2 else gb)[0:NS, 2, halves(j % 2)]
                drain_done(act.activation(dst, bank[4][32 * j:32 * j + NS, :], ACT.Copy if j < 2 else ACT.Sigmoid), name)
            pool_gate(1)
            for c in range(0, KD, 2):
                copy_out(("dT", c), dT[:, c, :], job_bank(("dT", c))[:, 0:T])
            wait_drained(act, ("os",))
            wait_drained(act, ("o", 1, 1))
            for h in range(H):
                sum_squares(v[0:NS, 2, h * P:(h + 1) * P], view(TMP + h * P, P, NS), stat[0:NS, 16 + h:17 + h])
            rms(stat[0:NS, 16:24], P, s_osq)
            turned("mT", mT)
            squares(view(TMP, D), 1)
            turned("h2T", hT)
            act.wait_ge(s_rt, 1)
            act.activation(exw, exw, ACT.Exp).then_inc(s_rta, 1)

            def rows_in(i):
                act.wait_ge(s_xg, i + 1)
                for c in range(2):
                    ins = act.activation(xg_tok[:, halves(c)], bank[6 + c][:, :], ACT.Copy)
                ins.then_inc(s_xgs, 1)
                act.wait_ge(s_xgt, i + 1)
                for c in range(2):
                    ins = act.activation(xT_e[:, halves(c)], bank[6 + c][:, :], ACT.Copy)
                ins.then_inc(s_xe, 1)

            rows_in(0)

            def pair(i):
                act.wait_ge(s_gclip, i + 1)
                act.activation(sig_sb, g_sb, ACT.Sigmoid, scale=ALPHA).then_inc(s_gsig, 1)
                act.wait_ge(s_cT, i + 1)
                act.activation(comb, bank[4][:, 0:T], ACT.Copy).then_inc(s_c, 1)
                act.wait_ge(s_dloop, i + 1)
                rows_in(i + 1)
                act.wait_ge(s_y, i + 1)
                act.activation(y_sb[:, halves(0)], bank[0][:, :], ACT.Copy).then_inc(s_ys, 1)

            with act.Fori(0, PAIRS) as i:
                pair(i)
            act.wait_ge(s_tab, 1)
            more = act.value_load(flag)
            with act.If(more > 0):
                with act.Fori(1, NBLK) as b:
                    with act.Fori(0, PAIRS) as e:
                        pair(b * PAIRS + e)

            act.wait_ge(s_end, 1)
            for k in range(2):
                name = ("pT", k)
                copy_out(name, pT[:, k, :], job_bank(name)[:, 0:T])
            squares(sq, 2)

            def rows_out(tag, dst, func):
                for t in range(NT):
                    for half in range(2):
                        name = (tag, t, half)
                        src = job_bank(name)
                        src = src[:, :] if t < 2 else src[32 * half:32 * half + NS, :]
                        wait_filled(act, name)
                        drain_done(act.activation(dst[lanes(t), t, halves(half)], src, func), name)

            rows_out("pp", pps, ACT.Copy)
            turned("h3T", hT)
            rows_out("pg", pgs, ACT.Sigmoid)
            for t in range(NT):
                act.wait_ge(s_xfin, t + 1)
                s = stat[lanes(t), 12 + t:13 + t]
                sum_squares(x[lanes(t), t, :], sq[lanes(t)], s)
                rms(s, D, s_sumsq)

        @block.vector
        def _(dve):
            chain = [0]

            def step(ins):
                chain[0] += 1
                ins.then_inc(s_dve, 1)
                dve.wait_ge(s_dve, chain[0])

            def copy_out(name, dst, src):
                wait_filled(dve, name)
                drain_done(dve.tensor_copy(dst, src), name)

            def turned(tag, dst):
                for t in range(NT):
                    for half in range(2 if t < 2 else 1):
                        name = (tag, t, half)
                        if drainer[name] == "v":
                            turned_bank(name, dst, copy_out)

            def normalise(count, gain, dst):
                for t in range(NT):
                    dve.wait_ge(s_sumsq, 3 * count + t + 1)
                    s = stat[lanes(t), 4 * count + t:4 * count + t + 1]
                    step(dve.reciprocal(s, s))
                    dve.scalar_tensor_tensor(dst[lanes(t), t, :], x[lanes(t), t, :], s, gain[lanes(t)],
                                             ALU.mult, ALU.mult).then_inc(s_rows, 1)

            dve.wait_ge(s_const, 1)
            for g, w in enumerate(WINDOWS):
                dve.tensor_scalar(dw8[:, g, :], ident[0:NS, 0:NS], 1.0 / w - 1.0, None, ALU.mult)
            dve.wait_ge(ld["gmix"], 16)
            normalise(0, gmix_b, htok)
            l0, l1, m = lbt[:, 0:8], lbt[:, 8:16], lbt[:, 16:24]
            wait_filled(dve, ("lb",))
            drain_done(dve.tensor_copy(lbt[:, 0:16], bank[7][:, 0:16]), ("lb",))
            wait_drained(dve, ("lb",))
            step(dve.tensor_tensor(m, l0, l1, ALU.max))
            dve.tensor_tensor(l0, l0, m, ALU.subtract)
            dve.tensor_tensor(l1, l1, m, ALU.subtract).then_inc(s_lb, 1)
            turned("hT", hT)
            dve.wait_ge(s_lbe, 1)
            step(dve.tensor_tensor(m, l0, l1, ALU.add))
            step(dve.reciprocal(m, m))
            step(dve.tensor_tensor(lb, l0, m, ALU.mult))
            step(dve.tensor_scalar(omlb, lb, -1.0, 1.0, ALU.mult, ALU.add))
            tmask = view(TMP, SEQ)
            step(dve.memset(tmask, 1.0))
            dve.memset(tmask[:, 0:SEQ:CH], 0.0)

            for h in range(H):
                wait_drained(dve, ("f", h))
                ins = dve.tensor_scalar(fh[:, h, :], fh[:, h, :], omlb[:, h:h + 1], lb[:, h:h + 1], ALU.mult, ALU.add)
            step(ins)
            step(dve.tensor_scalar(kh, fh, -1.0, 1.0, ALU.mult, ALU.add))
            dve.tensor_copy(ks, kh[:, :, SEQ:T])
            dve.tensor_copy(fs, fh[:, :, SEQ:T]).then_inc(s_fdone, 1)
            dve.wait_ge(s_prepa, 1)
            for h in range(H):
                ins = dve.tensor_tensor_scan(t2[:, h, 0:SEQ], tmask, fh[:, h, 0:SEQ], 0.0, ALU.mult, ALU.add)
            ins.then_inc(s_prep, 1)
            dve.wait_ge(s_prep, 1)
            b4 = [a[:, :, 0:SEQ].rearrange("p h (n c) -> p h n c", c=CH) for a in (fh, t2)]
            for h in range(H):
                ins = dve.tensor_tensor(b4[0][:, h], b4[1][:, h, :, CH - 1:CH].to_broadcast([P, NCH, CH]), b4[1][:, h],
                                        ALU.subtract)
            ins.then_inc(s_prep, 1)
            dve.wait_ge(s_prepa, 3)
            dve.tensor_tensor(fh[:, :, 0:SEQ], fh[:, :, 0:SEQ], kh[:, :, 0:SEQ], ALU.mult).then_inc(s_prep, 1)
            for h in range(H):
                dve.wait_ge(s_sig, h + 1)
                drain_done(dve.tensor_tensor(qh[:, h, :], job_bank(("q", h))[:, 0:T], qh[:, h, :], ALU.mult), ("q", h))
            wait_drained(dve, ("q", H - 1))
            dve.tensor_tensor(qh[:, :, 0:SEQ], qh[:, :, 0:SEQ], t1[:, :, 0:SEQ], ALU.mult).then_inc(s_prep, 1)
            dve.wait_ge(s_prepa, 5)
            dve.tensor_tensor(t1[:, :, 0:SEQ], t1[:, :, 0:SEQ], kh[:, :, 0:SEQ], ALU.mult).then_inc(s_prep, 1)

            n_tmp = [0]

            def tmp_full():
                n_tmp[0] += 1
                dve.wait_ge(s_tfull, n_tmp[0])
                return tmp[(n_tmp[0] - 1) % 2]

            def gate_chunk(kind, n):
                for t in range(2):
                    name = (kind, n, t)
                    o = og[:, t, halves(n)]
                    w = tmp_full()
                    src = job_bank(name)[:, :] if kind == "g" else o
                    drain_done(dve.tensor_tensor(o, src, w, ALU.mult), name)

            copy_out(("v", 0, 1), v[:, 1, halves(0)], job_bank(("v", 0, 1))[:, :])
            for j in range(2):
                copy_out(("v", "s", j), v[0:NS, 2, halves(j)], bank[4][32 * j:32 * j + NS, :])
            copy_out(("v", 1, 1), v[:, 1, halves(1)], job_bank(("v", 1, 1))[:, :])
            gate_chunk("g", 0)
            gate_chunk("g", 1)
            wait_drained(dve, ("g", 1, 1))
            gate_chunk("ga", 0)
            dve.wait_ge(s_sczero, 1)
            dve.wait_ge(s_const, 2)
            for t in range(2):
                for half in range(2):
                    name = ("score", t, half)
                    wait_filled(dve, name)
                    drain_done(dve.copy_predicated(score[:, 2 * t + half, :].rearrange("p (h c) -> p h c", h=4),
                                                   cmask.unsqueeze(1).to_broadcast([P, 4, P]),
                                                   job_bank(name)[:, :].rearrange("p (h c) -> p h c", h=4)), name)
            for j in range(4):
                w = tmp_full()
                o = og[0:NS, 2, halves(j % 2)]
                if j == 2:
                    wait_drained(dve, ("g", "s", 1))
                src = bank[4][32 * j:32 * j + NS, :] if j < 2 else o
                drain_done(dve.tensor_tensor(o, src, w[0:NS], ALU.mult), ("g", "s", j))
            gate_chunk("ga", 1)

            def head_norm(name, rows, t, half):
                tmp_full()
                s = stat[:, 16 + 4 * ((n_tmp[0] - 1) % 2):20 + 4 * ((n_tmp[0] - 1) % 2)]
                step(dve.reciprocal(s, s))
                for j in range(4):
                    hh = slice((4 * half + j) * P, (4 * half + j + 1) * P)
                    ins = dve.scalar_tensor_tensor(og[rows, t, hh], job_bank(name)[rows, j * P:(j + 1) * P],
                                                   s[:, j:j + 1], og[rows, t, hh], ALU.mult, ALU.mult)
                drain_done(ins, name)

            for n in range(NCH):
                if n >= 1:
                    wait_drained(dve, ("dS", n - 1, 1))
                if n >= 2:
                    dve.wait_ge(s_inter, n)
                for half in range(2):
                    name = ("dS", n, half)
                    if n == 0:
                        copy_out(name, state[1][:, 4 * half:4 * half + 4, :],
                                 job_bank(name)[:, :].rearrange("p (h v) -> p h v", h=4))
                        continue
                    wait_filled(dve, name)
                    for j in range(4):
                        h = 4 * half + j
                        ins = dve.scalar_tensor_tensor(state[(n + 1) % 2][:, h, :], state[n % 2][:, h, :],
                                                       ebl[:, h, n:n + 1], job_bank(name)[:, j * P:(j + 1) * P],
                                                       ALU.mult, ALU.add)
                    drain_done(ins, name)
                if n % 4 == 3:
                    t = n // 4
                    dve.wait_ge(s_ogp, t + 1)
                    for half in range(2):
                        head_norm(("o", t, half), slice(0, P), t, half)
            dve.wait_ge(s_sel8, 1)
            copy_out(("u", 0, 1), u[:, 1, halves(0)], job_bank(("u", 0, 1))[:, :])
            copy_out(("u", 1, 1), u[:, 1, halves(1)], job_bank(("u", 1, 1))[:, :])
            for b in range(NS):
                dve.wait_ge(s_decay, b + 1)
                for half in range(2):
                    name = ("vb", b, half)
                    wait_filled(dve, name)
                    for j in range(4):
                        h = 4 * half + j
                        ins = dve.scalar_tensor_tensor(s0[:, b, h, :], job_bank(name)[:, j * P:(j + 1) * P],
                                                       ks[:, h, b:b + 1], s0[:, b, h, :], ALU.mult, ALU.add)
                    drain_done(ins, name)
            name = ("os",)
            wait_filled(dve, name)
            osb = v[0:NS, 2, :].rearrange("p (a j v) -> p j a v", a=2, j=4)
            for j in range(4):
                ins = dve.tensor_copy(osb[:, j], bank[7][32 * j:32 * j + NS, 0:2 * P].rearrange("p (a v) -> p a v", a=2))
            drain_done(ins, name)
            wait_drained(dve, name)

            def sample_norm():
                flat, s = v[0:NS, 2, :], stat[0:NS, 16:24]
                by_head = flat.rearrange("p (h v) -> p h v", h=H)
                dve.wait_ge(s_osq, 1)
                step(dve.reciprocal(s, s))
                step(dve.tensor_tensor(by_head, by_head, s.unsqueeze(2).to_broadcast([NS, H, P]), ALU.mult))
                dve.wait_ge(s_ogp, NT)
                dve.tensor_tensor(og[0:NS, 2, :], og[0:NS, 2, :], flat, ALU.mult)

            for c in range(1, KD, 2):
                copy_out(("dT", c), dT[:, c, :], job_bank(("dT", c))[:, 0:T])
            dve.wait_ge(s_gbs, NT)
            for t in range(NT):
                if t == 2:
                    sample_norm()
                for half in range(2):
                    name = ("yp", t, half)
                    wait_filled(dve, name)
                    o = gb[lanes(t), t, halves(half)]
                    drain_done(dve.tensor_tensor(o, job_bank(name)[lanes(t), :], o, ALU.mult), name)
                wait_drained(dve, name)
                dve.tensor_tensor(og[lanes(t), t, :], og[lanes(t), t, :], gb[lanes(t), t, :], ALU.add)\
                   .then_inc(s_merged, 1)
            turned("mT", mT)

            def add_to_x(tag, t, half):
                name = (tag, t, half)
                wait_filled(dve, name)
                xs = x[lanes(t), t, halves(half)]
                src = job_bank(name)[:, :] if t < 2 else job_bank(name)[32 * half:32 * half + NS, :]
                drain_done(dve.tensor_tensor(xs, src, xs, ALU.add), name)

            for t in range(NT):
                for half in range(2):
                    add_to_x("x1", t, half)
            dve.wait_ge(ld["gffn"], 16)
            normalise(1, gffn_b, h2)
            turned("h2T", hT)

            dve.wait_ge(ld["br"], 16)
            wait_filled(dve, ("lgT",))
            drain_done(dve.tensor_scalar(lgT, bank[6][0:NE, 0:T], brt, None, ALU.add), ("lgT",))
            step(dve.memset(lg, 0.0))
            wait_filled(dve, ("lg",))
            dve.tensor_copy(lg[:, 0:2, :], bank[7][:, 0:2 * NE].rearrange("p (t e) -> p t e", t=2))
            drain_done(dve.tensor_copy(lg[0:NS, 2, :], bank[7][0:NS, 2 * NE:3 * NE]), ("lg",))
            wait_drained(dve, ("lg",))
            for t in range(NT):
                ins = dve.max(top[:, t, :], lg[:, t, :])
            step(ins)
            for t in range(NT):
                ins = dve.max_index(topi[:, t, :], top[:, t, :], lg[:, t, :])
            step(ins)
            dve.tensor_copy(topf, topi)
            dve.tensor_tensor(exw, top[:, :, 0:TOPK], top[:, :, 0:1].to_broadcast([P, NT, TOPK]), ALU.subtract)\
               .then_inc(s_rt, 1)
            dve.wait_ge(s_rta, 1)
            step(dve.tensor_reduce(ssum, exw, AX_X, ALU.add))
            step(dve.reciprocal(rsum, ssum))
            step(dve.tensor_tensor(exw, exw, rsum.to_broadcast([P, NT, TOPK]), ALU.mult))
            experts = iota[:, 0:NE].unsqueeze(1).to_broadcast([P, NT, NE])
            for k in range(TOPK):
                hit, dst_m, dst_w = (msk, msk, wdn) if k == 0 else (isk, tmpr, tmpw)
                step(dve.tensor_tensor(hit, experts, topf[:, :, k:k + 1].to_broadcast([P, NT, NE]), ALU.is_equal))
                if k == 0:
                    ins = dve.tensor_tensor(wdn, hit, exw[:, :, 0:1].to_broadcast([P, NT, NE]), ALU.mult)
                    step(ins)
                    continue
                step(dve.tensor_tensor(tmpw, hit, exw[:, :, k:k + 1].to_broadcast([P, NT, NE]), ALU.mult))
                step(dve.tensor_tensor(msk, msk, hit, ALU.add))
                ins = dve.tensor_tensor(wdn, wdn, tmpw, ALU.add)
                if k < TOPK - 1:
                    step(ins)
            ins.then_inc(s_rt, 1)
            dve.wait_ge(s_rt, 2)
            wait_filled(dve, ("rank",))
            for b in range(NBLK):
                cols = slice(b * NE, (b + 1) * NE)
                ins = dve.scalar_tensor_tensor(slot_tab[:, :, cols],
                                               bank[0][:, 0:NT * NE].rearrange("p (t e) -> p t e", t=NT),
                                               FAR - CAP * b, msk, ALU.add, ALU.mult)
                dve.tensor_copy(wt_tab[:, :, cols], wdn)
                dve.tensor_copy(eis[:, cols], ident[0:NE, 0:NE])
            step(dve.memset(slot_tab[:, :, NBLK * NE:NTAB], 0.0))
            drain_done(dve.tensor_scalar(slot_tab, slot_tab, -FAR, None, ALU.add), ("rank",))
            wait_filled(dve, ("count",))
            drain_done(dve.tensor_reduce(stat[0:8, 16:17], bank[1][0:8, 0:NE], AX_X, ALU.max), ("count",))
            wait_drained(dve, ("count",))
            dve.tensor_scalar(flag, stat[0:1, 16:17], CAP + 0.5, None, ALU.is_gt).then_inc(s_tab, 1)
            copy_out(("wT",), wT, bank[2][0:NE, 0:T])
            dve.memset(wt_tab[:, :, NBLK * NE:NTAB], 0.0).then_inc(s_free23, 1)
            dve.memset(eis[:, NBLK * NE:NTAB], 0.0).then_inc(s_free6, 1)
            step(dve.memset(stat[:, 20:21], 0.0))
            dve.memset(stat[:, 21:22], 0.0).then_inc(s_free45, 1)

            def by_expert(rows):
                return rows.rearrange("p t (e c) -> p t e c", e=2)

            slots = iota[:, 0:CAP].unsqueeze(1).unsqueeze(1).to_broadcast([P, NT, 2, CAP])

            def select_tokens(i):
                mine = slot_tab[:, :, bass.ds(2 * i, 2)].unsqueeze(3).to_broadcast([P, NT, 2, CAP])
                dve.tensor_tensor(by_expert(oh), slots, mine, ALU.is_equal).then_inc(s_oh, 1)

            def weigh_tokens(i):
                weight = wt_tab[:, :, bass.ds(2 * i, 2)].unsqueeze(3).to_broadcast([P, NT, 2, CAP])
                dve.wait_ge(s_oh, i + 1)
                dve.tensor_tensor(by_expert(ohw), by_expert(oh), weight, ALU.mult).then_inc(s_ohw, 1)

            def select_experts(i):
                mine = eis[:, bass.ds(2 * i, 2)].unsqueeze(2).to_broadcast([NE, 2, CAP])
                dve.tensor_copy(esel.rearrange("p (e c) -> p e c", e=2), mine).then_inc(s_esel, 1)

            select_tokens(0)
            select_experts(0)

            def pair(i):
                dve.wait_ge(s_xg, i + 1)
                weigh_tokens(i)
                dve.wait_ge(s_ohw, i + 1)
                select_tokens(i + 1)
                dve.wait_ge(s_gate, i + 1)
                for c in range(2):
                    ins = dve.tensor_scalar(g_sb[:, halves(c)], bank[c][:, :], LIMIT, None, ALU.min)
                ins.then_inc(s_gclip, 1)
                dve.wait_ge(s_gsig, i + 1)
                dve.tensor_tensor(g_sb, g_sb, sig_sb, ALU.mult).then_inc(s_dloop, 1)
                dve.wait_ge(s_up, i + 1)
                for c in range(2):
                    ins = dve.tensor_scalar(u_sb[:, halves(c)], bank[2 + c][:, :], LIMIT, -LIMIT, ALU.min, ALU.max)
                ins.then_inc(s_uclip, 1)
                select_experts(i + 1)
                dve.wait_ge(s_dloop, i + 1)
                dve.wait_ge(s_uclip, i + 1)
                dve.scalar_tensor_tensor(act_sb, u_sb, 1.0, g_sb, ALU.add, ALU.mult).then_inc(s_actr, 1)
                for c in range(2):
                    dve.wait_ge(s_aT, 2 * i + c + 1)
                    dve.tensor_copy(actT[:, halves(c)], bank[4 + c][:, :]).then_inc(s_aTs, 1)
                dve.wait_ge(s_y, i + 1)
                dve.tensor_copy(y_sb[:, halves(1)], bank[1][:, :]).then_inc(s_ys, 1)
                for t, done in ((0, s_free23), (1, s_free45), (2, s_free6)):
                    dve.wait_ge(s_mix, 3 * i + t + 1)
                    for c in range(2):
                        xs = x[lanes(t), t, halves(c)]
                        src = bank[2 + 2 * t + c][:, :] if t < 2 else bank[6][32 * c:32 * c + NS, :]
                        ins = dve.tensor_tensor(xs, src, xs, ALU.add)
                    ins.then_inc(done, 1)
                dve.wait_ge(s_free6, i + 2)

            with dve.Fori(0, PAIRS // 2) as i:
                pair(i)
            for t in range(NT):
                for half in range(2):
                    add_to_x("bd", t, half)
            wait_drained(dve, ("bd", 2, 1))
            with dve.Fori(PAIRS // 2, PAIRS) as i:
                pair(i)
            more = dve.value_load(flag)
            with dve.If(more > 0):
                with dve.Fori(1, NBLK) as b:
                    with dve.Fori(0, PAIRS) as e:
                        pair(b * PAIRS + e)

            dve.memset(stat[:, 22:23], 0.0).then_inc(s_end, 1)
            dve.wait_ge(ld["gple"], 16)
            normalise(2, gple_b, h3)
            turned("h3T", hT)
            dve.wait_ge(ld["gfin"], 16)
            for t in range(NT):
                for half in range(2):
                    wait_drained(dve, ("pg", t, half))
                    o = pgs[lanes(t), t, halves(half)]
                    step(dve.tensor_tensor(o, pps[lanes(t), t, halves(half)], o, ALU.mult))
                xs = x[lanes(t), t, :]
                dve.tensor_tensor(xs, xs, pgs[lanes(t), t, :], ALU.add).then_inc(s_xfin, 1)
            for t in range(NT):
                dve.wait_ge(s_sumsq, 9 + t + 1)
                s = stat[lanes(t), 12 + t:13 + t]
                step(dve.reciprocal(s, s))
                dve.scalar_tensor_tensor(yout[lanes(t), t, :], x[lanes(t), t, :], s, gfin_b[lanes(t)],
                                         ALU.mult, ALU.mult).then_inc(s_yout, 1)


_INS = ["x_prompt", "x_sample", "p_prompt", "p_sample", "state_hgrn", "state_pool", "g_mix", "w_in",
        "hg_lb_logits", "hg_norm", "w_pool", "pool_scale", "w_out", "g_ffn", "w_router", "b_router", "w_gate",
        "b_gate", "w_up", "b_up", "w_down", "b_down", "g_ple", "w_ple_gate", "w_ple_proj", "g_final"]
_OUTS = [(1, SEQ, D), (NS, 1, D), (1, 1, H, P, P), (1, 1, BUF, D), (1, NS, H, P, P), (1, NS, BUF, D)]


def kernel(**inputs):
    import concourse.bacc as _bacc
    from concourse.bass_utils import run_bass_kernel_spmd as _run

    nc = _bacc.Bacc("TRN2", target_bir_lowering=False, num_devices=1)
    arrays, args = {}, []
    for name in _INS:
        a = np.ascontiguousarray(inputs[name])
        arrays[f"in_{name}_dram"] = a
        args.append(nc.dram_tensor(f"in_{name}_dram", a.shape, mybir.dt.from_np(a.dtype), kind="ExternalInput").ap())
    for i, shape in enumerate(_OUTS):
        args.append(nc.dram_tensor(f"out_{i}_dram", shape, F32, kind="ExternalOutput").ap())
    build(nc, *args)
    r = _run(nc, [arrays], core_ids=[0])
    return tuple(r.results[0][f"out_{i}_dram"] for i in range(len(_OUTS)))
```

```python
from contextlib import ExitStack

import numpy as np

import concourse.bass as bass
from concourse import mybir

F32 = mybir.dt.float32
I32 = mybir.dt.int32
U32 = mybir.dt.uint32
ALU = mybir.AluOpType
ACT = mybir.ActivationFunctionType
AX_X = mybir.AxisListType.X

P = 128
D = 1024
SEQ = 256
NS = 8
T = SEQ + NS
TS = (P, P, NS)
NT = len(TS)
KD = D // P
H = 8
CH = 32
NCH = SEQ // CH
WINDOWS = (2, 4, 8, 16)
BUF = 15
NE = 32
TOPK = 4
CAP = 64
NBLK = -(-T // CAP)
NTAB = NBLK * NE + 2
LIMIT = 7.0
ALPHA = 1.702
EPS = 1e-6
FAR = 4096.0
HALF = 512
PLE = 256
GRAN = 2048
NGRAN = 3 * D * D // (P * GRAN)
RING = 16
PAIRS = NE // 2
PER = 2
assert PER * 2 * NGRAN % RING == 0 and PAIRS % (2 * PER) == 0

W_CHUNKS = [("f", 1024), ("f", 1536), ("q", 0), ("q", 512), ("v", 2048), ("v", 2560),
            ("g", 3072), ("g", 3584), ("ga", 5120), ("ga", 5632),
            ("u", 4096), ("u", 4608), ("gb", 6144), ("gb", 6656)]
NSLOT = 4


def bank_jobs():
    jobs = []

    def norm(tag, tiles=range(NT), drains="av"):
        for t in tiles:
            for half in range(2 if t < 2 else 1):
                n = 2 * t + half
                jobs.append(((tag, t, half), n, drains[n % 2]))

    def chunk(kind, n, pair, drains):
        for t in range(2):
            jobs.append(((kind, n, t), 2 * pair + t, drains[t]))

    jobs.append((("lb",), 7, "v"))
    norm("hT")
    for kind, drain in (("f", "a"), ("q", "v")):
        for h in range(H):
            jobs.append(((kind, h), h % 4, drain))
    chunk("v", 0, 0, "av")
    jobs += [(("v", "s", j), 4, "v") for j in range(4)]
    chunk("v", 1, 1, "av")
    chunk("g", 0, 0, "vv")
    chunk("g", 1, 1, "vv")
    chunk("ga", 0, 0, "vv")
    for n in range(4):
        jobs.append((("score", n // 2, n % 2), 5 + n % 3, "v"))
    for n in range(4):
        jobs.append((("kT", n // 2, n % 2), 5 + (n + 1) % 3, "a"))
    jobs += [(("g", "s", j), 4, "v") for j in range(4)]
    chunk("ga", 1, 1, "vv")
    for n in range(NCH):
        jobs.append((("dS", n, 0), 4, "v"))
        jobs.append((("dS", n, 1), 7, "v"))
        if n % 4 == 3:
            for half in range(2):
                jobs.append((("o", n // 4, half), 5 + half, "v"))
    chunk("u", 0, 0, "av")
    chunk("u", 1, 1, "av")
    chunk("gb", 0, 0, "aa")
    jobs += [(("u", "s", j), 4, "a") for j in range(4)]
    chunk("gb", 1, 1, "aa")
    jobs.append((("os",), 7, "v"))
    for c in range(KD):
        jobs.append((("dT", c), c % 4, "av"[c % 2]))
    for t in range(2):
        for half in range(2):
            jobs.append((("yp", t, half), 4 + 2 * t + half, "v"))
    jobs += [(("yp", 2, j), 4, "v") for j in range(4)]
    norm("mT", (0, 1), "aa")
    for t in range(2):
        for half in range(2):
            jobs.append((("x1", t, half), 2 * t + half, "v"))
    norm("mT", (2,), "aa")
    jobs += [(("x1", 2, j), 5, "v") for j in range(4)]
    norm("h2T")
    jobs.append((("lgT",), 6, "v"))
    jobs.append((("lg",), 7, "v"))
    jobs.append((("rank",), 0, "v"))
    jobs.append((("count",), 1, "v"))
    jobs.append((("wT",), 2, "v"))
    for t in range(2):
        for half in range(2):
            jobs.append((("bd", t, half), (0, 1, 6, 7)[2 * t + half], "v"))
    jobs += [(("bd", 2, j), 4, "v") for j in range(4)]
    jobs += [(("pT", k), (2, 5)[k], "a") for k in range(2)]
    for t in range(2):
        for half in range(2):
            jobs.append((("pp", t, half), (0, 1, 6, 7)[2 * t + half], "av"[t]))
    jobs += [(("pp", 2, j), 4, "a") for j in range(4)]
    norm("h3T")
    for t in range(2):
        for half in range(2):
            jobs.append((("pg", t, half), 4 * t + half, "a"))
    jobs += [(("pg", 2, j), 6, "a") for j in range(4)]
    return jobs


def build(nc, x_prompt, x_sample, p_prompt, p_sample, state_hgrn, state_pool, g_mix, w_in,
          hg_lb_logits, hg_norm, w_pool, pool_scale, w_out, g_ffn, w_router, b_router, w_gate, b_gate,
          w_up, b_up, w_down, b_down, g_ple, w_ple_gate, w_ple_proj, g_final,
          y_prompt, y_sample, new_hgrn_prompt, new_pool_prompt, new_hgrn_sample, new_pool_sample):
    jobs = bank_jobs()
    order = {name: n for n, (name, _, _) in enumerate(jobs)}
    drainer = {name: e for name, _, e in jobs}
    drain_count, before = {}, {}
    seen, last = {"a": 0, "v": 0}, {}
    for name, bank, e in jobs:
        seen[e] += 1
        drain_count[name] = seen[e]
        before[name] = last.get(bank)
        last[bank] = name

    with ExitStack() as ctx:
        def sem(name):
            return ctx.enter_context(nc.semaphore(name))

        arena = ctx.enter_context(nc.sbuf_tensor("arena", [P, 53200], F32))
        bank = [ctx.enter_context(nc.psum_tensor(f"bank{n}", [P, HALF], F32)) for n in range(8)]
        at = [0]

        def take(floats):
            at[0] += floats
            assert at[0] <= 53200, at[0]
            return at[0] - floats

        def view(start, floats, rows=P):
            return arena[0:rows, start:start + floats]

        R = take(NGRAN * GRAN)
        X = take(3 * D)
        HT = take(KD * T)
        HG = take(5 * KD * T)
        V = take(3 * D)
        OG = take(3 * D)
        TMP = take(2 * HALF)
        G0 = take(D)
        G12 = take(2 * D)
        ident = view(take(P), P)
        cmask = view(take(P), P).bitcast(I32)
        before_t = view(take(P), P)
        ones = view(take(P), P)
        BAND = take(4 * (144 + P))
        dm8 = view(take(64), 64).rearrange("p (b c) -> p b c", b=8)
        selw = view(take(32), 32).rearrange("p (g b) -> p g b", g=4)
        wr = view(take(KD * NE), KD * NE).rearrange("p (k e) -> p k e", k=KD)
        LB = take(8)
        lb = view(LB, 8)
        omlb = view(take(8), 8)
        lgin = view(OG, P)
        lbt = view(take(32), 32)
        hgn = view(take(P), P)
        brt = view(take(1), 1, NE)
        stat = view(take(32), 32)
        eps = view(take(1), 1)
        flag = view(take(1), 1, 1).bitcast(I32)
        fs = view(take(64), 64).rearrange("p (h b) -> p h b", h=H)
        ks = view(take(64), 64).rearrange("p (h b) -> p h b", h=H)
        ebl = view(take(64), 64).rearrange("p (h n) -> p h n", h=H)

        def rows3(start):
            return view(start, 3 * D).rearrange("p (t d) -> p t d", t=3)

        def heads(start):
            return view(start, KD * T).rearrange("p (k t) -> p k t", k=KD)

        x = rows3(X)
        hT = heads(HT)
        w_slot = [view(R + s * 4096, 4096).rearrange("p (k n) -> p k n", k=KD) for s in range(NSLOT)]
        s0 = view(R + 4 * 4096, 8192).rearrange("p (b h v) -> p b h v", b=NS, h=H)
        qh, fh, kh, t1, t2 = (heads(HG + n * KD * T) for n in range(5))
        score = view(HG + 4 * KD * T, 2048).rearrange("p (n c) -> p n c", n=4)
        ktok = view(HG + 2 * KD * T, 2048).rearrange("p (t k) -> p t k", t=2)
        qm = view(HG + 3 * KD * T + 1024, 512).rearrange("p (h b c) -> p h b c", h=H, b=NS)
        state = [view(HG + KD * T + n * 1024, 1024).rearrange("p (h v) -> p h v", h=H) for n in range(2)]
        v = rows3(V)
        og = rows3(OG)
        tmp = [view(TMP + n * HALF, HALF) for n in range(2)]
        u = rows3(HG)
        gb = rows3(HG + 3072)
        dT = heads(HG + 6144)
        mT = heads(HG + 8256)
        htok = rows3(V)
        bufrows = view(V, D, NS * BUF)
        gmix_b = view(G0, D)
        pscale_b = view(G0, D)
        gffn_b = view(V + D, D)
        v_all = [view(G12 + n * D, D) for n in range(2)]
        wpool = view(G12, 2048).rearrange("p (g k n) -> p g k n", g=4, k=2)
        wout = view(R + 8 * GRAN, 8192).rearrange("p (k n) -> p k n", k=KD)
        band0 = [view(BAND + g * 144, 144) for g in range(4)]
        band1 = [view(BAND + 4 * 144 + g * P, P) for g in range(4)]

        h2 = rows3(OG)
        gran = [view(R + g * GRAN if g < NGRAN else HG + (g - NGRAN) * GRAN, GRAN).rearrange(
            "p (j n) -> p j n", j=2) for g in range(RING)]
        wproj = view(HG + 8192, 2048).rearrange("p (k n) -> p k n", k=2)
        bias_g = view(V, D, NE)
        bias_u = view(V + D, D, NE)
        bias_d = view(V + 2 * D, D, NE)
        xT_e = view(G12, D)
        xg_tok = y_sb = sig_sb = view(G12 + D, D)
        g_sb = actT = view(TMP, D)
        u_sb = act_sb = view(G0, D)
        comb = view(BAND, T)
        slot_tab = view(HT, 3 * NTAB).rearrange("p (t c) -> p t c", t=3)
        wt_tab = view(HT + 3 * NTAB, 3 * NTAB).rearrange("p (t c) -> p t c", t=3)
        ohw = view(HT + 6 * NTAB, 3 * P).rearrange("p (t c) -> p t c", t=3)
        oh = view(HT + 6 * NTAB + 3 * P, 3 * P).rearrange("p (t c) -> p t c", t=3)
        esel = view(HT + 6 * NTAB + 6 * P, P, NE)
        eis = view(HT + 6 * NTAB + 7 * P, NTAB, NE)
        iota = view(take(P), P)
        dw8 = view(take(32), 32, NS).rearrange("p (g b) -> p g b", g=4)

        def small(n, k=1):
            start = G12 + small.at
            small.at += 3 * n
            return view(start, 3 * n).rearrange("p (t c) -> p t c", t=3)
        small.at = 0
        lg, msk, wdn = (small(NE) for _ in range(3))
        hit, hit_w = (small(TOPK * NE).rearrange("p t (k e) -> p t k e", k=TOPK) for _ in range(2))
        top, topf, exw = small(8), small(8), small(4)
        topi = small(8).bitcast(U32)
        ssum, rsum = small(1), small(1)
        wT = view(HG + 10240, T, NE)
        lgT = view(G12 + small.at, T, NE)
        assert small.at + T <= 2048

        ptok = view(BAND + T, 3 * PLE).rearrange("p (t d) -> p t d", t=3)
        pT = view(G0, 2 * T).rearrange("p (k t) -> p k t", k=2)
        pps = [view(HG + 8192, D), view(HG + 8192 + D, D), view(V + 2 * D, D)]
        gple_b = view(BAND + T, D)
        assert BAND + T + D <= LB
        h3 = rows3(R + 8192)
        gfin_b = view(R + 12288, D)
        pgs = rows3(R + 13312)
        yout = rows3(R + 16384)
        sq = view(R + 22528, D)

        filled = sem("bank_filled")
        drained = {"a": sem("bank_drained_by_scalar"), "v": sem("bank_drained_by_vector")}
        s_pool = sem("pool_step")
        s_dve = sem("vector_step")
        s_act = sem("scalar_step")
        s_const = sem("constants_ready")
        s_x = sem("x_loaded")
        s_w = [sem(f"w_in_slot{n}_loaded") for n in range(NSLOT)]
        names = ("gmix pscale gffn lbin hgn br wr wpool s0 wout bufrows bias bdown ple wproj gple gfin ptok").split()
        ld = {n: sem(f"{n}_loaded") for n in names}
        s_rows = sem("normalised_rows_ready")
        s_sumsq = sem("squares_summed")
        s_osq = sem("sample_output_rms_ready")
        s_lb = sem("lower_bound_ready")
        s_lbe = sem("lower_bound_exponentials")
        s_sig = sem("sigmoid_in_sbuf")
        s_tfull = sem("tmp_filled")
        s_fdone = sem("forget_gate_ready")
        s_prep = sem("hgrn_vector_step")
        s_prepa = sem("hgrn_scalar_step")
        s_sczero = sem("score_buffer_zeroed")
        s_inter = sem("state_read_by_tensor")
        s_ogp = sem("output_gate_times_norm_gain")
        s_qm = sem("sample_queries_ready")
        s_vall = [sem(f"sample_values{n}_loaded") for n in range(2)]
        s_snew = sem("sample_state_ready")
        s_decay = sem("sample_state_decayed")
        s_snst = sem("sample_state_stored")
        s_merged = sem("merged_ready")
        s_rt = sem("router_vector_step")
        s_rta = sem("router_exponentials")
        s_tab = sem("routing_tables_ready")
        s_oh = sem("token_selectors_ready")
        s_ohw = sem("weighted_selectors_ready")
        s_used = sem("granule_used")
        s_gr = [sem(f"granule{g}_loaded") for g in range(RING)]
        s_ust = sem("pooling_rows_stored")
        s_gbs = sem("pool_gate_scaled")
        s_gate = sem("gate_sums_ready")
        s_up = sem("up_sums_ready")
        s_gclip = sem("gate_clipped")
        s_gsig = sem("gate_sigmoid_ready")
        s_uclip = sem("up_clipped")
        s_actr = sem("activation_ready")
        s_xg = sem("gathered_rows_in_psum")
        s_xgs = sem("gathered_rows_in_sbuf")
        s_xgt = sem("gathered_rows_transposed")
        s_xe = sem("expert_input_ready")
        s_cT = sem("combine_matrix_in_psum")
        s_c = sem("combine_matrix_ready")
        s_aT = sem("activation_transposed")
        s_aTs = sem("activation_transposed_in_sbuf")
        s_y = sem("expert_output_in_psum")
        s_ys = sem("expert_output_in_sbuf")
        s_mix = sem("combined_rows_in_psum")
        s_free23, s_free45, s_free6 = (sem(f"banks_{n}_added_to_x") for n in ("23", "45", "6"))
        s_esel = sem("expert_selector_ready")
        s_end = sem("experts_done")
        s_stst = sem("prompt_state_stored")
        s_dloop = sem("vector_step_in_expert")
        s_xfin = sem("x_final")
        s_yout = sem("y_ready")
        s_out = sem("outputs_stored")
        n_out = [0]

        def fill_done(ins, name):
            ins.then_inc(filled, 1)

        def wait_filled(eng, name):
            eng.wait_ge(filled, order[name] + 1)

        def wait_drained(eng, name):
            eng.wait_ge(drained[drainer[name]], drain_count[name])

        def drain_done(ins, name):
            ins.then_inc(drained[drainer[name]], 1)

        def job_bank(name):
            return bank[jobs[order[name]][1]]

        def lanes(t):
            return slice(0, TS[t])

        def toks(t):
            return slice(t * P, t * P + TS[t])

        def halves(h):
            return slice(h * HALF, (h + 1) * HALF)

        def pieces(t):
            return range(2 if t < 2 else 4)

        def cols(t, n):
            return halves(n) if t < 2 else slice(n * 256, (n + 1) * 256)

        def piece(name):
            _, t, n = name
            return job_bank(name)[:, :] if t < 2 else job_bank(name)[32 * n:32 * n + NS, 0:256]

        last_use = [("f", 3), ("f", 7), ("q", 3), ("q", 7), ("v", "s", 3), ("v", 1, 1),
                    ("g", "s", 3), ("g", "s", 3), ("g", "s", 3), ("ga", 1, 1)]
        rows_of = state_pool.rearrange("o b j d -> (o b j) d")

        tmp_jobs = [("g", n, t) for n in range(2) for t in range(2)] + [("ga", 0, 0), ("ga", 0, 1)]
        tmp_jobs += [("g", "s", j) for j in range(4)] + [("ga", 1, 0), ("ga", 1, 1)]
        tmp_jobs += [("o", t, half) for t in range(2) for half in range(2)]
        after_x = [(), ("x1",), ()]

        def turned_bank(name, dst, copy):
            _, t, half = name
            n = TS[t]
            ks_ = slice(4 * half, 4 * half + 4) if t < 2 else slice(0, KD)
            src = job_bank(name)[:, 0:(ks_.stop - ks_.start) * n].rearrange("p (k t) -> p k t", t=n)
            copy(name, dst[:, ks_, toks(t)], src)

        block = ctx.enter_context(nc.Block())

        @block.sync
        def _(sp):
            xp = x_prompt[0].rearrange("(t p) d -> p t d", p=P)
            sp.dma_start(x[:, 0, :], xp[:, 0, :]).then_inc(s_x, 16)
            sp.dma_start(x[:, 1, :], xp[:, 1, :]).then_inc(s_x, 16)
            sp.dma_start(x[0:NS, 2, :], x_sample[:, 0, :]).then_inc(s_x, 16)
            wi = w_in[0].rearrange("(k p) n -> p k n", p=P)
            for c, (_, col) in enumerate(W_CHUNKS):
                if c >= NSLOT:
                    wait_filled(sp, last_use[c - NSLOT])
                sp.dma_start(w_slot[c % NSLOT], wi[:, :, col:col + HALF]).then_inc(s_w[c % NSLOT], 16)

            parts = [w.rearrange("o e (g j p) n -> (o e) g p j n", j=2, p=P) for w in (w_gate, w_up, w_down)]
            ple = w_ple_gate[0].rearrange("(g j p) n -> g p j n", j=2, p=P)

            def load_experts(i, e):
                for n in range(PER):
                    for m in range(3):
                        for g in range(4):
                            for one in range(2):
                                at_ = 2 * NGRAN * n + 8 * m + 2 * g + one
                                sp.wait_ge(s_used, 2 * NGRAN * i + at_ + 1)
                                sp.dma_start(gran[at_ % RING], parts[m][e + 2 * n + one, g])\
                                  .then_inc(s_gr[at_ % RING], 16)

            def load_ple():
                for g in range(4):
                    sp.dma_start(gran[g], ple[g]).then_inc(ld["ple"], 16)

            wait_drained(sp, ("v", "s", 3))
            for b in range(NS):
                if b >= 2:
                    sp.wait_ge(s_snew, b - 1)
                sp.dma_start(v_all[b % 2], v[b:b + 1, 2, :].unsqueeze(1).to_broadcast([1, P, D])).then_inc(s_vall[b % 2], 16)
            sp.wait_ge(s_snew, NS)
            sp.dma_start(wpool, w_pool[0].rearrange("g (k p) n -> p g k n", p=P)).then_inc(ld["wpool"], 16)
            sp.wait_ge(s_snst, 16 * NS)
            wait_drained(sp, ("os",))
            for k in range(4):
                sp.dma_start(wout[:, 2 * k:2 * k + 2], w_out[0].rearrange("(k p) n -> p k n", p=P)[
                    :, 2 * k:2 * k + 2]).then_inc(ld["wout"], 16)
            sp.wait_ge(s_ust, 32)
            with sp.Fori(0, PAIRS // PER) as q:
                load_experts(PER * q, 2 * PER * q)
            sp.wait_ge(s_used, NGRAN * NE + 4)
            load_ple()
            more = sp.value_load(flag)
            with sp.If(more > 0):
                sp.wait_ge(ld["ple"], 64)
                with sp.Fori(1, NBLK) as b:
                    with sp.Fori(0, PAIRS // PER) as q:
                        load_experts(b * PAIRS + PER * q, 2 * PER * q)
                sp.wait_ge(s_used, NGRAN * NE * NBLK + 4)
                load_ple()

        @block.gpsimd
        def _(pool):
            chain = [0]

            def step(ins):
                chain[0] += 1
                ins.then_inc(s_pool, 1)
                pool.wait_ge(s_pool, chain[0])

            def store(dst, src):
                pool.dma_start(dst, src).then_inc(s_out, 16)
                n_out[0] += 1

            step(pool.memset(ident, 0.0))
            step(pool.affine_select(out=ident, in_=ident, compare_op=ALU.not_equal, fill=1.0, base=0,
                                    pattern=[[-1, P]], channel_multiplier=1))
            step(pool.memset(ones, 1.0))
            step(pool.memset(eps, EPS))
            pool.memset(stat, 0.0).then_inc(s_const, 1)
            for b in range(NS):
                pool.dma_start(s0[:, b], state_hgrn[0, b].rearrange("h k v -> k h v")).then_inc(ld["s0"], 16)
            step(pool.memset(before_t, 1.0))
            step(pool.affine_select(out=before_t, in_=before_t, compare_op=ALU.is_gt, fill=0.0, base=0,
                                    pattern=[[1, P]], channel_multiplier=-1))
            cm = iota
            step(pool.memset(cm, 1.0))
            step(pool.affine_select(out=cm, in_=cm, compare_op=ALU.is_ge, fill=0.0, base=0,
                                    pattern=[[1, P]], channel_multiplier=-1))
            step(pool.affine_select(out=cm, in_=cm, compare_op=ALU.is_ge, fill=0.0, base=0,
                                    pattern=[[-CH, P // CH], [0, CH]], channel_multiplier=1))
            step(pool.tensor_copy(cmask, cm))
            step(pool.iota(iota.rearrange("p (c n) -> p c n", c=2), [[0, 2], [1, CAP]], base=0,
                           channel_multiplier=0, allow_small_or_imprecise_dtypes=True))
            step(pool.memset(dm8, 0.0))
            step(pool.affine_select(out=dm8, in_=dm8, compare_op=ALU.not_equal, fill=1.0, base=0,
                                    pattern=[[1, 8], [-1, 8]], channel_multiplier=0))
            for g, w in enumerate(WINDOWS):
                step(pool.memset(band0[g], 1.0 / w))
                for t in range(w - 1):
                    pool.memset(band0[g][:, t:t + 1], 1.0 / (t + 1))
                step(pool.memset(band1[g], 1.0 / w))
                for m, n in ((band0[g], 144), (band1[g], P)):
                    step(pool.affine_select(out=m, in_=m, compare_op=ALU.is_ge, fill=0.0, base=0,
                                            pattern=[[1, n]], channel_multiplier=-1))
                    step(pool.affine_select(out=m, in_=m, compare_op=ALU.is_ge, fill=0.0, base=w - 1,
                                            pattern=[[-1, n]], channel_multiplier=1))
                    step(pool.tensor_tensor(m[:, 0:P], m[:, 0:P], ident, ALU.subtract))
                m = selw[:, g, :]
                step(pool.memset(m, 1.0 / w))
                step(pool.affine_select(out=m, in_=m, compare_op=ALU.is_ge, fill=0.0, base=-(BUF + 1 - w),
                                        pattern=[[-BUF, 8]], channel_multiplier=1))
                step(pool.affine_select(out=m, in_=m, compare_op=ALU.is_ge, fill=0.0, base=BUF - 1,
                                        pattern=[[BUF, 8]], channel_multiplier=-1))
            pool.memset(dm8[:, 0, 0:1], 1.0).then_inc(s_const, 1)

            pool.wait_ge(s_prepa, 5)
            pool.memset(score, 0.0).then_inc(s_sczero, 1)
            wait_drained(pool, ("score", 1, 1))
            pool.tensor_tensor(qm, dm8.unsqueeze(1).to_broadcast([P, H, 8, 8]),
                               qh[:, :, SEQ:T].unsqueeze(3).to_broadcast([P, H, 8, 8]),
                               ALU.mult).then_inc(s_qm, 1)
            for b in range(NS):
                store(new_pool_sample[0, b, 0:BUF - 1, :], state_pool[0, b, 1:BUF, :])
            pool.wait_ge(ld["hgn"], 16)
            wait_drained(pool, ("ga", 1, 1))
            for t in range(NT):
                o = og[lanes(t), t, :].rearrange("p (h v) -> p h v", h=H)
                pool.tensor_tensor(o, o, hgn[lanes(t)].unsqueeze(1).to_broadcast([TS[t], H, P]),
                                   ALU.mult).then_inc(s_ogp, 1)
            wait_drained(pool, ("o", 1, 1))
            wait_drained(pool, ("dS", NCH - 1, 1))
            pool.dma_start(pscale_b, pool_scale.partition_broadcast(P)[:, 0, :]).then_inc(ld["pscale"], 16)
            pool.dma_start(bufrows, rows_of).then_inc(ld["bufrows"], 16)
            pool.dma_start(gffn_b, g_ffn.partition_broadcast(P)[:, 0, :]).then_inc(ld["gffn"], 16)
            pool.dma_start(new_hgrn_prompt[0, 0].rearrange("h k v -> k h v"), state[NCH % 2]).then_inc(s_stst, 16)
            for b in range(NS):
                pool.wait_ge(s_snew, b + 1)
                pool.dma_start(new_hgrn_sample[0, b].rearrange("h k v -> k h v"), s0[:, b]).then_inc(s_snst, 16)
            wait_drained(pool, ("u", 0, 1))
            wait_drained(pool, ("u", 1, 1))
            pool.dma_start(new_pool_prompt[0, 0], u[P - BUF:P, 1, :]).then_inc(s_ust, 16)
            wait_drained(pool, ("u", "s", 3))
            pool.dma_start(new_pool_sample[0, :, BUF - 1, :], u[0:NS, 2, :]).then_inc(s_ust, 16)
            pool.wait_ge(ld["pscale"], 16)
            wait_drained(pool, ("gb", 1, 1))
            for t in range(NT):
                pool.tensor_tensor(gb[lanes(t), t, :], gb[lanes(t), t, :], pscale_b[lanes(t)],
                                   ALU.mult).then_inc(s_gbs, 1)
            pool.wait_ge(s_rows, 6)
            pool.dma_start(bias_g, b_gate[0]).then_inc(ld["bias"], 16)
            pool.dma_start(bias_u, b_up[0]).then_inc(ld["bias"], 16)
            pool.dma_start(bias_d, b_down[0]).then_inc(ld["bdown"], 16)
            pool.dma_start(ptok[:, 0:2, :], p_prompt[0, 0].rearrange("(t p) d -> p t d", p=P)).then_inc(ld["ptok"], 16)
            pool.dma_start(ptok[0:NS, 2, :], p_sample[0, :, 0, :]).then_inc(ld["ptok"], 16)
            pool.wait_ge(s_stst, 16)
            pool.wait_ge(s_ust, 32)
            pool.dma_start(wproj, w_ple_proj[0].rearrange("(k p) n -> p k n", p=P)).then_inc(ld["wproj"], 16)
            wait_filled(pool, ("pT", 1))
            pool.dma_start(gple_b, g_ple.partition_broadcast(P)[:, 0, :]).then_inc(ld["gple"], 16)
            pool.wait_ge(s_end, 1)
            pool.dma_start(gfin_b, g_final.partition_broadcast(P)).then_inc(ld["gfin"], 16)
            for t in range(2):
                pool.wait_ge(s_yout, t + 1)
                store(y_prompt[0, toks(t), :], yout[:, t, :])
            pool.wait_ge(s_yout, 3)
            store(y_sample[:, 0, :], yout[0:NS, 2, :])
            pool.wait_ge(s_out, 16 * n_out[0])

        @block.tensor
        def _(pe):
            def begin(name):
                if before[name]:
                    wait_drained(pe, before[name])

            def turn_rows(tag, src, ready, n_used=0, tiles=range(NT)):
                for t in tiles:
                    pe.wait_ge(*ready(t))
                    n = TS[t]
                    for half in range(2 if t < 2 else 1):
                        name = (tag, t, half)
                        begin(name)
                        ks_ = range(4 * half, 4 * half + 4) if t < 2 else range(KD)
                        for j, k in enumerate(ks_):
                            ins = pe.transpose(job_bank(name)[:, j * n:(j + 1) * n], src[0:n, t, k * P:(k + 1) * P],
                                               ident[0:n, 0:n])
                            if n_used and k != ks_[-1]:
                                n_used -= 1
                                ins.then_inc(s_used, 1)
                        fill_done(ins, name)

            def keep_warm(n, out):
                for _ in range(n):
                    pe.matmul(out[:, :], ident, h2[:, 0, 0:HALF], start=True, stop=True)

            def wait_turned(tag, tiles=range(NT)):
                for t in tiles:
                    for half in range(2 if t < 2 else 1):
                        wait_drained(pe, (tag, t, half))

            chunk_no = {}
            for c, (kind, _) in enumerate(W_CHUNKS):
                chunk_no[(kind, c - [k for k, _ in W_CHUNKS].index(kind))] = c

            def wait_chunk(c):
                pe.wait_ge(s_w[c % NSLOT], 16 * (c // NSLOT + 1))

            def chunk_step(kind, n, k, signal=None):
                w = w_slot[chunk_no[(kind, n)] % NSLOT]
                for t in range(2):
                    name = (kind, n, t)
                    if k == 0:
                        begin(name)
                    ins = pe.matmul(job_bank(name)[:, :], hT[:, k, toks(t)], w[:, k, :],
                                    start=(k == 0), stop=(k == KD - 1))
                    if k == KD - 1:
                        fill_done(ins, name)
                    elif t == 0 and signal:
                        ins.then_inc(signal, 1)

            def chunk(kind, n):
                wait_chunk(chunk_no[(kind, n)])
                for k in range(KD):
                    chunk_step(kind, n, k)

            def sample_rows(kind, chunks):
                per = 4 // len(chunks)
                width = HALF // per
                name = (kind, "s", 0)
                begin(name)
                for c in chunks:
                    wait_chunk(c)
                for k in range(KD):
                    for j in range(4):
                        c, at_ = chunks[j // per], width * (j % per)
                        ins = pe.matmul(job_bank(name)[32 * j:32 * j + NS, 0:width], hT[:, k, toks(2)],
                                        w_slot[c % NSLOT][:, k, at_:at_ + width], start=(k == 0), stop=(k == KD - 1))
                        if k == KD - 1:
                            fill_done(ins, (kind, "s", j))

            pe.wait_ge(s_const, 1)
            pe.wait_ge(ld["lbin"], 16)
            fill_done(pe.transpose(bank[7][:, 0:16], lgin[0:16, :], ident[0:16, 0:16]), ("lb",))
            turn_rows("hT", htok, lambda t: (s_rows, t + 1))
            wait_turned("hT")

            for kind in ("f", "q"):
                for h in range(H):
                    c = chunk_no[(kind, h // 4)]
                    wait_chunk(c)
                    begin((kind, h))
                    for k in range(KD):
                        ins = pe.matmul(job_bank((kind, h))[:, 0:T],
                                        w_slot[c % NSLOT][:, k, (h % 4) * P:(h % 4 + 1) * P], hT[:, k, :],
                                        start=(k == 0), stop=(k == KD - 1))
                    fill_done(ins, (kind, h))
            chunk("v", 0)
            sample_rows("v", (4, 5))
            chunk("v", 1)
            chunk("g", 0)
            chunk("g", 1)
            chunk("ga", 0)

            pe.wait_ge(s_prep, 5)
            for t in range(2):
                for half in range(2):
                    name = ("score", t, half)
                    begin(name)
                    for j in range(4):
                        h = 4 * half + j
                        ins = pe.matmul(job_bank(name)[:, j * P:(j + 1) * P], t1[:, h, toks(t)], qh[:, h, toks(t)],
                                        start=True, stop=True)
                    fill_done(ins, name)
            for t in range(2):
                for half in range(2):
                    name = ("kT", t, half)
                    begin(name)
                    for j in range(4):
                        ins = pe.transpose(job_bank(name)[:, j * P:(j + 1) * P], fh[:, 4 * half + j, toks(t)], ident)
                    fill_done(ins, name)
            sample_rows("g", (6, 7, 8, 9))
            chunk("ga", 1)

            wait_chunk(chunk_no[("u", 0)])
            for name in [("kT", t, half) for t in range(2) for half in range(2)] + [("v", n, t) for n in range(2) for t in range(2)]:
                wait_drained(pe, name)
            for n in range(NCH):
                t, row = n // 4, CH * (n % 4)
                rr = slice(row, row + CH)
                for half in range(2):
                    name = ("dS", n, half)
                    begin(name)
                    for j in range(4):
                        hh = slice((4 * half + j) * P, (4 * half + j + 1) * P)
                        ins = pe.matmul(job_bank(name)[:, j * P:(j + 1) * P], ktok[rr, t, hh], v[rr, t, hh],
                                        start=True, stop=True)
                    fill_done(ins, name)
                for half in range(2):
                    name = ("o", t, half)
                    if n % 4 == 0:
                        begin(name)
                        wait_drained(pe, ("score", t, half))
                        for j in range(4):
                            h = 4 * half + j
                            ins = pe.matmul(job_bank(name)[:, j * P:(j + 1) * P],
                                            score[:, 2 * t + half, j * P:(j + 1) * P], v[:, t, h * P:(h + 1) * P],
                                            start=(j == 0), stop=True, skip_group_check=True)
                    if n > 0:
                        wait_drained(pe, ("dS", n - 1, 1))
                        for j in range(4):
                            h = 4 * half + j
                            ins = pe.matmul(job_bank(name)[rr, j * P:(j + 1) * P], qh[:, h, n * CH:(n + 1) * CH],
                                            state[n % 2][:, h, :], start=False, stop=True,
                                            skip_group_check=True, tile_position=(0, row))
                    if n % 4 == 3:
                        fill_done(ins, name)
                chunk_step("u", 0, n, signal=s_inter)
            chunk("u", 1)
            chunk("gb", 0)
            sample_rows("u", (10, 11, 12, 13))
            chunk("gb", 1)
            begin(("os",))
            pe.wait_ge(s_qm, 1)
            pe.wait_ge(s_snew, NS)
            for hh in range(2):
                for b in range(NS):
                    for j in range(4):
                        h = 4 * hh + j
                        ins = pe.matmul(job_bank(("os",))[32 * j:32 * j + NS, hh * P:(hh + 1) * P], qm[:, h, b, :],
                                        s0[:, b, h, :], start=(b == 0), stop=(b == NS - 1))
            fill_done(ins, ("os",))

            for name in [("u", n, t) for n in range(2) for t in range(2)] + [("u", "s", 3)]:
                wait_drained(pe, name)
            pe.wait_ge(ld["bufrows"], 16)
            pe.wait_ge(s_const, 2)
            for c in range(KD):
                name, g = ("dT", c), c // 2
                begin(name)
                o, cc = job_bank(name), slice(c * P, (c + 1) * P)
                pe.matmul(o[:, 0:144], u[:, 0, cc], band0[g], start=True, stop=True, skip_group_check=True).then_inc(s_used, 1)
                pe.matmul(o[:, P:SEQ], u[:, 1, cc], band1[g], start=False, stop=True, skip_group_check=True)
                pe.matmul(o[:, SEQ:T], bufrows[:, cc], selw[0:NS * BUF, g, :], start=True, stop=False)
                ins = pe.matmul(o[:, SEQ:T], u[0:NS, 2, cc], dw8[0:NS, g, :], start=False, stop=True)
                fill_done(ins, name)
            pe.wait_ge(ld["wpool"], 16)
            for c in range(KD):
                wait_drained(pe, ("dT", c))
            for t in range(2):
                for half in range(2):
                    name = ("yp", t, half)
                    begin(name)
                    for gg in range(2):
                        g = 2 * half + gg
                        for k in range(2):
                            ins = pe.matmul(job_bank(name)[lanes(t), gg * 256:(gg + 1) * 256],
                                            dT[:, 2 * g + k, toks(t)], wpool[:, g, k, :],
                                            start=(k == 0), stop=(k == 1))
                    fill_done(ins, name)
            begin(("yp", 2, 0))
            for k in range(2):
                for g in range(4):
                    ins = pe.matmul(piece(("yp", 2, g)), dT[:, 2 * g + k, toks(2)], wpool[:, g, k, :],
                                    start=(k == 0), stop=(k == 1))
                    if k == 1:
                        fill_done(ins, ("yp", 2, g))
            turn_rows("mT", og, lambda t: (s_merged, t + 1), tiles=(0, 1))
            pe.wait_ge(ld["wout"], 64)

            def weights(w, k, half):
                return gran[k // 2][:, k % 2, halves(half)] if w is None else w[:, k, halves(half)]

            def quarter(w, k, n):
                return gran[k // 2][:, k % 2, cols(2, n)] if w is None else w[:, k, cols(2, n)]

            def product(tag, t, src, w, slices=KD):
                if t < 2:
                    for half in range(2):
                        name = (tag, t, half)
                        begin(name)
                        for k in range(slices):
                            ins = pe.matmul(job_bank(name)[:, :], src[:, k, toks(t)], weights(w, k, half),
                                            start=(k == 0), stop=(k == slices - 1))
                        fill_done(ins, name)
                else:
                    begin((tag, 2, 0))
                    for k in range(slices):
                        for n in pieces(t):
                            ins = pe.matmul(piece((tag, 2, n)), src[:, k, toks(2)],
                                            quarter(w, k, n), start=(k == 0), stop=(k == slices - 1))
                            if k == slices - 1:
                                fill_done(ins, (tag, 2, n))

            for t in range(NT):
                if t == 2:
                    turn_rows("mT", og, lambda t: (s_merged, t + 1), tiles=(2,))
                wait_turned("mT", (t,))
                product("x1", t, mT, wout)

            turn_rows("h2T", h2, lambda t: (s_rows, t + 4), n_used=8)
            pe.wait_ge(ld["wr"], 16)
            wait_turned("h2T")
            begin(("lgT",))
            for k in range(KD):
                ins = pe.matmul(bank[6][0:NE, 0:T], wr[:, k, :], hT[:, k, :], start=(k == 0), stop=(k == KD - 1))
            fill_done(ins, ("lgT",))
            begin(("lg",))
            wait_drained(pe, ("lgT",))
            for t in range(NT):
                ins = pe.transpose(bank[7][lanes(t), t * NE:(t + 1) * NE], lgT[:, toks(t)], ident[0:NE, 0:NE])
            fill_done(ins, ("lg",))
            keep_warm(4, bank[3])
            pe.wait_ge(s_rt, 2)
            begin(("rank",))
            for t in range(NT):
                for s in range(t):
                    pe.matmul(bank[0][:, t * NE:(t + 1) * NE], ones, msk[:, s, :], start=(s == 0), stop=False)
                n = TS[t]
                ins = pe.matmul(bank[0][:, t * NE:(t + 1) * NE], before_t[0:n, :], msk[0:n, t, :],
                                start=(t == 0), stop=True)
            fill_done(ins, ("rank",))
            begin(("count",))
            for t in range(NT):
                n = TS[t]
                ins = pe.matmul(bank[1][0:8, 0:NE], ones[0:n, 0:8], msk[0:n, t, :], start=(t == 0), stop=(t == NT - 1))
            fill_done(ins, ("count",))
            pe.wait_ge(s_rt, 3)
            begin(("wT",))
            for t in range(NT):
                ins = pe.transpose(bank[2][0:NE, toks(t)], wdn[lanes(t), t, :], ident[lanes(t), lanes(t)])
            fill_done(ins, ("wT",))
            GATE, UP, AT, XG, Y, CT = bank[0:2], bank[2:4], bank[4:6], bank[6:8], bank[0:2], bank[4]

            def hp(one):
                return slice(CAP * one, CAP * one + CAP)

            def gather():
                for c in range(2):
                    for t in range(NT):
                        ins = pe.matmul(XG[c][:, :], oh[lanes(t), t, :], h2[lanes(t), t, halves(c)],
                                        start=(t == 0), stop=(t == NT - 1))
                return ins

            def turn_half(out, src, c):
                for j in range(4):
                    k = 4 * c + j
                    ins = pe.transpose(out[c][:, j * P:(j + 1) * P], src[:, k * P:(k + 1) * P], ident)
                return ins

            def turn_gathered():
                turn_half(XG, xg_tok, 0)
                return turn_half(XG, xg_tok, 1)

            def pair(i0, n):
                i = i0 + n

                def granules(m, g):
                    for one in range(2):
                        turn, place = divmod(2 * NGRAN * n + 8 * m + 2 * g + one, RING)
                        pe.wait_ge(s_gr[place], i0 * (16 * 2 * NGRAN // RING) + 16 * (turn + 1))
                        yield gran[place]

                def products(m, out, src, first):
                    for g in range(4):
                        if m == 2 and g % 2 == 0:
                            pe.wait_ge(s_aTs, 2 * i + g // 2 + 1)
                        w = list(granules(m, g))
                        for j in range(2):
                            k = 2 * g + j
                            for c in range(2):
                                for one in range(2):
                                    ins = pe.matmul(out[c][hp(one), :],
                                                    src[:, k * P + CAP * one:k * P + CAP * one + CAP],
                                                    w[one][:, j, halves(c)], start=(first and k == 0),
                                                    stop=(k == KD - 1))
                                    if j == 1 and c == 1 and not (g == 3 and one == 1):
                                        ins.then_inc(s_used, 1)
                    return ins

                pe.wait_ge(s_esel, i + 1)
                pe.wait_ge(s_xe, i + 1)
                for m, (out, bias, done) in enumerate(((GATE, bias_g, s_gate), (UP, bias_u, s_up))):
                    if m == 1:
                        pe.wait_ge(s_free23, i + 1)
                    for c in range(2):
                        ins = pe.matmul(out[c][:, :], esel, bias[:, halves(c)], start=True, stop=False)
                        if m == 1 and c == 0:
                            ins.then_inc(s_used, 1)
                    products(m, out, xT_e, False).then_inc(done, 1)
                pe.wait_ge(s_ohw, i + 1)
                pe.wait_ge(s_free45, i + 1)
                for t in range(NT):
                    ins = pe.transpose(CT[:, toks(t)], ohw[lanes(t), t, :], ident[lanes(t), lanes(t)])
                    if t == 0:
                        ins.then_inc(s_used, 1)
                ins.then_inc(s_cT, 1)
                pe.wait_ge(s_oh, i + 2)
                pe.wait_ge(s_free6, i + 1)
                gather().then_inc(s_xg, 1)
                pe.wait_ge(s_actr, i + 1)
                pe.wait_ge(s_c, i + 1)
                for c in range(2):
                    turn_half(AT, act_sb, c).then_inc(s_aT, 1)
                pe.wait_ge(s_xgs, i + 2)
                turn_gathered().then_inc(s_xgt, 1)
                products(2, Y, actT, True).then_inc(s_y, 1)
                pe.wait_ge(s_ys, 2 * i + 2)
                for t, banks in ((0, UP), (1, AT)):
                    for c in range(2):
                        ins = pe.matmul(banks[c][:, :], comb[:, toks(t)], y_sb[:, halves(c)], start=True, stop=True)
                        if t == 0 and c == 0:
                            ins.then_inc(s_used, 1)
                    ins.then_inc(s_mix, 1)
                pe.wait_ge(s_xe, i + 2)
                for c in range(2):
                    ins = pe.matmul(bank[6][32 * c:32 * c + NS, :], comb[:, toks(2)], y_sb[:, halves(c)],
                                    start=True, stop=True)
                ins.then_inc(s_mix, 1)

            keep_warm(2, bank[3])
            pe.wait_ge(s_oh, 1)
            wait_drained(pe, ("lg",))
            gather().then_inc(s_xg, 1)
            pe.wait_ge(s_xgs, 1)
            turn_gathered().then_inc(s_xgt, 1)
            for name in (("rank",), ("count",), ("wT",)):
                wait_drained(pe, name)
            pe.wait_ge(ld["bias"], 32)
            with pe.Fori(0, PAIRS // 2 // PER) as q:
                for n in range(PER):
                    pair(PER * q, n)
            for done in (s_free23, s_free45, s_free6):
                pe.wait_ge(done, PAIRS // 2 + 1)
            pe.wait_ge(ld["bdown"], 16)
            wait_drained(pe, ("wT",))
            for t in range(2):
                for half in range(2):
                    name = ("bd", t, half)
                    begin(name)
                    fill_done(pe.matmul(job_bank(name)[:, :], wT[:, toks(t)], bias_d[:, halves(half)],
                                        start=True, stop=True), name)
            begin(("bd", 2, 0))
            for n in pieces(2):
                fill_done(pe.matmul(piece(("bd", 2, n)), wT[:, toks(2)], bias_d[:, cols(2, n)],
                                    start=True, stop=True), ("bd", 2, n))
            pe.wait_ge(ld["ptok"], 32)
            pe.wait_ge(ld["wproj"], 16)
            for k in range(2):
                begin(("pT", k))
                for t in range(NT):
                    ins = pe.transpose(job_bank(("pT", k))[:, toks(t)], ptok[lanes(t), t, k * P:(k + 1) * P],
                                       ident[lanes(t), lanes(t)])
                fill_done(ins, ("pT", k))
            wait_drained(pe, ("pT", 1))
            for t in range(NT):
                product("pp", t, pT, wproj, 2)
            for t in range(NT):
                wait_drained(pe, ("pp", t, pieces(t)[-1]))
            with pe.Fori(PAIRS // 2 // PER, PAIRS // PER) as q:
                for n in range(PER):
                    pair(PER * q, n)
            more = pe.value_load(flag)
            with pe.If(more > 0):
                with pe.Fori(1, NBLK) as b:
                    with pe.Fori(0, PAIRS // PER) as q:
                        for n in range(PER):
                            pair(b * PAIRS + PER * q, n)
                pe.wait_ge(ld["ple"], 128)

            keep_warm(8, Y[1])
            pe.wait_ge(s_end, 1)
            turn_rows("h3T", h3, lambda t: (s_rows, t + 7))
            pe.wait_ge(ld["ple"], 64)
            for t in range(NT):
                wait_turned("h3T", (t,))
                product("pg", t, hT, None)

        @block.scalar
        def _(act):
            def copy_out(name, dst, src):
                wait_filled(act, name)
                drain_done(act.activation(dst, src, ACT.Copy), name)

            def turned(tag, dst):
                for t in range(NT):
                    for half in range(2 if t < 2 else 1):
                        name = (tag, t, half)
                        if drainer[name] == "a":
                            turned_bank(name, dst, copy_out)

            chain = [0]

            def rms(s, n, done):
                act.wait_ge(s_act, chain[0])
                act.activation(s, s, ACT.Sqrt, bias=eps[0:s.shape[0]], scale=1.0 / n).then_inc(done, 1)

            def sum_squares(src, dst, s):
                chain[0] += 1
                act.activation(dst, src, ACT.Square, accum_out=s).then_inc(s_act, 1)

            def squares(scratch, count):
                for t in range(NT):
                    for tag in after_x[count]:
                        wait_drained(act, (tag, t, pieces(t)[-1]))
                    s = stat[lanes(t), 4 * count + t:4 * count + t + 1]
                    sum_squares(x[lanes(t), t, :], scratch[lanes(t)], s)
                    rms(s, D, s_sumsq)

            act.dma_start(gmix_b, g_mix.partition_broadcast(P)[:, 0, :]).then_inc(ld["gmix"], 16)
            act.dma_start(lgin[0:16, :], hg_lb_logits.rearrange("d (h k) -> (d h) k", k=P)).then_inc(ld["lbin"], 16)
            act.dma_start(hgn, hg_norm.partition_broadcast(P)[:, 0, :]).then_inc(ld["hgn"], 16)
            act.dma_start(brt, b_router.rearrange("o e -> e o")).then_inc(ld["br"], 16)
            act.dma_start(wr, w_router[0].rearrange("(k p) e -> p k e", p=P)).then_inc(ld["wr"], 16)
            act.wait_ge(s_x, 48)
            act.wait_ge(s_const, 1)
            squares(view(TMP, D), 0)
            turned("hT", hT)
            act.wait_ge(s_lb, 1)
            act.activation(lbt[:, 0:16], lbt[:, 0:16], ACT.Exp).then_inc(s_lbe, 1)
            for h in range(H):
                wait_filled(act, ("f", h))
                drain_done(act.activation(fh[:, h, :], job_bank(("f", h))[:, 0:T], ACT.Sigmoid), ("f", h))
            act.wait_ge(s_fdone, 1)
            act.activation(fh[:, :, 0:SEQ], fh[:, :, 0:SEQ], ACT.Ln).then_inc(s_prepa, 1)
            act.wait_ge(s_prep, 1)
            act.activation(t1[:, :, 0:SEQ], t2[:, :, 0:SEQ], ACT.Exp).then_inc(s_prepa, 1)
            act.wait_ge(s_prep, 2)
            act.activation(fh[:, :, 0:SEQ], fh[:, :, 0:SEQ], ACT.Exp).then_inc(s_prepa, 1)
            act.activation(ebl, t2[:, :, CH - 1:SEQ:CH], ACT.Exp).then_inc(s_prepa, 1)
            for h in range(H):
                wait_filled(act, ("q", h))
                act.activation(qh[:, h, :], job_bank(("q", h))[:, 0:T], ACT.Sigmoid).then_inc(s_sig, 1)
            act.wait_ge(s_prep, 4)
            act.activation(t1[:, :, 0:SEQ], t2[:, :, 0:SEQ], ACT.Exp, scale=-1.0).then_inc(s_prepa, 1)

            n_tmp = [0]

            def to_tmp(name, rows, src, func):
                m = n_tmp[0]
                n_tmp[0] += 1
                wait_filled(act, name)
                if m >= 2:
                    wait_drained(act, tmp_jobs[m - 2])
                act.activation(tmp[m % 2][rows], src, func).then_inc(s_tfull, 1)

            def gate_chunk(kind, n):
                for t in range(2):
                    to_tmp((kind, n, t), slice(0, P), job_bank((kind, n, t))[:, :], ACT.Sigmoid)

            copy_out(("v", 0, 0), v[:, 0, halves(0)], job_bank(("v", 0, 0))[:, :])
            copy_out(("v", 1, 0), v[:, 0, halves(1)], job_bank(("v", 1, 0))[:, :])
            gate_chunk("g", 0)
            gate_chunk("g", 1)
            gate_chunk("ga", 0)
            act.wait_ge(s_prep, 5)
            for t in range(2):
                for half in range(2):
                    name = ("kT", t, half)
                    copy_out(name, ktok[:, t, halves(half)], job_bank(name)[:, :])
            for j in range(4):
                to_tmp(("g", "s", j), slice(0, NS), bank[4][32 * j:32 * j + NS, :], ACT.Sigmoid)
            gate_chunk("ga", 1)

            def decay(b):
                for h in range(H):
                    ins = act.activation(s0[:, b, h, :], s0[:, b, h, :], ACT.Copy, scale=fs[:, h, b:b + 1])
                ins.then_inc(s_decay, 1)

            act.wait_ge(ld["s0"], 16 * NS)
            for t in range(2):
                for b in range(4 * t, 4 * t + 4):
                    decay(b)
                for half in range(2):
                    name, m = ("o", t, half), n_tmp[0]
                    n_tmp[0] += 1
                    wait_filled(act, name)
                    wait_drained(act, tmp_jobs[m - 2])
                    for j in range(4):
                        hh = slice(j * P, (j + 1) * P)
                        sum_squares(job_bank(name)[:, hh], tmp[m % 2][:, hh],
                                    stat[:, 16 + 4 * (m % 2) + j:17 + 4 * (m % 2) + j])
                    rms(stat[:, 16 + 4 * (m % 2):20 + 4 * (m % 2)], P, s_tfull)
            act.wait_ge(s_qm, 1)
            copy_out(("u", 0, 0), u[:, 0, halves(0)], job_bank(("u", 0, 0))[:, :])
            copy_out(("u", 1, 0), u[:, 0, halves(1)], job_bank(("u", 1, 0))[:, :])
            act.wait_ge(s_stst, 16)

            def pool_gate(n):
                for t in range(2):
                    name = ("gb", n, t)
                    wait_filled(act, name)
                    drain_done(act.activation(gb[:, t, halves(n)], job_bank(name)[:, :], ACT.Sigmoid), name)

            pool_gate(0)
            for j in range(4):
                name = ("u", "s", j)
                wait_filled(act, name)
                dst = (u if j < 2 else gb)[0:NS, 2, halves(j % 2)]
                drain_done(act.activation(dst, bank[4][32 * j:32 * j + NS, :], ACT.Copy if j < 2 else ACT.Sigmoid), name)
            pool_gate(1)
            for c in range(0, KD, 2):
                copy_out(("dT", c), dT[:, c, :], job_bank(("dT", c))[:, 0:T])
            wait_drained(act, ("os",))
            wait_drained(act, ("o", 1, 1))
            for h in range(H):
                sum_squares(v[0:NS, 2, h * P:(h + 1) * P], view(TMP + h * P, P, NS), stat[0:NS, 16 + h:17 + h])
            rms(stat[0:NS, 16:24], P, s_osq)
            turned("mT", mT)
            squares(view(TMP, D), 1)
            turned("h2T", hT)
            act.wait_ge(s_rt, 1)
            act.activation(exw, exw, ACT.Exp).then_inc(s_rta, 1)

            def rows_in(i):
                act.wait_ge(s_xg, i + 1)
                for c in range(2):
                    ins = act.activation(xg_tok[:, halves(c)], bank[6 + c][:, :], ACT.Copy)
                ins.then_inc(s_xgs, 1)
                act.wait_ge(s_xgt, i + 1)
                for c in range(2):
                    ins = act.activation(xT_e[:, halves(c)], bank[6 + c][:, :], ACT.Copy)
                ins.then_inc(s_xe, 1)

            act.wait_ge(s_tab, 1)
            rows_in(0)

            def pair(i):
                act.wait_ge(s_gclip, i + 1)
                act.activation(sig_sb, g_sb, ACT.Sigmoid, scale=ALPHA).then_inc(s_gsig, 1)
                act.wait_ge(s_cT, i + 1)
                act.activation(comb, bank[4][:, 0:T], ACT.Copy).then_inc(s_c, 1)
                act.wait_ge(s_dloop, i + 1)
                rows_in(i + 1)
                act.wait_ge(s_y, i + 1)
                act.activation(y_sb[:, halves(0)], bank[0][:, :], ACT.Copy).then_inc(s_ys, 1)

            with act.Fori(0, PAIRS // 2) as i:
                pair(i)
            for k in range(2):
                name = ("pT", k)
                copy_out(name, pT[:, k, :], job_bank(name)[:, 0:T])
            wait_filled(act, ("pp", 2, 3))
            for t in (0, 2):
                for n in pieces(t):
                    copy_out(("pp", t, n), pps[t][lanes(t), cols(t, n)], piece(("pp", t, n)))
            with act.Fori(PAIRS // 2, PAIRS) as i:
                pair(i)
            more = act.value_load(flag)
            with act.If(more > 0):
                with act.Fori(1, NBLK) as b:
                    with act.Fori(0, PAIRS) as e:
                        pair(b * PAIRS + e)

            act.activation(stat[:, 31:32], eps, ACT.Sqrt)
            act.wait_ge(s_end, 1)
            squares(sq, 2)
            turned("h3T", hT)
            for t in range(NT):
                for n in pieces(t):
                    name = ("pg", t, n)
                    wait_filled(act, name)
                    drain_done(act.activation(pgs[lanes(t), t, cols(t, n)], piece(name), ACT.Sigmoid), name)
            for t in range(NT):
                act.wait_ge(s_xfin, t + 1)
                s = stat[lanes(t), 12 + t:13 + t]
                sum_squares(x[lanes(t), t, :], sq[lanes(t)], s)
                rms(s, D, s_sumsq)

        @block.vector
        def _(dve):
            chain = [0]

            def step(ins):
                chain[0] += 1
                ins.then_inc(s_dve, 1)
                dve.wait_ge(s_dve, chain[0])

            def copy_out(name, dst, src):
                wait_filled(dve, name)
                drain_done(dve.tensor_copy(dst, src), name)

            def turned(tag, dst):
                for t in range(NT):
                    for half in range(2 if t < 2 else 1):
                        name = (tag, t, half)
                        if drainer[name] == "v":
                            turned_bank(name, dst, copy_out)

            def normalise(count, gain, dst, tiles=range(NT)):
                for t in tiles:
                    dve.wait_ge(s_sumsq, 3 * count + t + 1)
                    s = stat[lanes(t), 4 * count + t:4 * count + t + 1]
                    step(dve.reciprocal(s, s))
                    dve.scalar_tensor_tensor(dst[lanes(t), t, :], x[lanes(t), t, :], s, gain[lanes(t)],
                                             ALU.mult, ALU.mult).then_inc(s_rows, 1)

            dve.wait_ge(s_const, 1)
            for g, w in enumerate(WINDOWS):
                dve.tensor_scalar(dw8[:, g, :], ident[0:NS, 0:NS], 1.0 / w - 1.0, None, ALU.mult)
            dve.wait_ge(ld["gmix"], 16)
            normalise(0, gmix_b, htok)
            l0, l1, m = lbt[:, 0:8], lbt[:, 8:16], lbt[:, 16:24]
            wait_filled(dve, ("lb",))
            drain_done(dve.tensor_copy(lbt[:, 0:16], bank[7][:, 0:16]), ("lb",))
            wait_drained(dve, ("lb",))
            step(dve.tensor_tensor(m, l0, l1, ALU.max))
            dve.tensor_tensor(l0, l0, m, ALU.subtract)
            dve.tensor_tensor(l1, l1, m, ALU.subtract).then_inc(s_lb, 1)
            turned("hT", hT)
            dve.wait_ge(s_lbe, 1)
            step(dve.tensor_tensor(m, l0, l1, ALU.add))
            step(dve.reciprocal(m, m))
            step(dve.tensor_tensor(lb, l0, m, ALU.mult))
            step(dve.tensor_scalar(omlb, lb, -1.0, 1.0, ALU.mult, ALU.add))
            tmask = view(TMP, SEQ)
            step(dve.memset(tmask, 1.0))
            dve.memset(tmask[:, 0:SEQ:CH], 0.0)

            for h in range(H):
                wait_drained(dve, ("f", h))
                ins = dve.tensor_scalar(fh[:, h, :], fh[:, h, :], omlb[:, h:h + 1], lb[:, h:h + 1], ALU.mult, ALU.add)
            step(ins)
            step(dve.tensor_scalar(kh, fh, -1.0, 1.0, ALU.mult, ALU.add))
            dve.tensor_copy(ks, kh[:, :, SEQ:T])
            dve.tensor_copy(fs, fh[:, :, SEQ:T]).then_inc(s_fdone, 1)
            dve.wait_ge(s_prepa, 1)
            for h in range(H):
                ins = dve.tensor_tensor_scan(t2[:, h, 0:SEQ], tmask, fh[:, h, 0:SEQ], 0.0, ALU.mult, ALU.add)
            ins.then_inc(s_prep, 1)
            dve.wait_ge(s_prep, 1)
            b4 = [a[:, :, 0:SEQ].rearrange("p h (n c) -> p h n c", c=CH) for a in (fh, t2)]
            for h in range(H):
                ins = dve.tensor_tensor(b4[0][:, h], b4[1][:, h, :, CH - 1:CH].to_broadcast([P, NCH, CH]), b4[1][:, h],
                                        ALU.subtract)
            ins.then_inc(s_prep, 1)
            dve.wait_ge(s_prepa, 3)
            dve.tensor_tensor(fh[:, :, 0:SEQ], fh[:, :, 0:SEQ], kh[:, :, 0:SEQ], ALU.mult).then_inc(s_prep, 1)
            for h in range(H):
                dve.wait_ge(s_sig, h + 1)
                drain_done(dve.tensor_tensor(qh[:, h, :], job_bank(("q", h))[:, 0:T], qh[:, h, :], ALU.mult), ("q", h))
            wait_drained(dve, ("q", H - 1))
            dve.tensor_tensor(qh[:, :, 0:SEQ], qh[:, :, 0:SEQ], t1[:, :, 0:SEQ], ALU.mult).then_inc(s_prep, 1)
            dve.wait_ge(s_prepa, 5)
            dve.tensor_tensor(t1[:, :, 0:SEQ], t1[:, :, 0:SEQ], kh[:, :, 0:SEQ], ALU.mult).then_inc(s_prep, 1)

            n_tmp = [0]

            def tmp_full():
                n_tmp[0] += 1
                dve.wait_ge(s_tfull, n_tmp[0])
                return tmp[(n_tmp[0] - 1) % 2]

            def gate_chunk(kind, n):
                for t in range(2):
                    name = (kind, n, t)
                    o = og[:, t, halves(n)]
                    w = tmp_full()
                    src = job_bank(name)[:, :] if kind == "g" else o
                    drain_done(dve.tensor_tensor(o, src, w, ALU.mult), name)

            copy_out(("v", 0, 1), v[:, 1, halves(0)], job_bank(("v", 0, 1))[:, :])
            for j in range(4):
                copy_out(("v", "s", j), v[0:NS, 2, cols(2, j)], bank[4][32 * j:32 * j + NS, 0:256])
            copy_out(("v", 1, 1), v[:, 1, halves(1)], job_bank(("v", 1, 1))[:, :])
            gate_chunk("g", 0)
            gate_chunk("g", 1)
            wait_drained(dve, ("g", 1, 1))
            gate_chunk("ga", 0)
            dve.wait_ge(s_sczero, 1)
            dve.wait_ge(s_const, 2)
            for t in range(2):
                for half in range(2):
                    name = ("score", t, half)
                    wait_filled(dve, name)
                    drain_done(dve.copy_predicated(score[:, 2 * t + half, :].rearrange("p (h c) -> p h c", h=4),
                                                   cmask.unsqueeze(1).to_broadcast([P, 4, P]),
                                                   job_bank(name)[:, :].rearrange("p (h c) -> p h c", h=4)), name)
            for j in range(4):
                w = tmp_full()
                o = og[0:NS, 2, halves(j % 2)]
                if j == 2:
                    wait_drained(dve, ("g", "s", 1))
                src = bank[4][32 * j:32 * j + NS, :] if j < 2 else o
                drain_done(dve.tensor_tensor(o, src, w[0:NS], ALU.mult), ("g", "s", j))
            gate_chunk("ga", 1)

            def head_norm(name, rows, t, half):
                tmp_full()
                s = stat[:, 16 + 4 * ((n_tmp[0] - 1) % 2):20 + 4 * ((n_tmp[0] - 1) % 2)]
                step(dve.reciprocal(s, s))
                for j in range(4):
                    hh = slice((4 * half + j) * P, (4 * half + j + 1) * P)
                    ins = dve.scalar_tensor_tensor(og[rows, t, hh], job_bank(name)[rows, j * P:(j + 1) * P],
                                                   s[:, j:j + 1], og[rows, t, hh], ALU.mult, ALU.mult)
                drain_done(ins, name)

            for n in range(NCH):
                if n >= 1:
                    wait_drained(dve, ("dS", n - 1, 1))
                if n >= 2:
                    dve.wait_ge(s_inter, n)
                for half in range(2):
                    name = ("dS", n, half)
                    if n == 0:
                        copy_out(name, state[1][:, 4 * half:4 * half + 4, :],
                                 job_bank(name)[:, :].rearrange("p (h v) -> p h v", h=4))
                        continue
                    wait_filled(dve, name)
                    for j in range(4):
                        h = 4 * half + j
                        ins = dve.scalar_tensor_tensor(state[(n + 1) % 2][:, h, :], state[n % 2][:, h, :],
                                                       ebl[:, h, n:n + 1], job_bank(name)[:, j * P:(j + 1) * P],
                                                       ALU.mult, ALU.add)
                    drain_done(ins, name)
                if n % 4 == 3:
                    t = n // 4
                    dve.wait_ge(s_ogp, t + 1)
                    for half in range(2):
                        head_norm(("o", t, half), slice(0, P), t, half)
            dve.wait_ge(s_qm, 1)
            copy_out(("u", 0, 1), u[:, 1, halves(0)], job_bank(("u", 0, 1))[:, :])
            copy_out(("u", 1, 1), u[:, 1, halves(1)], job_bank(("u", 1, 1))[:, :])
            for b in range(NS):
                dve.wait_ge(s_decay, b + 1)
                dve.wait_ge(s_vall[b % 2], 16 * (b // 2 + 1))
                for h in range(H):
                    ins = dve.scalar_tensor_tensor(s0[:, b, h, :], v_all[b % 2][:, h * P:(h + 1) * P],
                                                   ks[:, h, b:b + 1], s0[:, b, h, :], ALU.mult, ALU.add)
                ins.then_inc(s_snew, 1)
            name = ("os",)
            wait_filled(dve, name)
            osb = v[0:NS, 2, :].rearrange("p (a j v) -> p j a v", a=2, j=4)
            for j in range(4):
                ins = dve.tensor_copy(osb[:, j], bank[7][32 * j:32 * j + NS, 0:2 * P].rearrange("p (a v) -> p a v", a=2))
            drain_done(ins, name)
            wait_drained(dve, name)

            def sample_norm():
                flat, s = v[0:NS, 2, :], stat[0:NS, 16:24]
                by_head = flat.rearrange("p (h v) -> p h v", h=H)
                dve.wait_ge(s_osq, 1)
                step(dve.reciprocal(s, s))
                step(dve.tensor_tensor(by_head, by_head, s.unsqueeze(2).to_broadcast([NS, H, P]), ALU.mult))
                dve.wait_ge(s_ogp, NT)
                dve.tensor_tensor(og[0:NS, 2, :], og[0:NS, 2, :], flat, ALU.mult)

            for c in range(1, KD, 2):
                copy_out(("dT", c), dT[:, c, :], job_bank(("dT", c))[:, 0:T])
            dve.wait_ge(s_gbs, NT)
            for t in range(NT):
                if t == 2:
                    sample_norm()
                for n in pieces(t):
                    name = ("yp", t, n)
                    wait_filled(dve, name)
                    o = gb[lanes(t), t, cols(t, n)]
                    drain_done(dve.tensor_tensor(o, piece(name), o, ALU.mult), name)
                wait_drained(dve, name)
                dve.tensor_tensor(og[lanes(t), t, :], og[lanes(t), t, :], gb[lanes(t), t, :], ALU.add)\
                   .then_inc(s_merged, 1)

            def add_to_x(tag, t):
                for n in pieces(t):
                    name = (tag, t, n)
                    wait_filled(dve, name)
                    xs = x[lanes(t), t, cols(t, n)]
                    drain_done(dve.tensor_tensor(xs, piece(name), xs, ALU.add), name)

            add_to_x("x1", 0)
            dve.wait_ge(ld["gffn"], 16)
            add_to_x("x1", 1)
            normalise(1, gffn_b, h2, (0, 1))
            add_to_x("x1", 2)
            normalise(1, gffn_b, h2, (2,))
            turned("h2T", hT)

            def by_expert(rows):
                return rows.rearrange("p t (e c) -> p t e c", e=2)

            slots = iota[:, 0:CAP].unsqueeze(1).unsqueeze(1).to_broadcast([P, NT, 2, CAP])

            def select_tokens(i):
                mine = slot_tab[:, :, bass.ds(2 * i, 2)].unsqueeze(3).to_broadcast([P, NT, 2, CAP])
                dve.tensor_tensor(by_expert(oh), slots, mine, ALU.is_equal).then_inc(s_oh, 1)

            def weigh_tokens(i):
                weight = wt_tab[:, :, bass.ds(2 * i, 2)].unsqueeze(3).to_broadcast([P, NT, 2, CAP])
                dve.wait_ge(s_oh, i + 1)
                dve.tensor_tensor(by_expert(ohw), by_expert(oh), weight, ALU.mult).then_inc(s_ohw, 1)

            def select_experts(i):
                mine = eis[:, bass.ds(2 * i, 2)].unsqueeze(2).to_broadcast([NE, 2, CAP])
                dve.tensor_copy(esel.rearrange("p (e c) -> p e c", e=2), mine).then_inc(s_esel, 1)

            dve.wait_ge(ld["br"], 16)
            wait_filled(dve, ("lgT",))
            drain_done(dve.tensor_scalar(lgT, bank[6][0:NE, 0:T], brt, None, ALU.add), ("lgT",))
            step(dve.memset(lg, 0.0))
            wait_filled(dve, ("lg",))
            dve.tensor_copy(lg[:, 0:2, :], bank[7][:, 0:2 * NE].rearrange("p (t e) -> p t e", t=2))
            drain_done(dve.tensor_copy(lg[0:NS, 2, :], bank[7][0:NS, 2 * NE:3 * NE]), ("lg",))
            wait_drained(dve, ("lg",))
            for t in range(NT):
                ins = dve.max(top[:, t, :], lg[:, t, :])
            step(ins)
            for t in range(NT):
                ins = dve.max_index(topi[:, t, :], top[:, t, :], lg[:, t, :])
            step(ins)
            dve.tensor_copy(topf, topi)
            dve.tensor_tensor(exw, top[:, :, 0:TOPK], top[:, :, 0:1].to_broadcast([P, NT, TOPK]), ALU.subtract)\
               .then_inc(s_rt, 1)
            one_hot = [P, NT, TOPK, NE]
            experts = iota[:, 0:NE].unsqueeze(1).unsqueeze(1).to_broadcast(one_hot)
            dve.wait_ge(s_rt, 1)
            step(dve.tensor_tensor(hit, experts, topf[:, :, 0:TOPK].unsqueeze(3).to_broadcast(one_hot), ALU.is_equal))
            dve.tensor_reduce(msk, hit.rearrange("p t k e -> p t e k"), AX_X, ALU.add).then_inc(s_rt, 1)
            dve.wait_ge(s_rta, 1)
            step(dve.tensor_reduce(ssum, exw, AX_X, ALU.add))
            step(dve.reciprocal(rsum, ssum))
            step(dve.tensor_tensor(exw, exw, rsum.to_broadcast([P, NT, TOPK]), ALU.mult))
            step(dve.tensor_tensor(hit_w, hit, exw.unsqueeze(3).to_broadcast(one_hot), ALU.mult))
            dve.tensor_reduce(wdn, hit_w.rearrange("p t k e -> p t e k"), AX_X, ALU.add).then_inc(s_rt, 1)
            dve.wait_ge(s_rt, 3)
            for b in range(NBLK):
                columns = slice(b * NE, (b + 1) * NE)
                dve.tensor_copy(wt_tab[:, :, columns], wdn)
                dve.tensor_copy(eis[:, columns], ident[0:NE, 0:NE])
            dve.memset(slot_tab[:, :, NBLK * NE:NTAB], 0.0)
            wait_filled(dve, ("rank",))

            def slots_of(b):
                return dve.scalar_tensor_tensor(slot_tab[:, :, b * NE:(b + 1) * NE],
                                                bank[0][:, 0:NT * NE].rearrange("p (t e) -> p t e", t=NT),
                                                FAR - CAP * b, msk, ALU.add, ALU.mult)

            step(slots_of(0))
            first, others = slot_tab[:, :, 0:NE], slot_tab[:, :, NE:NTAB]
            step(dve.tensor_scalar(first, first, -FAR, None, ALU.add))
            select_tokens(0)
            for b in range(1, NBLK):
                ins = slots_of(b)
            step(ins)
            drain_done(dve.tensor_scalar(others, others, -FAR, None, ALU.add), ("rank",))
            wait_filled(dve, ("count",))
            drain_done(dve.tensor_reduce(stat[0:8, 16:17], bank[1][0:8, 0:NE], AX_X, ALU.max), ("count",))
            wait_drained(dve, ("count",))
            dve.tensor_scalar(flag, stat[0:1, 16:17], CAP + 0.5, None, ALU.is_gt).then_inc(s_tab, 1)
            copy_out(("wT",), wT, bank[2][0:NE, 0:T])
            dve.memset(wt_tab[:, :, NBLK * NE:NTAB], 0.0).then_inc(s_free23, 1)
            dve.memset(eis[:, NBLK * NE:NTAB], 0.0).then_inc(s_free6, 1)
            step(dve.memset(stat[:, 20:21], 0.0))
            dve.memset(stat[:, 21:22], 0.0).then_inc(s_free45, 1)

            select_experts(0)

            def pair(i):
                dve.wait_ge(s_xg, i + 1)
                weigh_tokens(i)
                dve.wait_ge(s_ohw, i + 1)
                select_tokens(i + 1)
                dve.wait_ge(s_gate, i + 1)
                for c in range(2):
                    ins = dve.tensor_scalar(g_sb[:, halves(c)], bank[c][:, :], LIMIT, None, ALU.min)
                ins.then_inc(s_gclip, 1)
                dve.wait_ge(s_gsig, i + 1)
                dve.tensor_tensor(g_sb, g_sb, sig_sb, ALU.mult).then_inc(s_dloop, 1)
                dve.wait_ge(s_up, i + 1)
                for c in range(2):
                    ins = dve.tensor_scalar(u_sb[:, halves(c)], bank[2 + c][:, :], LIMIT, -LIMIT, ALU.min, ALU.max)
                ins.then_inc(s_uclip, 1)
                select_experts(i + 1)
                dve.wait_ge(s_dloop, i + 1)
                dve.wait_ge(s_uclip, i + 1)
                dve.scalar_tensor_tensor(act_sb, u_sb, 1.0, g_sb, ALU.add, ALU.mult).then_inc(s_actr, 1)
                for c in range(2):
                    dve.wait_ge(s_aT, 2 * i + c + 1)
                    dve.tensor_copy(actT[:, halves(c)], bank[4 + c][:, :]).then_inc(s_aTs, 1)
                dve.wait_ge(s_y, i + 1)
                dve.tensor_copy(y_sb[:, halves(1)], bank[1][:, :]).then_inc(s_ys, 1)
                for t, done in ((0, s_free23), (1, s_free45), (2, s_free6)):
                    dve.wait_ge(s_mix, 3 * i + t + 1)
                    for c in range(2):
                        xs = x[lanes(t), t, halves(c)]
                        src = bank[2 + 2 * t + c][:, :] if t < 2 else bank[6][32 * c:32 * c + NS, :]
                        ins = dve.tensor_tensor(xs, src, xs, ALU.add)
                    ins.then_inc(done, 1)
                dve.wait_ge(s_free6, i + 2)

            with dve.Fori(0, PAIRS // 2) as i:
                pair(i)
            for t in range(NT):
                add_to_x("bd", t)
            wait_filled(dve, ("pp", 2, 3))
            for n in pieces(1):
                copy_out(("pp", 1, n), pps[1][:, cols(1, n)], piece(("pp", 1, n)))
            wait_drained(dve, ("pp", 1, 1))
            with dve.Fori(PAIRS // 2, PAIRS) as i:
                pair(i)
            more = dve.value_load(flag)
            with dve.If(more > 0):
                with dve.Fori(1, NBLK) as b:
                    with dve.Fori(0, PAIRS) as e:
                        pair(b * PAIRS + e)

            dve.memset(stat[:, 22:23], 0.0).then_inc(s_end, 1)
            dve.wait_ge(ld["gple"], 16)
            normalise(2, gple_b, h3)
            turned("h3T", hT)
            dve.wait_ge(ld["gfin"], 16)
            for t in range(NT):
                for n in pieces(t):
                    wait_drained(dve, ("pg", t, n))
                    o = pgs[lanes(t), t, cols(t, n)]
                    ins = dve.tensor_tensor(o, pps[t][lanes(t), cols(t, n)], o, ALU.mult)
                step(ins)
                xs = x[lanes(t), t, :]
                dve.tensor_tensor(xs, xs, pgs[lanes(t), t, :], ALU.add).then_inc(s_xfin, 1)
            for t in range(NT):
                dve.wait_ge(s_sumsq, 9 + t + 1)
                s = stat[lanes(t), 12 + t:13 + t]
                step(dve.reciprocal(s, s))
                dve.scalar_tensor_tensor(yout[lanes(t), t, :], x[lanes(t), t, :], s, gfin_b[lanes(t)],
                                         ALU.mult, ALU.mult).then_inc(s_yout, 1)


_INS = ["x_prompt", "x_sample", "p_prompt", "p_sample", "state_hgrn", "state_pool", "g_mix", "w_in",
        "hg_lb_logits", "hg_norm", "w_pool", "pool_scale", "w_out", "g_ffn", "w_router", "b_router", "w_gate",
        "b_gate", "w_up", "b_up", "w_down", "b_down", "g_ple", "w_ple_gate", "w_ple_proj", "g_final"]
_OUTS = [(1, SEQ, D), (NS, 1, D), (1, 1, H, P, P), (1, 1, BUF, D), (1, NS, H, P, P), (1, NS, BUF, D)]


def kernel(**inputs):
    import concourse.bacc as _bacc
    from concourse.bass_utils import run_bass_kernel_spmd as _run

    nc = _bacc.Bacc("TRN2", target_bir_lowering=False, num_devices=1)
    arrays, args = {}, []
    for name in _INS:
        a = np.ascontiguousarray(inputs[name])
        arrays[f"in_{name}_dram"] = a
        args.append(nc.dram_tensor(f"in_{name}_dram", a.shape, mybir.dt.from_np(a.dtype), kind="ExternalInput").ap())
    for i, shape in enumerate(_OUTS):
        args.append(nc.dram_tensor(f"out_{i}_dram", shape, F32, kind="ExternalOutput").ap())
    build(nc, *args)
    r = _run(nc, [arrays], core_ids=[0])
    return tuple(r.results[0][f"out_{i}_dram"] for i in range(len(_OUTS)))
```
